# Optimizing a Trainium2 kernel written in Bass

```python
import jax, jax.numpy as jnp
from jax import lax
import numpy as np

D_MODEL = 1024
BATCH = 1
SEQ = 512
DEPTH = 1

PLE_DIM = 256
EPS = 1e-6
GM_WIDTH = 512
GM_GROUPS = 8
GM_CHUNK = 128
HG_HEADS = 4
HG_KEY = 128
HG_VAL = 128
HG_CHUNK = 64
HG_KW = HG_HEADS * HG_KEY
HG_VW = HG_HEADS * HG_VAL
IN_SPLITS = [GM_WIDTH, GM_WIDTH, HG_KW, HG_KW, HG_VW, HG_VW, D_MODEL, D_MODEL]
IN_COLS = sum(IN_SPLITS)
N_GROUPS = 4
EXP_PER_GROUP = 8
N_EXPERTS = N_GROUPS * EXP_PER_GROUP
TOP_K = 2
D_EXPERT = 512
MOE_BLOCK = 128


def rmsnorm(x, g):
    xf = x.astype(jnp.float32)
    y = xf * lax.rsqrt(jnp.mean(xf * xf, axis=-1, keepdims=True) + EPS)
    return y.astype(x.dtype) * g

def layernorm(x, g, b):
    xf = x.astype(jnp.float32)
    mu = jnp.mean(xf, axis=-1, keepdims=True)
    var = jnp.mean(jnp.square(xf - mu), axis=-1, keepdims=True)
    y = (xf - mu) * lax.rsqrt(var + EPS)
    return y.astype(x.dtype) * g + b

def gmlp_branch(u, v, ln_g, ln_b, w_sp, b_sp):
    B, S, _ = u.shape
    n_c = S // GM_CHUNK
    dg = GM_WIDTH // GM_GROUPS
    v = layernorm(v, ln_g, ln_b).reshape(B, n_c, GM_CHUNK, GM_GROUPS, dg)
    mask = jnp.tril(jnp.ones((GM_CHUNK, GM_CHUNK), dtype=bool))
    w = jnp.where(mask[None], w_sp, jnp.zeros_like(w_sp))
    s = jnp.einsum('gts,bcsgd->bctgd', w, v) + b_sp.T[:, :, None]
    return u * s.reshape(B, S, GM_WIDTH)

def hgrn2_branch(q, f_raw, i_in, og, lb, norm_g):
    B, S, _ = q.shape
    C = HG_CHUNK
    n_c = S // C
    dt = q.dtype
    qf = jax.nn.silu(q.astype(jnp.float32)).reshape(B, n_c, C, HG_HEADS, HG_KEY)
    f = lb + (1.0 - lb) * jax.nn.sigmoid(f_raw.astype(jnp.float32))
    log_f = jnp.log(f).reshape(B, n_c, C, HG_HEADS, HG_KEY)
    k = (1.0 - f).reshape(B, n_c, C, HG_HEADS, HG_KEY)
    v = i_in.astype(jnp.float32).reshape(B, n_c, C, HG_HEADS, HG_VAL)
    b = jnp.cumsum(log_f, axis=2)
    b_last = b[:, :, -1:]
    q_dec = qf * jnp.exp(b)
    k_inv = k * jnp.exp(-b)
    k_end = k * jnp.exp(b_last - b)
    mask = jnp.tril(jnp.ones((C, C), dtype=bool))
    att = jnp.einsum('bcthk,bcshk->bchts', q_dec, k_inv)
    att = jnp.where(mask, att, jnp.zeros_like(att))
    o_intra = jnp.einsum('bchts,bcshv->bcthv', att, v)
    dS = jnp.einsum('bcshk,bcshv->bchkv', k_end, v)
    decay = jnp.exp(b_last[:, :, 0])

    def step(s_prev, inp):
        dec, ds = inp
        return dec[..., None] * s_prev + ds, s_prev

    s0 = jnp.zeros((B, HG_HEADS, HG_KEY, HG_VAL), jnp.float32)
    _, s_starts = lax.scan(step, s0, (jnp.moveaxis(decay, 1, 0), jnp.moveaxis(dS, 1, 0)))
    o_inter = jnp.einsum('bcthk,cbhkv->bcthv', q_dec, s_starts)
    o = (o_intra + o_inter).reshape(B, S, HG_HEADS, HG_VAL)
    o = o * lax.rsqrt(jnp.mean(o * o, axis=-1, keepdims=True) + EPS)
    o = o * norm_g.astype(jnp.float32).reshape(HG_HEADS, HG_VAL)
    return o.reshape(B, S, HG_VW).astype(dt) * jax.nn.sigmoid(og)

def hier_moe(h, w_grp, w_exp, w1, w3, w2):
    B, S, D = h.shape
    T = B * S
    xt = h.reshape(T, D)
    grp_logits = (xt @ w_grp).astype(jnp.float32)
    grp_prob = jax.nn.softmax(grp_logits, axis=-1)
    p_g, g_sel = lax.top_k(grp_prob, 1)
    exp_logits = (xt @ w_exp).astype(jnp.float32).reshape(T, N_GROUPS, EXP_PER_GROUP)
    sel_logits = jnp.take_along_axis(exp_logits, g_sel[:, :, None], axis=1)[:, 0]
    top_l, top_e = lax.top_k(sel_logits, TOP_K)
    gate = jax.nn.softmax(top_l, axis=-1) * p_g

    A = T * TOP_K
    eid = (g_sel * EXP_PER_GROUP + top_e).reshape(A)
    tok = jnp.repeat(jnp.arange(T, dtype=jnp.int32), TOP_K)
    wa = gate.reshape(A)
    order = jnp.argsort(eid)
    eid_s, tok_s, w_s = eid[order], tok[order], wa[order]
    counts = jnp.bincount(eid, length=N_EXPERTS)
    padded = ((counts + MOE_BLOCK - 1) // MOE_BLOCK) * MOE_BLOCK
    pad_end = jnp.cumsum(padded)
    pad_start = pad_end - padded
    start = jnp.cumsum(counts) - counts
    rank = jnp.arange(A, dtype=jnp.int32) - start[eid_s]
    dest = pad_start[eid_s] + rank
    n_blk = -(-A // MOE_BLOCK) + N_EXPERTS
    P = n_blk * MOE_BLOCK
    buf = jnp.zeros((P, D), xt.dtype).at[dest].set(xt[tok_s])
    blk_start = jnp.arange(n_blk, dtype=jnp.int32) * MOE_BLOCK
    blk_e = jnp.minimum(jnp.searchsorted(pad_end, blk_start, side='right'), N_EXPERTS - 1)

    def expert_block(args):
        xb, e = args
        return (jax.nn.silu(xb @ w1[e]) * (xb @ w3[e])) @ w2[e]

    ybuf = lax.map(expert_block, (buf.reshape(n_blk, MOE_BLOCK, D), blk_e)).reshape(P, D)
    contrib = ybuf[dest] * w_s[:, None].astype(xt.dtype)
    out = jax.ops.segment_sum(contrib, tok_s, num_segments=T)
    return out.reshape(B, S, D)

def first_inputs(seed: int = 0) -> dict:
    key = jax.random.key(seed)
    ks = jax.random.split(key, 24)

    def nrm(k, shape, scale):
        return jax.random.normal(k, shape, jnp.float32) * scale

    def gain(k, shape):
        return 1.0 + 0.05 * jax.random.normal(k, shape, jnp.float32)

    L = DEPTH
    return {
        "x": nrm(ks[0], (BATCH, SEQ, D_MODEL), 1.0),
        "p": nrm(ks[1], (DEPTH, BATCH, SEQ, PLE_DIM), 1.0),
        "g_mix": gain(ks[2], (L, D_MODEL)),
        "w_in": nrm(ks[3], (L, D_MODEL, IN_COLS), D_MODEL ** -0.5),
        "gm_ln_g": gain(ks[4], (L, GM_WIDTH)),
        "gm_ln_b": nrm(ks[5], (L, GM_WIDTH), 0.02),
        "gm_w_sp": nrm(ks[6], (L, GM_GROUPS, GM_CHUNK, GM_CHUNK), 0.1 * GM_CHUNK ** -0.5),
        "gm_b_sp": gain(ks[7], (L, GM_GROUPS, GM_CHUNK)),
        "w_up_a": nrm(ks[8], (L, GM_WIDTH, D_MODEL), GM_WIDTH ** -0.5),
        "hg_lb_param": gain(ks[9], (L + 1, HG_KW)),
        "hg_norm_g": gain(ks[10], (L, HG_VW)),
        "w_up_b": nrm(ks[11], (L, HG_VW, D_MODEL), HG_VW ** -0.5),
        "w_out": nrm(ks[12], (L, D_MODEL, D_MODEL), D_MODEL ** -0.5),
        "g_ffn": gain(ks[13], (L, D_MODEL)),
        "w_grp": nrm(ks[14], (L, D_MODEL, N_GROUPS), D_MODEL ** -0.5),
        "w_exp": nrm(ks[15], (L, D_MODEL, N_EXPERTS), D_MODEL ** -0.5),
        "w1": nrm(ks[16], (L, N_EXPERTS, D_MODEL, D_EXPERT), D_MODEL ** -0.5),
        "w3": nrm(ks[17], (L, N_EXPERTS, D_MODEL, D_EXPERT), D_MODEL ** -0.5),
        "w2": nrm(ks[18], (L, N_EXPERTS, D_EXPERT, D_MODEL), D_EXPERT ** -0.5),
        "g_ple": gain(ks[19], (L, D_MODEL)),
        "w_pg": nrm(ks[20], (L, D_MODEL, D_MODEL), D_MODEL ** -0.5),
        "w_ple": nrm(ks[21], (L, PLE_DIM, D_MODEL), PLE_DIM ** -0.5),
        "g_final": gain(ks[22], (D_MODEL,)),
    }

def first_block(x, p, g_mix, w_in, gm_ln_g, gm_ln_b, gm_w_sp, gm_b_sp, w_up_a,
              hg_lb_param, hg_norm_g, w_up_b, w_out, g_ffn, w_grp, w_exp,
              w1, w3, w2, g_ple, w_pg, w_ple, g_final):
    lb_all = jnp.cumsum(jax.nn.softmax(hg_lb_param.astype(jnp.float32), axis=0), axis=0)
    split_idx = [int(s) for s in np.cumsum(IN_SPLITS)[:-1]]
    for i in range(DEPTH):
        h = rmsnorm(x, g_mix[i])
        z = h @ w_in[i]
        u, v, hq, hf, hi, hog, gate_a, gate_b = jnp.split(z, split_idx, axis=-1)
        y_a = gmlp_branch(jax.nn.gelu(u), jax.nn.gelu(v), gm_ln_g[i], gm_ln_b[i], gm_w_sp[i], gm_b_sp[i])
        y_b = hgrn2_branch(hq, hf, hi, hog, lb_all[i], hg_norm_g[i])
        merged = jax.nn.sigmoid(gate_a) * (y_a @ w_up_a[i]) + jax.nn.sigmoid(gate_b) * (y_b @ w_up_b[i])
        x = x + merged @ w_out[i]
        h = rmsnorm(x, g_ffn[i])
        x = x + hier_moe(h, w_grp[i], w_exp[i], w1[i], w3[i], w2[i])
        h = rmsnorm(x, g_ple[i])
        x = x + jax.nn.sigmoid(h @ w_pg[i]) * (p[i] @ w_ple[i])
    return rmsnorm(x, g_final)


CHUNK = 64
Q_BLOCK = 128
SB_HEADS = 8
SB_HEAD_DIM = 64
SB_WIDTH = SB_HEADS * SB_HEAD_DIM
GLA_HEADS = 4
GLA_KEY_WIDTH = D_MODEL // 2
GLA_VALUE_WIDTH = D_MODEL
GLA_DK = GLA_KEY_WIDTH // GLA_HEADS
GLA_DV = GLA_VALUE_WIDTH // GLA_HEADS
GLA_GATE_RANK = 16
GLA_GATE_TAU = 16.0
D_FF = 4 * D_MODEL

SPLIT_SIZES = (SB_WIDTH, SB_WIDTH, SB_WIDTH,
               GLA_KEY_WIDTH, GLA_KEY_WIDTH, GLA_VALUE_WIDTH, GLA_VALUE_WIDTH, GLA_GATE_RANK,
               D_MODEL, D_MODEL)
D_IN = 3 * SB_WIDTH + 2 * GLA_KEY_WIDTH + 2 * GLA_VALUE_WIDTH + GLA_GATE_RANK + 2 * D_MODEL


def rms_norm(x, g):
    xf = x.astype(jnp.float32)
    y = xf * lax.rsqrt(jnp.mean(xf * xf, axis=-1, keepdims=True) + EPS)
    return (y * g.astype(jnp.float32)).astype(x.dtype)

def split_heads(t, n_heads):
    b, s, _ = t.shape
    return t.reshape(b, s, n_heads, -1).transpose(0, 2, 1, 3)

def merge_heads(t):
    b, h, s, d = t.shape
    return t.transpose(0, 2, 1, 3).reshape(b, s, h * d)

def stick_breaking_attention(q, k, v):
    _, _, s_len, d = q.shape
    scale = d ** -0.5
    outs = []
    for start in range(0, s_len, Q_BLOCK):
        end = start + Q_BLOCK
        kb = k[:, :, :end]
        vb = v[:, :, :end]
        z = jnp.einsum('bhtd,bhsd->bhts', q[:, :, start:end], kb) * scale
        t_idx = start + jnp.arange(Q_BLOCK)[:, None]
        s_idx = jnp.arange(end)[None, :]
        past = s_idx < t_idx
        log_beta = jax.nn.log_sigmoid(z)
        log_fail = jnp.where(past, log_beta - z, 0.0)
        later = lax.cumsum(log_fail, axis=3, reverse=True) - log_fail
        w = jnp.where(past, jnp.exp(log_beta + later), 0.0)
        outs.append(jnp.einsum('bhts,bhsd->bhtd', w, vb))
    return jnp.concatenate(outs, axis=2)

def gla_chunked(q, k, v, log_a):
    b, h, s_len, dk = q.shape
    dv = v.shape[-1]
    nc = s_len // CHUNK

    def to_chunks(t):
        return t.reshape(b, h, nc, CHUNK, t.shape[-1]).transpose(2, 0, 1, 3, 4)

    qc, kc, vc, ac = (to_chunks(t) for t in (q * dk ** -0.5, k, v, log_a))
    bc = jnp.cumsum(ac, axis=3)
    causal = jnp.tril(jnp.ones((CHUNK, CHUNK), dtype=bool))

    def step(state, inp):
        qi, ki, vi, bi = inp
        b_last = bi[:, :, -1:, :]
        o_inter = jnp.einsum('bhtk,bhkv->bhtv', qi * jnp.exp(bi), state)
        diff = bi[:, :, :, None, :] - bi[:, :, None, :, :]
        decay = jnp.exp(jnp.where(causal[:, :, None], diff, -jnp.inf))
        scores = jnp.einsum('bhtk,bhsk,bhtsk->bhts', qi, ki, decay)
        o_intra = jnp.einsum('bhts,bhsv->bhtv', scores, vi)
        new_state = (jnp.exp(b_last[:, :, 0, :, None]) * state
                     + jnp.einsum('bhsk,bhsv->bhkv', ki * jnp.exp(b_last - bi), vi))
        return new_state, o_inter + o_intra

    state0 = jnp.zeros((b, h, dk, dv), jnp.float32)
    _, o = lax.scan(step, state0, (qc, kc, vc, bc))
    return o.transpose(1, 2, 0, 3, 4).reshape(b, h, s_len, dv)

def second_inputs(seed: int = 0) -> dict:
    key = jax.random.key(seed)
    ks = jax.random.split(key, 16)
    f32 = jnp.float32

    def w(k, shape, fan_in):
        return jax.random.normal(k, shape, f32) * (fan_in ** -0.5)

    def gain(k, shape):
        return 1.0 + 0.02 * jax.random.normal(k, shape, f32)

    return {
        'x': jax.random.normal(ks[0], (BATCH, SEQ, D_MODEL), f32),
        'norm_mix': gain(ks[1], (DEPTH, D_MODEL)),
        'w_in': w(ks[2], (DEPTH, D_MODEL, D_IN), D_MODEL),
        'w_gate_up': w(ks[3], (DEPTH, GLA_GATE_RANK, GLA_KEY_WIDTH), GLA_GATE_RANK),
        'b_gate_up': 0.1 * jax.random.normal(ks[4], (DEPTH, GLA_KEY_WIDTH), f32),
        'gla_norm': gain(ks[5], (DEPTH, GLA_DV)),
        'w_proj_sb': w(ks[6], (DEPTH, SB_WIDTH, D_MODEL), SB_WIDTH),
        'w_proj_gla': w(ks[7], (DEPTH, GLA_VALUE_WIDTH, D_MODEL), GLA_VALUE_WIDTH),
        'w_out': w(ks[8], (DEPTH, D_MODEL, D_MODEL), D_MODEL),
        'norm_mlp': gain(ks[9], (DEPTH, D_MODEL)),
        'w_ff1': w(ks[10], (DEPTH, D_MODEL, D_FF), D_MODEL),
        'w_ff2': w(ks[11], (DEPTH, D_FF, D_MODEL), D_FF),
        'norm_final': gain(ks[12], (D_MODEL,)),
    }

def second_block(x, norm_mix, w_in, w_gate_up, b_gate_up, gla_norm, w_proj_sb, w_proj_gla,
              w_out, norm_mlp, w_ff1, w_ff2, norm_final):
    f32 = jnp.float32
    bsz, s_len, _ = x.shape
    split_points = np.cumsum(SPLIT_SIZES)[:-1].tolist()
    for layer in range(DEPTH):
        h = rms_norm(x, norm_mix[layer])
        proj = h @ w_in[layer]
        (sb_q, sb_k, sb_v, g_q, g_k, g_v, g_out, g_low, gate_sb, gate_gla) = jnp.split(
            proj, split_points, axis=-1)

        o_sb = stick_breaking_attention(split_heads(sb_q, SB_HEADS).astype(f32),
                                        split_heads(sb_k, SB_HEADS).astype(f32),
                                        split_heads(sb_v, SB_HEADS).astype(f32))
        o_sb = merge_heads(o_sb).astype(x.dtype)

        log_a = jax.nn.log_sigmoid((g_low @ w_gate_up[layer] + b_gate_up[layer]).astype(f32)) / GLA_GATE_TAU
        o_gla = gla_chunked(split_heads(g_q, GLA_HEADS).astype(f32),
                            split_heads(g_k, GLA_HEADS).astype(f32),
                            split_heads(g_v, GLA_HEADS).astype(f32),
                            split_heads(log_a, GLA_HEADS))
        o_gla = o_gla.transpose(0, 2, 1, 3)
        o_gla = rms_norm(o_gla, gla_norm[layer])
        o_gla = o_gla * jax.nn.silu(g_out.astype(f32).reshape(bsz, s_len, GLA_HEADS, GLA_DV))
        o_gla = o_gla.reshape(bsz, s_len, GLA_VALUE_WIDTH).astype(x.dtype)

        mix = (jax.nn.sigmoid(gate_sb) * (o_sb @ w_proj_sb[layer])
               + jax.nn.sigmoid(gate_gla) * (o_gla @ w_proj_gla[layer]))
        x = x + mix @ w_out[layer]

        h2 = rms_norm(x, norm_mlp[layer])
        x = x + jnp.square(jax.nn.relu(h2 @ w_ff1[layer])) @ w_ff2[layer]
    return rms_norm(x, norm_final)


def setup_inputs(seed=0):
    out = dict(first_inputs(seed))
    for name, value in second_inputs(seed + 1).items():
        if name != "x":
            out[name + "_2"] = value
    return out


def reference(
    x, p, g_mix, w_in, gm_ln_g, gm_ln_b, gm_w_sp, gm_b_sp, w_up_a, hg_lb_param, hg_norm_g,
    w_up_b, w_out, g_ffn, w_grp, w_exp, w1, w3, w2, g_ple, w_pg, w_ple, g_final, norm_mix_2,
    w_in_2, w_gate_up_2, b_gate_up_2, gla_norm_2, w_proj_sb_2, w_proj_gla_2, w_out_2,
    norm_mlp_2, w_ff1_2, w_ff2_2, norm_final_2,
):
    x = first_block(
        x, p, g_mix, w_in, gm_ln_g, gm_ln_b, gm_w_sp, gm_b_sp, w_up_a, hg_lb_param, hg_norm_g,
        w_up_b, w_out, g_ffn, w_grp, w_exp, w1, w3, w2, g_ple, w_pg, w_ple, g_final,
    )
    return second_block(
        x, norm_mix_2, w_in_2, w_gate_up_2, b_gate_up_2, gla_norm_2, w_proj_sb_2, w_proj_gla_2,
        w_out_2, norm_mlp_2, w_ff1_2, w_ff2_2, norm_final_2,
    )


_drawn_inputs = setup_inputs


def setup_inputs(seed=0):
    import zlib

    import numpy as np

    out = dict(_drawn_inputs(seed))
    spreads = {}
    factors = {'gm_ln_g': 8.0,
     'gm_ln_b': 27.722,
     'hg_lb_param': 4.399,
     'g_ple': 5.382,
     'norm_mix_2': 3.531,
     'b_gate_up_2': 3.983,
     'gla_norm_2': 21.502,
     'norm_mlp_2': 10.646,
     'norm_final_2': 8.046}
    for name, (base, spread) in spreads.items():
        noise = np.random.default_rng([zlib.crc32(name.encode()), seed]).standard_normal(out[name].shape)
        drawn = base * np.exp(spread * noise) if base else spread * noise
        out[name] = __import__('jax').numpy.asarray(drawn.astype(out[name].dtype))
    for name, factor in factors.items():
        out[name] = (out[name] * factor).astype(out[name].dtype)
    return out
```

```python
from contextlib import ExitStack

import concourse.bass as bass
from concourse import mybir

ALU = mybir.AluOpType
ACT = mybir.ActivationFunctionType
F32 = mybir.dt.float32
F32R = mybir.dt.float32r
I32 = mybir.dt.int32
U32 = mybir.dt.uint32
AX = mybir.AxisListType
ds = bass.ds

P = 128
EPS = 1e-6
HUGE = 3.0e38


class Gemm:

    def __init__(self, after, units, chunks, taker, ktiles=4):
        self.taker, self.other_taker = taker, bool(after) and after.taker != taker
        self.units, self.chunks, self.ktiles = units, chunks, ktiles
        self.chunk0 = after.chunk1 if after else 0
        self.tile0 = after.tile1 if after else 0
        self.chunk1 = self.chunk0 + units * chunks
        self.tile1 = self.tile0 + 4 * units


class Chain:

    def __init__(self, eng, sem):
        self.eng, self.sem, self.n = eng, sem, 0
        self.turn, self.per = None, 0

    def did(self, ins):
        ins.then_inc(self.sem, 1)
        self.n += 1

    def settle(self):
        self.eng.wait_ge(self.sem, self.n if self.turn is None else self.turn * self.per + self.n)

    def enter(self, turn, per):
        self.turn, self.per, self.start = turn, per, self.n

    def leave(self, turns):
        assert self.n - self.start == self.per, (self.n - self.start, self.per)
        self.n += (turns - 1) * self.per
        self.turn = None


def two_blocks(nc, A, out):
    T, D = A["x"].shape[1:]
    NT, KT = T // P, D // P
    GW = A["gm_ln_g"].shape[1]
    GG = A["gm_w_sp"].shape[1]
    GD = GW // GG
    HW = A["hg_norm_g"].shape[1]
    NH = HW // P
    HC = 64
    NE = A["w1"].shape[1]
    EG = 8
    NG = NE // EG
    FE = A["w1"].shape[3]
    PD = A["p"].shape[3]
    SBH, SBD = 8, 64
    GR = A["w_gate_up_2"].shape[1]
    DV = A["gla_norm_2"].shape[1]
    FF = A["w_ff1_2"].shape[2]
    SLOTS = 64
    ROUNDS = T // SLOTS
    PAIRS = NE // 2
    ROUTED = NG + NE
    LEVELS = 7
    assert (T, D, GW, HW, FE, DV) == (512, 1024, 512, 512, 512, 256)

    g_vi = Gemm(None, 2, 2, "act")
    g_fquo = Gemm(g_vi, 4, 2, "act")
    g_ga = Gemm(g_fquo, 2, 2, "act")
    g_gb = Gemm(g_ga, 2, 2, "act")
    g_upa = Gemm(g_gb, 2, 1, "dve")
    g_upb = Gemm(g_upa, 2, 1, "dve")
    g_out = Gemm(g_upb, 2, 2, "dve")
    g_pg = Gemm(g_out, 2, 2, "act")
    g_ple = Gemm(g_pg, 2, 1, "dve", ktiles=PD // P)
    g_qk = Gemm(g_ple, 2, 2, "act")
    g_vv = Gemm(g_qk, 3, 2, "act")
    g_gla = Gemm(g_vv, 4, 2, "act")
    g_gates = Gemm(g_gla, 4, 2, "act")
    g_psb = Gemm(g_gates, 2, 1, "dve")
    g_pgla = Gemm(g_psb, 2, 2, "dve")
    g_out2 = Gemm(g_pgla, 2, 2, "dve")
    HALVES = 2
    FH = FF // HALVES
    g_ff = []
    last = g_out2
    for _ in range(HALVES):
        up = Gemm(last, FH // 512, 2, "act")
        last = Gemm(up, 2, FH // 512, "dve")
        g_ff.append((up, last))

    h2_dram = nc.dram_tensor("moe_rows", [T, D], F32).ap()
    slot_dram = nc.dram_tensor("moe_slot_choice", [ROUNDS * P * PAIRS, 1], I32).ap()
    y_dram = nc.dram_tensor("moe_choice_out", [2 * T, D], F32).ap()

    ctx = ExitStack()
    with ctx:
        PAGE = 2048
        base = (nc.sbuf_base + 63) // 64 * 64
        ctx.enter_context(nc.sbuf_tensor("fence", [P, 103 * 512], F32))

        def at(name, page, shape, dt=F32):
            return nc.alloc_sbuf_tensor_at(name, shape, dt, offset=base + int(page * PAGE))

        def sem(name):
            return ctx.enter_context(nc.semaphore(name))

        x = at("x_tm", 0, [P, NT, D])
        small_at = [8 * PAGE]

        def small(name, shape, dt=F32):
            n = 4
            for s in shape[1:]:
                n *= s
            t = nc.alloc_sbuf_tensor_at(name, shape, dt, offset=base + small_at[0])
            small_at[0] += (n + 31) // 32 * 32
            assert small_at[0] <= 13 * PAGE, small_at
            return t

        ident = small("ident", [P, P])
        ones = small("ones", [P, T])
        earlier = small("earlier", [P, P])
        level_mask = small("level_mask", [P, LEVELS, P], I32)
        eps_col = small("eps_col", [P, 1])
        one_col = small("one_col", [P, 1])
        lb_par = small("lb_par", [P, 2, NH])
        lb = small("lb", [P, NH])
        lb_not = small("lb_not", [P, NH])
        lb_neg = small("lb_neg", [P, NH])
        hg_gain = small("hg_gain", [P, NH])
        gate_bias = small("gate_bias", [P, NH])
        gla_gain = small("gla_gain", [P, DV // P])
        ssq = small("ssq", [P, NT])
        rstd = small("rstd", [P, NT])
        ln_stats = small("ln_stats", [P, NT, 6])
        ln_mv = small("ln_mv", [P, NT, 2])
        ln_rstd = small("ln_rstd", [P, NT])
        decay = small("decay", [P, NH, T // HC])
        b_sp = small("b_sp", [GG, P])
        gate1 = small("gate1", [P, NT])
        gate2 = small("gate2", [P, NT])
        most = small("most", [P, 1], I32)
        slot_choice = small("slot_choice", [P, PAIRS], I32)
        slot_token = small("slot_token", [P, PAIRS], I32)
        choice_now = [small(f"choice_now{s}", [P, 1], I32) for s in range(2)]
        token_now = [small(f"token_now{s}", [P, 1], I32) for s in range(2)]

        act_hi = at("act_hi", 13, [P, KT, T], F32R)
        act_lo = at("act_lo", 21, [P, KT, T], F32R)
        w_stage = [at(f"w_stage{s}", 29 + 4 * s, [P, 4, 512]) for s in range(2)]
        w_hi = [at(f"w_hi{s}", 37 + 4 * s, [P, 4, 512], F32R) for s in range(2)]
        w_lo = [at(f"w_lo{s}", 45 + 4 * s, [P, 4, 512], F32R) for s in range(2)]
        xn = at("xn", 45, [P, NT, D])
        gain = at("gain", 101, [P, D])

        F = 53
        u_fm = at("u_fm", F + 0, [P, NH, T])
        v_tm = at("v_tm", F + 4, [P, NT, GW])
        q_fm = at("q_fm", F + 8, [P, NH, T])
        f_fm = at("f_fm", F + 12, [P, NH, T])
        i_tm = at("i_tm", F + 16, [P, NT, HW])
        og_fm = at("og_fm", F + 20, [P, NH, T])
        ga_fm = at("ga_fm", F + 24, [P, KT, T])
        gb_fm = at("gb_fm", F + 32, [P, KT, T])
        b_fm = at("b_fm", F + 40, [P, NH, T])
        kend_fm = at("kend_fm", F + 44, [P, NH, T])
        w_sp = at("w_sp", F + 40, [P, GG, P])
        w_spT = at("w_spT", F + 42, [P, GG, P])
        ln_g = at("ln_g", F + 44, [P, GW])
        ln_b = at("ln_b", F + 45, [P, GW])
        group_sel = at("group_sel", F + 32, [GG, GW])
        eb_fm = at("eb_fm", F + 32, [P, NH, T])
        order_xor = at("order_xor", F + 47, [P, P], I32)
        attT = at("attT", F + 4, [P, NT, NH, P])
        kend_tm = at("kend_tm", F + 40, [P, NT, HW])
        s_hg = at("s_hg", F + 12, [P, NT - 1, NH, P])
        o_fm = at("o_fm", F + 44, [P, NH, T])
        sq_fm = at("sq_fm", F + 8, [P, NH, T])
        rs_hg = at("rs_hg", F + 40, [P, T])
        head_sel = at("head_sel", F + 41, [P, NH, P])
        ring = [at(f"ring{j}", F + 4 * j, [P, 4, 512]) for j in range(12)]
        xg = [at(f"xg{s}", 13 + 2 * s, [P, D]) for s in range(2)]
        xgT = [at(f"xgT{s}", 17 + 2 * s, [P, KT, P]) for s in range(2)]
        silu_h = [at(f"silu_h{s}", 21 + s, [P, FE]) for s in range(2)]
        gated = [at(f"gated{s}", 23 + s, [P, FE]) for s in range(2)]
        gatedT = [at(f"gatedT{s}", 25 + s, [P, FE // P, P]) for s in range(2)]
        y_sb = [at(f"y_sb{s}", 45 + 2 * s, [P, D]) for s in range(2)]
        route_f = at("route_f", 33, [P, KT, P])
        route_hi = at("route_hi", 41, [P, KT, P], F32R)
        route_lo = at("route_lo", 43, [P, KT, P], F32R)
        logitT = at("logitT", 27, [P, T])
        routes_at = [37 * PAGE]

        def routes(name, shape, dt=F32):
            n = 4
            for s in shape[1:]:
                n *= s
            t = nc.alloc_sbuf_tensor_at(name, shape, dt, offset=base + routes_at[0])
            routes_at[0] += (n + 31) // 32 * 32
            assert routes_at[0] <= 41 * PAGE, routes_at
            return t

        logits = routes("logits", [P, NT, ROUTED])
        r_iota = routes("r_iota", [P, NT, NE])
        r_slot0 = routes("r_slot0", [P, NE])
        r_max = routes("r_max", [P, NT])
        r_grp = routes("r_grp", [P, NT, NG])
        r_exp = routes("r_exp", [P, NT, NG])
        r_pg = routes("r_pg", [P, NT])
        r_first = routes("r_first", [P, NT])
        r_bias = routes("r_bias", [P, NT, NG])
        r_sel = routes("r_sel", [P, NT, NE])
        r_pick = [routes(f"r_pick{n}", [P, NT, NE]) for n in range(2)]
        r_tmp = routes("r_tmp", [P, NT, NE])
        r_any = routes("r_any", [P, NT, NE])
        r_rank = routes("r_rank", [P, NT, NE])
        r_top = [routes(f"r_top{n}", [P, NT]) for n in range(2)]
        r_d = routes("r_d", [P, NT])
        r_pos = routes("r_pos", [P, 2, NT])
        r_s0 = routes("r_s0", [P, 2, NT])
        r_posi = routes("r_posi", [P, 2, NT], I32)
        r_hi = routes("r_hi", [P, 2, NT], I32)
        r_lo = routes("r_lo", [P, 2, NT], I32)
        r_slot = routes("r_slot", [P, 2, NT], I32)
        r_choice = routes("r_choice", [P, 2, NT], I32)
        r_none = routes("r_none", [P, P], I32)
        r_tot = routes("r_tot", [P, NE])
        y_in = [at(f"y_in{n}", F + 2 * n, [P, D]) for n in range(2 * NT)]
        sg_tm = at("sg_tm", F + 16, [P, NT, D])
        p_tm = at("p_tm", F + 24, [P, NT, PD])
        pT_hi = at("pT_hi", F + 26, [P, PD // P, T], F32R)
        pT_lo = at("pT_lo", F + 28, [P, PD // P, T], F32R)
        ple_t = [at(f"ple_t{s}", F + 30 + s, [P, 512]) for s in range(2)]
        sbq = at("sbq", F + 0, [P, 4, T])
        sbk = at("sbk", F + 4, [P, 4, T])
        sbv = at("sbv", F + 8, [P, NT, 512])
        gv_tm = at("gv_tm", F + 12, [P, NT, D])
        gq_fm = at("gq_fm", F + 20, [P, NH, T])
        gk_fm = at("gk_fm", F + 24, [P, NH, T])
        gout_fm = at("gout_fm", F + 28, [P, KT, T])
        sb_q = at("sb_q", F + 36, [P, T])
        sb_k = at("sb_k", F + 37, [P, T])
        sb_v = at("sb_v", F + 38, [P, NT, P])
        sb_fail = [at(f"sb_fail{s}", F + 39 + s, [P, T]) for s in range(2)]
        sb_w = [at(f"sb_w{s}", F + 41 + s, [P, T]) for s in range(2)]
        sb_later = [at(f"sb_later{s}", F + 43 + s, [P, T]) for s in range(2)]
        sb_wT = [at(f"sb_wT{s}", F + 45 + s, [P, NT, P]) for s in range(2)]
        la_fm = at("la_fm", F + 36, [P, NH, T])
        la_sum = at("la_sum", F + 44, [P, NH, T])
        low_hi = at("low_hi", F + 4, [P, KT, P], F32R)
        low_lo = at("low_lo", F + 6, [P, KT, P], F32R)
        low_f = at("low_f", F + 40, [P, KT, P])
        lowT = at("lowT", F + 42, [GR, T])
        gate_up = at("gate_up", F + 43, [GR, HW])
        gl_e = at("gl_e", F + 36, [P, NH, T])
        gl_qk = at("gl_qk", F + 40, [P, NH, T])
        g_att = at("g_att", F + 4, [P, NT, NH, P])
        gkend_tm = at("gkend_tm", F + 40, [P, NT, HW])
        s_gla = [at(f"s_gla{n}", F + 8 + 2 * n, [P, NH, DV]) for n in range(2)]
        s_gla.append(at("s_gla2", F + 36, [P, NH, DV]))
        go_a = at("go_a", F + 24, [P, 4, T])
        go_b = at("go_b", F + 44, [P, 4, T])
        gsq = [at(f"gsq{s}", F + 40 + 2 * s, [P, 2, T]) for s in range(2)]
        rs_gla = at("rs_gla", F + 38, [P, T])
        gsel = at("gsel", F + 39, [P, NH, P])
        gs_fm = at("gs_fm", F + 12, [P, KT, T])
        gg_fm = at("gg_fm", F + 4, [P, KT, T])
        hid_hi = at("hid_hi", F + 0, [P, FH // P, T], F32R)
        hid_lo = at("hid_lo", F + 16, [P, FH // P, T], F32R)
        relu_t = [at(f"relu_t{s}", F + 32 + s, [P, T]) for s in range(4)]
        relu_sq = [at(f"relu_sq{s}", F + 36 + s, [P, T]) for s in range(4)]

        bank = [ctx.enter_context(nc.psum_tensor(f"bank{b}", [P, 512], F32)) for b in range(8)]
        gb, mb = bank[:4], bank[4:]

        x_in = [sem(f"x_in{t}") for t in range(NT)]
        w_loaded = [sem(f"w_loaded{s}") for s in range(2)]
        w_hi_done, w_lo_done = sem("w_hi_done"), sem("w_lo_done")
        pe_tiles = sem("pe_tiles")
        evacuated = sem("evacuated")
        n_sq, n_var, n_sd, n_rstd = sem("n_sq"), sem("n_var"), sem("n_sd"), sem("n_rstd")
        n_xn, n_tp, n_hi, n_lo = sem("n_xn"), sem("n_tp"), sem("n_hi"), sem("n_lo")
        gain_in = sem("gain_in")
        const_pool, const_dve, params_in = sem("const_pool"), sem("const_dve"), sem("params_in")
        dve_own, act_own, pool_own = sem("dve_own"), sem("act_own"), sem("pool_own")
        lb_diff, lb_sig = sem("lb_diff"), sem("lb_sig")
        wsp_masked, wsp_turned, wspT_done = sem("wsp_masked"), sem("wsp_turned"), sem("wspT_done")
        ln_var, ln_sd, v_normed = sem("ln_var"), sem("ln_sd"), sem("v_normed")
        spatial_done, ya_done = sem("spatial_done"), sem("ya_done")
        hg_log, hg_k, hg_cum, hg_exp = sem("hg_log"), sem("hg_k"), sem("hg_cum"), sem("hg_exp")
        hg_ready, hg_att, hg_att_out = sem("hg_ready"), sem("hg_att"), sem("hg_att_out")
        att_zero, att_masked = sem("att_zero"), sem("att_masked")
        hg_scaled, kend_turned, kend_done = sem("hg_scaled"), sem("kend_turned"), sem("kend_done")
        hg_ds, hg_state = sem("hg_ds"), sem("hg_state")
        hg_o, hg_o_out, hg_sq = sem("hg_o"), sem("hg_o_out"), sem("hg_sq")
        hg_ss, hg_sd, hg_rs, hg_rsb, yb_done = (sem("hg_ss"), sem("hg_sd"), sem("hg_rs"),
                                                sem("hg_rsb"), sem("yb_done"))
        y_hi, y_lo = sem("y_hi"), sem("y_lo")
        AT_MERGED = 2 * NH
        AT_YO = AT_MERGED + KT
        AT_YG = AT_YO + NH
        AT_MIX = AT_YG + KT
        merged = sem("merged")
        route_in, route_pad, rw_hi, rw_lo = (sem("route_in"), sem("route_pad"), sem("rw_hi"),
                                             sem("rw_lo"))
        lgT_done, lgT_out, lg_done = sem("lgT_done"), sem("lgT_out"), sem("lg_done")
        r_expd = sem("r_expd")
        r_shift, r_pool = sem("r_shift"), sem("r_pool")
        picked, ranked, routed = sem("picked"), sem("ranked"), sem("routed")
        h2_stored, slots_cleared, slots_sent = sem("h2_stored"), sem("slots_cleared"), sem("slots_sent")

        moe_pe, moe_act, moe_dve = sem("moe_pe"), sem("moe_act"), sem("moe_dve")
        slots_in, tokens_done = sem("slots_in"), sem("tokens_done")
        token_copied, choice_copied, y_free = sem("token_copied"), sem("choice_copied"), sem("y_free")
        gathered = [sem(f"gathered{s}") for s in range(2)]
        ring_in = [sem(f"ring_in{j}") for j in range(6)]
        y_stored = [sem(f"y_stored{s}") for s in range(2)]
        round_done, pool_turn = sem("round_done"), sem("pool_turn")
        y_back, x_moe = [sem(f"y_back{t}") for t in range(NT)], sem("x_moe")
        p_in, p_turned, p_hi, p_lo = sem("p_in"), sem("p_turned"), sem("p_hi"), sem("p_lo")
        x_ple = sem("x_ple")
        sb_staged, sb_z, sb_sig, sb_past = sem("sb_staged"), sem("sb_z"), sem("sb_sig"), sem("sb_past")
        sb_weight, sb_turned, sb_wT_done = sem("sb_weight"), sem("sb_turned"), sem("sb_wT_done")
        sb_o, sb_o_out, sb_ones = sem("sb_o"), sem("sb_o_out"), sem("sb_ones")
        low_in, low_pad, low_split, low_z = sem("low_in"), sem("low_pad"), sem("low_split"), sem("low_z")
        lowT_done, la_z, la_act, la_dve = sem("lowT_done"), sem("la_z"), sem("la_act"), sem("la_dve")
        gl_dist, gl_exp, gl_prod, gl_mm, gl_copied = (sem("gl_dist"), sem("gl_exp"), sem("gl_prod"),
                                                      sem("gl_mm"), sem("gl_copied"))
        g_att_zero, gl_edge, gl_edge_exp, gl_scaled = (sem("g_att_zero"), sem("gl_edge"),
                                                       sem("gl_edge_exp"), sem("gl_scaled"))
        gkend_turned, gkend_done = sem("gkend_turned"), sem("gkend_done")
        gl_ds, gl_state, gl_o, gl_o_out, gl_sq = (sem("gl_ds"), sem("gl_state"), sem("gl_o"),
                                                  sem("gl_o_out"), sem("gl_sq"))
        gl_ss, gl_sd, gl_rs, gl_rsb, yg_done = (sem("gl_ss"), sem("gl_sd"), sem("gl_rs"),
                                                sem("gl_rsb"), sem("yg_done"))
        mixed = sem("mixed")
        hid_hi_done, hid_sq, hid_lo_done = sem("hid_hi_done"), sem("hid_sq"), sem("hid_lo_done")
        out_stored = sem("out_stored")

        block = ctx.enter_context(nc.Block())
        HALF = SLOTS

        ROWS_ONLY = (3, 6)

        def turned_before(n):
            return 2 * NT * (n - sum(m < n for m in ROWS_ONLY))

        def all_out(g):
            return g.tile1 + 4

        def pair_count(turn, s, round_turn):
            pair = turn * 2 + s
            return pair if round_turn is None else pair + round_turn * PAIRS

        def main_round_done(eng):
            for s in range(2):
                eng.wait_ge(y_stored[s], 16 * PAIRS // 2)

        @block.sync
        def _(sp):
            def load_chunk(c, s, w, cols, kc, ktiles=4):
                if isinstance(c, int):
                    if c >= 2:
                        sp.wait_ge(w_lo_done, c - 1)
                else:
                    sp.wait_ge(w_lo_done, c - 1)
                src = w[kc * 512:kc * 512 + ktiles * P, cols].rearrange("(k p) n -> p k n", p=P)
                sp.dma_start(w_stage[s][:, 0:ktiles, :], src).then_inc(w_loaded[s], 16)

            def load_unit(g, u, w, col):
                for kc in range(g.chunks):
                    c = g.chunk0 + u * g.chunks + kc
                    load_chunk(c, c % 2, w, slice(col, col + 512), kc, g.ktiles)

            def load_units(g, w, col, k0=0):
                if g.units * g.chunks == 2:
                    for u in range(g.units):
                        load_unit(g, u, w, col + 512 * u)
                    return
                with sp.Fori(0, g.units) as u:
                    for kc in range(g.chunks):
                        load_chunk(g.chunk0 + g.chunks * u + kc, kc % 2, w,
                                   ds(u * 512 + col, 512), k0 + kc, g.ktiles)

            def load_gain(n, g):
                if n:
                    sp.wait_ge(n_xn, NT * n)
                sp.dma_start(gain[:, :], g.rearrange("(o d) -> o d", o=1).broadcast_to([P, D]))\
                    .then_inc(gain_in, 16)

            x_dram = A["x"][0].rearrange("(t p) d -> t p d", p=P)
            for t in range(NT):
                sp.dma_start(x[:, t, :], x_dram[t]).then_inc(x_in[t], 16)
            load_gain(0, A["g_mix"][0])
            w_in = A["w_in"][0]
            load_unit(g_vi, 0, w_in, 1 * 512)
            load_unit(g_vi, 1, w_in, 4 * 512)
            for u, col in enumerate((3, 2, 0, 5)):
                load_unit(g_fquo, u, w_in, col * 512)
            load_units(g_ga, w_in, 6 * 512)
            load_units(g_gb, w_in, 8 * 512)
            load_units(g_upa, A["w_up_a"][0], 0)
            load_units(g_upb, A["w_up_b"][0], 0)
            load_units(g_out, A["w_out"][0], 0)
            load_gain(1, A["g_ffn"][0])

            sp.wait_ge(w_lo_done, g_out.chunk1)
            sp.wait_ge(route_pad, 1)
            sp.dma_start(route_f[:, :, 0:NG], A["w_grp"][0].rearrange("(k p) n -> p k n", p=P))\
                .then_inc(route_in, 16)
            sp.dma_start(route_f[:, :, NG:ROUTED], A["w_exp"][0].rearrange("(k p) n -> p k n", p=P))\
                .then_inc(route_in, 16)

            PIECE_USED = [3, 3, 4, 4, 5, 5, 6, 6, 8, 8, 9, 9]

            def load_piece(j, e0, free):
                q = j % 2
                if free is not None:
                    sp.wait_ge(moe_pe, free)
                e = e0 + q
                h = (j // 2) % 2
                if j < 8:
                    w = A["w1"] if j < 4 else A["w3"]
                    src = w[0, ds(e, 1), h * 512:(h + 1) * 512, :].rearrange("e (k p) n -> p (e k) n", p=P)
                else:
                    src = A["w2"][0, ds(e, 1), :, h * 512:(h + 1) * 512]\
                        .rearrange("e (k p) n -> p (e k) n", p=P)
                sp.dma_start(ring[j][:, :, :], src).then_inc(ring_in[j // 2], 16)

            sp.wait_ge(y_lo, AT_MERGED + KT)
            for j in range(12):
                load_piece(j, 0, None)
            for t in range(NT):
                sp.wait_ge(n_xn, NT + t + 1)
                sp.dma_start(h2_dram[t * P:(t + 1) * P, :], xn[:, t, :]).then_inc(h2_stored, 16)
            load_gain(2, A["g_ple"][0])

            with sp.Fori(0, PAIRS - 1) as i:
                for j in range(12):
                    load_piece(j, i * 2 + 2, i * 9 + (18 + PIECE_USED[j]))
            main_round_done(sp)
            sp.wait_ge(routed, 1)
            fullest = sp.value_load(most[0:1, 0:1], min_val=0, max_val=T)
            with sp.Fori(1, ROUNDS) as r:
                with sp.If(fullest > r * SLOTS):
                    with sp.Fori(0, PAIRS) as i:
                        for j in range(12):
                            load_piece(j, i * 2, i * 9 + r * (9 * PAIRS) + (9 + PIECE_USED[j]))
                    for s in range(2):
                        sp.wait_ge(y_stored[s], r * (16 * PAIRS // 2) + 16 * PAIRS // 2)
                    sp.sem_inc(round_done, 1)
            for t in range(NT):
                for c in range(2):
                    sp.dma_start(y_in[2 * t + c][:, :], y_dram[c * T + t * P:c * T + (t + 1) * P, :])\
                        .then_inc(y_back[t], 16)
            sp.dma_start(p_tm[:, :, :], A["p"][0, 0].rearrange("(t p) d -> p t d", p=P)).then_inc(p_in, 16)
            load_units(g_pg, A["w_pg"][0], 0)
            load_units(g_ple, A["w_ple"][0], 0)
            load_gain(3, A["g_final"])
            load_gain(4, A["norm_mix_2"][0])
            w_in2 = A["w_in_2"][0]
            load_units(g_qk, w_in2, 0)
            load_unit(g_vv, 0, w_in2, 2 * 512)
            for u in range(2):
                load_unit(g_vv, 1 + u, w_in2, (5 + u) * 512)
            sp.wait_ge(low_pad, 1)
            sp.dma_start(low_f[:, :, 0:GR], w_in2[:, 9 * 512:9 * 512 + GR]
                         .rearrange("(k p) n -> p k n", p=P)).then_inc(low_in, 16)
            sp.dma_start(gate_up[:, :], A["w_gate_up_2"][0]).then_inc(low_in, 16)
            for u, col in enumerate((3, 4, 7, 8)):
                load_unit(g_gla, u, w_in2, col * 512)
            load_units(g_gates, w_in2, 9 * 512 + GR)
            load_units(g_psb, A["w_proj_sb_2"][0], 0)
            load_units(g_pgla, A["w_proj_gla_2"][0], 0)
            load_units(g_out2, A["w_out_2"][0], 0)
            load_gain(5, A["norm_mlp_2"][0])
            for h, (up, down) in enumerate(g_ff):
                load_units(up, A["w_ff1_2"][0], h * FH)
                load_units(down, A["w_ff2_2"][0], 0, k0=h * FH // 512)
            load_gain(6, A["norm_final_2"])
            out_dram = out[0].rearrange("(t p) d -> t p d", p=P)
            for t in range(NT):
                sp.wait_ge(n_xn, 6 * NT + t + 1)
                sp.dma_start(out_dram[t], xn[:, t, :]).then_inc(out_stored, 16)
            sp.wait_ge(out_stored, 16 * NT)

        @block.gpsimd
        def _(pool):
            own = Chain(pool, pool_own)

            pool.dma_start(lb_par[:, :, :], A["hg_lb_param"].rearrange("l (h p) -> p l h", p=P),
                           allow_slow_non_contiguous=True).then_inc(params_in, 16)
            pool.dma_start(hg_gain[:, :], A["hg_norm_g"][0].rearrange("(h p) -> p h", p=P),
                           allow_slow_non_contiguous=True).then_inc(params_in, 16)
            pool.dma_start(gate_bias[:, :], A["b_gate_up_2"][0].rearrange("(h p) -> p h", p=P),
                           allow_slow_non_contiguous=True).then_inc(params_in, 16)
            pool.dma_start(gla_gain[:, :], A["gla_norm_2"][0].rearrange("(h p) -> p h", p=P),
                           allow_slow_non_contiguous=True).then_inc(params_in, 16)
            pool.dma_start(w_sp[:, :, :], A["gm_w_sp"][0].rearrange("g t s -> t g s")).then_inc(params_in, 16)
            pool.dma_start(b_sp[:, :], A["gm_b_sp"][0]).then_inc(params_in, 16)
            for t, name in ((ln_g, "gm_ln_g"), (ln_b, "gm_ln_b")):
                pool.dma_start(t[:, :], A[name].broadcast_to([P, GW])).then_inc(params_in, 16)

            own.did(pool.memset(ident[:, :], 0.0))
            own.did(pool.memset(earlier[:, :], 1.0))
            own.did(pool.memset(group_sel[:, :], 1.0))
            own.did(pool.iota(level_mask[:, 0, :], pattern=[[0, P]], base=0, channel_multiplier=1))
            own.did(pool.iota(level_mask[:, 1, :], pattern=[[1, P]], base=0, channel_multiplier=0))
            own.settle()
            pool.affine_select(out=ident[:, :], in_=ident[:, :], compare_op=ALU.not_equal, fill=1.0,
                               base=0, pattern=[[-1, P]], channel_multiplier=1).then_inc(const_pool, 1)
            pool.affine_select(out=earlier[:, :], in_=earlier[:, :], compare_op=ALU.is_gt, fill=0.0,
                               base=0, pattern=[[1, P]], channel_multiplier=-1).then_inc(const_pool, 1)
            pool.memset(ones[:, :], 1.0).then_inc(const_pool, 1)
            pool.memset(eps_col[:, :], EPS).then_inc(const_pool, 1)
            pool.memset(one_col[:, :], 1.0).then_inc(const_pool, 1)
            own.did(pool.affine_select(out=group_sel[:, :], in_=group_sel[:, :], compare_op=ALU.is_ge,
                                       fill=0.0, base=0, pattern=[[1, GW]], channel_multiplier=-GD))
            own.settle()
            pool.affine_select(out=group_sel[:, :], in_=group_sel[:, :], compare_op=ALU.is_ge, fill=0.0,
                               base=GD - 1, pattern=[[-1, GW]], channel_multiplier=GD)\
                .then_inc(const_pool, 1)
            pool.wait_ge(const_dve, 1)
            pool.affine_select(out=level_mask[:, 2, :], in_=level_mask[:, 2, :], compare_op=ALU.is_gt,
                               fill=0.0, base=0, pattern=[[1, P]], channel_multiplier=-1)\
                .then_inc(const_pool, 1)
            pool.wait_ge(params_in, 16 * 8)
            pool.affine_select(out=w_sp[:, :, :], in_=w_sp[:, :, :], compare_op=ALU.is_ge, fill=0.0,
                               base=0, pattern=[[0, GG], [-1, P]], channel_multiplier=1)\
                .then_inc(wsp_masked, 1)

            pool.wait_ge(ya_done, NH)
            pool.memset(attT[:, :, :, :], 0.0).then_inc(att_zero, 1)
            for t in range(NT):
                pool.wait_ge(hg_att_out, 3 * (t + 1))
                pool.affine_select(out=attT[:, t, :, :], in_=attT[:, t, :, :], compare_op=ALU.is_ge,
                                   fill=0.0, base=0, pattern=[[0, NH], [1, P]], channel_multiplier=-1)\
                    .then_inc(att_masked, 1)
            pool.wait_ge(hg_state, NH * (NT - 1))
            own.did(pool.memset(head_sel[:, :, :], 0.0))
            own.settle()
            own.did(pool.affine_select(out=head_sel[:, :, :], in_=head_sel[:, :, :],
                                       compare_op=ALU.not_equal, fill=1.0, base=0,
                                       pattern=[[-32, NH], [0, P]], channel_multiplier=1))
            own.settle()
            pool.sem_inc(r_pool, 1)

            pool.wait_ge(w_lo_done, g_out.chunk1)
            pool.memset(route_f[:, :, :], 0.0).then_inc(route_pad, 1)
            pool.wait_ge(pe_tiles, 4 * g_out.chunk1)
            opts = dict(allow_small_or_imprecise_dtypes=True)
            own.did(pool.iota(r_iota[:, :, :], pattern=[[0, NT], [1, NE]], base=0, channel_multiplier=0, **opts))
            own.did(pool.iota(r_slot0[:, :], pattern=[[1, PAIRS], [SLOTS * PAIRS, 2]], base=0,
                              channel_multiplier=0, **opts))
            own.did(pool.iota(r_choice[:, :, :], pattern=[[T, 2], [P, NT]], base=0, channel_multiplier=1))
            own.did(pool.iota(r_none[:, :], pattern=[[0, P]], base=2 * T, channel_multiplier=0))
            own.settle()
            pool.sem_inc(r_pool, 1)
            pool.dma_start(slot_dram.rearrange("(a b) o -> a (b o)", a=P), r_none[:, :])\
                .then_inc(slots_cleared, 16)
            pool.wait_ge(slots_cleared, 16)

            pool.wait_ge(routed, 1)
            for c in range(2):
                for t in range(NT):
                    pool.indirect_dma_start(slot_dram, bass.IndirectOffsetOnAxis(r_slot[:, c, t:t + 1], 0),
                                            r_choice[:, c, t:t + 1], None).then_inc(slots_sent, 16)
            pool.wait_ge(slots_sent, 16 * 2 * NT)
            pool.wait_ge(h2_stored, 16 * NT)

            def at_col(c):
                return slice(c, c + 1) if isinstance(c, int) else ds(c, 1)

            def gather_round(r):
                first = 0 if r is None else r * (P * PAIRS)
                table = slot_dram[ds(first, P * PAIRS), :] if r is not None else slot_dram[0:P * PAIRS, :]
                pool.dma_start(slot_choice[:, :], table.rearrange("(p a) o -> p (a o)", p=P))\
                    .then_inc(slots_in, 16)
                pool.wait_ge(tokens_done, 1 if r is None else r + 1)
                pool.sem_inc(pool_turn, 1)

                def half_count(i):
                    return i if r is None else i + r * (PAIRS // 2)

                def gather(i, s):
                    n = pair_count(i, s, r)
                    if not (r is None and isinstance(i, int) and i == 0):
                        pool.wait_ge(gathered[s], half_count(i) * 16)
                        pool.sem_inc(pool_turn, 1)
                    pool.tensor_copy(token_now[s][:, :], slot_token[:, at_col(i * 2 + s)]).then_inc(token_copied, 1)
                    pool.wait_ge(token_copied, n + 1)
                    pool.wait_ge(moe_pe, n * 9 + 2)
                    pool.sem_inc(pool_turn, 1)
                    pool.indirect_dma_start(xg[s][:, :], None, h2_dram,
                                            bass.IndirectOffsetOnAxis(token_now[s][:, :], 0))\
                        .then_inc(gathered[s], 16)

                def scatter(i, s):
                    n = pair_count(i, s, r)
                    if not (r is None and isinstance(i, int) and i == 0):
                        pool.wait_ge(y_stored[s], half_count(i) * 16)
                    pool.sem_inc(y_free, 1)
                    pool.tensor_copy(choice_now[s][:, :], slot_choice[:, at_col(i * 2 + s)])\
                        .then_inc(choice_copied, 1)
                    pool.wait_ge(choice_copied, n + 1)
                    pool.wait_ge(moe_act, n * 5 + 15)
                    pool.sem_inc(pool_turn, 1)
                    pool.indirect_dma_start(y_dram, bass.IndirectOffsetOnAxis(choice_now[s][:, :], 0),
                                            y_sb[s][:, :], None, bounds_check=2 * T - 1, oob_is_err=False)\
                        .then_inc(y_stored[s], 16)

                for s in range(2):
                    gather(0, s)
                first_turn = 0
                if r is None:
                    first_turn = 1
                    for s in range(2):
                        scatter(0, s)
                        gather(1, s)
                with pool.Fori(first_turn, PAIRS // 2 - 1) as i:
                    for s in range(2):
                        scatter(i, s)
                        gather(i + 1, s)
                for s in range(2):
                    scatter(PAIRS // 2 - 1, s)
                for s in range(2):
                    pool.wait_ge(y_stored[s], half_count(PAIRS // 2) * 16)
                pool.sem_inc(round_done, 1)

            gather_round(None)
            main_round_done(pool)
            fullest = pool.value_load(most[0:1, 0:1], min_val=0, max_val=T)
            with pool.Fori(1, ROUNDS) as r:
                with pool.If(fullest > r * SLOTS):
                    gather_round(r)
            pool.wait_ge(evacuated, g_vv.tile0 + 4 + 4)
            for s in range(2):
                pool.memset(sb_later[s][:, :], 1.0).then_inc(sb_ones, 1)
            with pool.Fori(0, SBH // 2) as h:
                pool.wait_ge(sb_o, h * 8 + 8)
                pool.tensor_copy(sb_q[:, :], sbq[:, ds(h, 1), :].rearrange("p o t -> p (o t)")).then_inc(sb_staged, 1)
                pool.tensor_copy(sb_k[:, :], sbk[:, ds(h, 1), :].rearrange("p o t -> p (o t)")).then_inc(sb_staged, 1)
                pool.tensor_copy(sb_v[:, :, :], sbv[:, :, ds(h * P, P)]).then_inc(sb_staged, 1)
                for n in range(8):
                    s, t = n % 2, n % 4
                    a, b = t * P, (t + 1) * P
                    pool.wait_ge(sb_sig, h * 16 + 2 * n + 4)
                    pool.sem_inc(pool_turn, 1)
                    pool.affine_select(out=sb_fail[s][:, a:b], in_=sb_fail[s][:, a:b], compare_op=ALU.is_gt,
                                       fill=1.0, base=0, pattern=[[-1, P]], channel_multiplier=1)\
                        .then_inc(sb_past, 1)
                    pool.affine_select(out=sb_w[s][:, a:b], in_=sb_w[s][:, a:b], compare_op=ALU.is_gt,
                                       fill=0.0, base=0, pattern=[[-1, P]], channel_multiplier=1)\
                        .then_inc(sb_past, 1)
            pool.wait_ge(sb_o_out, SBH // 2 + 1)
            pool.memset(low_f[:, :, :], 0.0).then_inc(low_pad, 1)
            pool.wait_ge(low_z, 1)
            pool.memset(g_att[:, :, :, :], 0.0).then_inc(g_att_zero, 1)
            pool.wait_ge(gl_state, NH * (NT - 1))
            own.did(pool.memset(gsel[:, :, :], 0.0))
            own.settle()
            own.did(pool.affine_select(out=gsel[:, :, :], in_=gsel[:, :, :],
                                       compare_op=ALU.not_equal, fill=1.0, base=0,
                                       pattern=[[-32, NH], [0, P]], channel_multiplier=1))
            own.settle()
            pool.sem_inc(r_pool, 1)

        @block.scalar
        def _(act):
            own = Chain(act, act_own)

            def split_hi(c, s, ktiles=4):
                act.wait_ge(w_loaded[s], (c // 2 + 1) * 16 if isinstance(c, int) else c * 8 + (16 - 8 * s))
                if not isinstance(c, int) or c >= 2:
                    act.wait_ge(pe_tiles, (c - 1) * 4)
                act.activation(w_hi[s][:, 0:ktiles, :], w_stage[s][:, 0:ktiles, :], ACT.Copy)\
                    .then_inc(w_hi_done, 1)

            def evac_unit(last_chunk, put):
                for j in range(4):
                    act.wait_ge(pe_tiles, last_chunk * 4 + j + 1)
                    put(j).then_inc(evacuated, 1)

            def evac_f(dst, func, scale=1.0):
                return lambda j: act.activation(dst[:, j, :], gb[j][:, :], func, scale=scale)

            def at_tile(dst, u, j):
                return dst[:, ds(u * 4 + j, 1), :].rearrange("p o t -> p (o t)")

            def norm(n, ready):
                for t in range(NT):
                    ready(t)
                    act.activation(xn[:, t, :], x[:, t, :], ACT.Square, accum_out=ssq[:, t:t + 1])\
                        .then_inc(n_sq, 1)
                act.wait_ge(n_var, n + 1)
                act.activation(rstd[:, :], ssq[:, :], ACT.Sqrt).then_inc(n_sd, 1)
                if n in ROWS_ONLY:
                    return
                for q in range(2 * NT):
                    t, b = q // 2, q % 2
                    act.wait_ge(n_tp, turned_before(n) + q + 1)
                    act.activation(act_hi[:, 4 * b:4 * b + 4, t * P:(t + 1) * P],
                                   mb[q % 4][:, :].rearrange("p (k t) -> p k t", k=4), ACT.Copy)\
                        .then_inc(n_hi, 1)

            norm(0, lambda t: act.wait_ge(x_in[t], 16))

            c = g_vi.chunk0
            split_hi(c, 0)
            split_hi(c + 1, 1)
            act.wait_ge(lb_diff, 1)
            act.activation(lb[:, :], lb_neg[:, :], ACT.Sigmoid).then_inc(lb_sig, 1)
            split_hi(c + 2, 0)
            evac_unit(c + 1, evac_f(v_tm, ACT.Gelu_apprx_tanh))
            split_hi(c + 3, 1)
            act.wait_ge(ln_var, 1)
            act.activation(ln_rstd[:, :], ln_mv[:, :, 1], ACT.Sqrt, bias=eps_col[:, 0:1]).then_inc(ln_sd, 1)
            for u, (dst, func) in enumerate(((f_fm, ACT.Sigmoid), (q_fm, ACT.Silu),
                                             (u_fm, ACT.Gelu_apprx_tanh), (og_fm, ACT.Sigmoid))):
                split_hi(g_fquo.chunk0 + 2 * u, 0)
                if u == 0:
                    evac_unit(g_vi.chunk1 - 1, evac_f(i_tm, ACT.Copy))
                else:
                    evac_unit(g_fquo.chunk0 + 2 * u - 1, evac_f(*prev))
                split_hi(g_fquo.chunk0 + 2 * u + 1, 1)
                prev = (dst, func)
            for b in range(2):
                act.wait_ge(wsp_turned, b + 1)
                act.activation(w_spT[:, 4 * b:4 * b + 4, :],
                               mb[b][:, :].rearrange("p (g t) -> p g t", g=4), ACT.Copy).then_inc(wspT_done, 1)
            split_hi(g_ga.chunk0, 0)
            evac_unit(g_fquo.chunk1 - 1, evac_f(og_fm, ACT.Sigmoid))
            split_hi(g_ga.chunk0 + 1, 1)
            act.wait_ge(ya_done, NH)
            act.wait_ge(const_dve, 2)
            for h in range(NH):
                act.activation(b_fm[:, h, :], f_fm[:, h, :], ACT.Ln, bias=lb[:, h:h + 1],
                               scale=lb_not[:, h:h + 1]).then_inc(hg_log, 1)
            split_hi(g_ga.chunk0 + 2, 0)
            evac_unit(g_ga.chunk0 + 1, evac_f(ga_fm, ACT.Sigmoid))
            split_hi(g_ga.chunk0 + 3, 1)
            act.wait_ge(hg_cum, NH * (T // HC))
            act.activation(eb_fm[:, :, :], kend_fm[:, :, :], ACT.Exp).then_inc(hg_exp, 1)
            act.activation(b_fm[:, :, :], kend_fm[:, :, :], ACT.Exp, scale=-1.0).then_inc(hg_exp, 1)
            for t in range(NT):
                act.wait_ge(att_zero, 1)
                act.wait_ge(hg_att, 2 * t + 1)
                diag = mb[2 * (t % 2)][:, :].rearrange("p (h t) -> p h t", h=NH)
                act.activation(attT[0:HC, t, :, 0:HC], diag[0:HC, :, 0:HC], ACT.Copy).then_inc(hg_att_out, 1)
                act.activation(attT[HC:P, t, :, HC:P], diag[HC:P, :, HC:P], ACT.Copy).then_inc(hg_att_out, 1)
                act.wait_ge(hg_att, 2 * t + 2)
                low = mb[2 * (t % 2) + 1][:, :].rearrange("p (h t) -> p h t", h=NH)
                act.activation(attT[0:HC, t, :, HC:P], low[0:HC, :, HC:P], ACT.Copy).then_inc(hg_att_out, 1)
            for t in range(NT):
                act.wait_ge(kend_turned, t + 1)
                act.activation(kend_tm[:, t, :], mb[t][:, :], ACT.Copy).then_inc(kend_done, 1)
            for u in range(2):
                split_hi(g_gb.chunk0 + 2 * u, 0)
                if u == 0:
                    evac_unit(g_ga.chunk1 - 1, lambda j: act.activation(ga_fm[:, 4 + j, :], gb[j][:, :], ACT.Sigmoid))
                else:
                    evac_unit(g_gb.chunk0 + 1, evac_f(gb_fm, ACT.Sigmoid))
                split_hi(g_gb.chunk0 + 2 * u + 1, 1)
            for h in range(NH):
                act.wait_ge(hg_o, h + 1)
                act.activation(o_fm[:, h, :], mb[h][:, :], ACT.Copy).then_inc(hg_o_out, 1)
                act.activation(sq_fm[:, h, :], mb[h][:, :], ACT.Square).then_inc(hg_sq, 1)
            evac_unit(g_gb.chunk1 - 1, lambda j: act.activation(gb_fm[:, 4 + j, :], gb[j][:, :], ACT.Sigmoid))
            act.wait_ge(ya_done, NH)
            for h in range(NH):
                act.activation(act_hi[:, h, :], u_fm[:, h, :], ACT.Copy).then_inc(y_hi, 1)
            act.wait_ge(hg_ss, 1)
            act.activation(rs_hg[:, :], mb[0][:, :], ACT.Sqrt, bias=eps_col[:, 0:1], scale=1.0 / P)\
                .then_inc(hg_sd, 1)
            split_hi(g_upa.chunk0, 0)
            split_hi(g_upa.chunk0 + 1, 1)
            for h in range(NH):
                act.wait_ge(yb_done, h + 1)
                act.activation(act_hi[:, 4 + h, :], o_fm[:, h, :], ACT.Copy).then_inc(y_hi, 1)
            split_hi(g_upb.chunk0, 0)
            split_hi(g_upb.chunk0 + 1, 1)
            split_hi(g_out.chunk0, 0)
            split_hi(g_out.chunk0 + 1, 1)
            act.wait_ge(pe_tiles, 4 * g_upb.chunk1)
            for k in range(KT):
                act.wait_ge(merged, k + 1)
                act.activation(act_hi[:, k, :], ga_fm[:, k, :], ACT.Copy).then_inc(y_hi, 1)
            split_hi(g_out.chunk0 + 2, 0)
            split_hi(g_out.chunk0 + 3, 1)

            norm(1, lambda t: act.wait_ge(evacuated, all_out(g_out)))
            act.wait_ge(route_in, 32)
            act.activation(route_hi[:, :, :], route_f[:, :, :], ACT.Copy).then_inc(rw_hi, 1)
            act.wait_ge(lgT_done, 1)
            act.activation(logitT[:, :], mb[0][:, :], ACT.Copy).then_inc(lgT_out, 1)
            act.wait_ge(r_shift, 1)
            act.activation(r_exp[:, :, :], r_grp[:, :, :], ACT.Exp).then_inc(r_expd, 1)
            act.wait_ge(r_shift, 2)
            act.activation(r_d[:, :], r_top[1][:, :], ACT.Exp).then_inc(r_expd, 1)

            def experts_act(r):
                with act.Fori(0, PAIRS // 2) as i:
                    for s in range(2):
                        n = pair_count(i, s, r)
                        for b in range(2):
                            act.wait_ge(moe_pe, 9 * (n + 2) + b + 1)
                            act.activation(xgT[s][:, 4 * b:4 * b + 4, :],
                                           mb[b][:, :].rearrange("p (k t) -> p k t", k=4), ACT.Copy)\
                                .then_inc(moe_act, 1)
                        act.wait_ge(moe_pe, 9 * (n + 2) + 4)
                        act.activation(silu_h[s][:, :], mb[2][:, :], ACT.Silu).then_inc(moe_act, 1)
                        act.wait_ge(y_free, n + 1)
                        for b in range(2):
                            act.wait_ge(moe_pe, 9 * (n + 2) + 8 + b)
                            act.activation(y_sb[s][:, b * 512:(b + 1) * 512], gb[1 + b][:, :], ACT.Copy)\
                                .then_inc(moe_act, 1)

            act.sem_inc(moe_act, 10)
            experts_act(None)
            main_round_done(act)
            fullest = act.value_load(most[0:1, 0:1], min_val=0, max_val=T)
            with act.Fori(1, ROUNDS) as r:
                with act.If(fullest > r * SLOTS):
                    experts_act(r)

            norm(2, lambda t: act.wait_ge(x_moe, t + 1))
            split_hi(g_pg.chunk0, 0)
            split_hi(g_pg.chunk0 + 1, 1)
            act.wait_ge(p_turned, 2)
            for b in range(2):
                act.activation(pT_hi[:, b, :], mb[b][:, :], ACT.Copy).then_inc(p_hi, 1)
            split_hi(g_pg.chunk0 + 2, 0)
            evac_unit(g_pg.chunk0 + 1, lambda j: act.activation(sg_tm[:, j, 0:512], gb[j][:, :], ACT.Sigmoid))
            split_hi(g_pg.chunk0 + 3, 1)
            split_hi(g_ple.chunk0, 0, g_ple.ktiles)
            evac_unit(g_pg.chunk1 - 1, lambda j: act.activation(sg_tm[:, j, 512:D], gb[j][:, :], ACT.Sigmoid))
            split_hi(g_ple.chunk0 + 1, 1, g_ple.ktiles)

            norm(3, lambda t: act.wait_ge(x_ple, 2 * NT))
            norm(4, lambda t: act.wait_ge(n_xn, 3 * NT + t + 1))
            split_hi(g_qk.chunk0, 0)
            split_hi(g_qk.chunk0 + 1, 1)
            units = ([(g_qk, 0, evac_f(sbq, ACT.Copy)), (g_qk, 1, evac_f(sbk, ACT.Copy)),
                      (g_vv, 0, evac_f(sbv, ACT.Copy)),
                      (g_vv, 1, lambda j: act.activation(gv_tm[:, j, 0:512], gb[j][:, :], ACT.Copy)),
                      (g_vv, 2, lambda j: act.activation(gv_tm[:, j, 512:D], gb[j][:, :], ACT.Copy))])
            for n, (g, u, put) in enumerate(units):
                c = g.chunk0 + 2 * u
                if n + 1 < len(units):
                    split_hi(c + 2, 0)
                    evac_unit(c + 1, put)
                    split_hi(c + 3, 1)
                else:
                    evac_unit(c + 1, put)

            with act.Fori(0, SBH // 2) as h:
                for n in range(8):
                    s, t = n % 2, n % 4
                    end = (t + 1) * P
                    act.wait_ge(sb_z, h * 8 + n + 1)
                    if n >= 2:
                        act.wait_ge(sb_turned, h * 8 + n - 1)
                    act.activation(sb_fail[s][:, 0:end], gb[s][:, 0:end], ACT.Sigmoid, scale=-SBD ** -0.5)\
                        .then_inc(sb_sig, 1)
                    act.activation(sb_w[s][:, 0:end], gb[s][:, 0:end], ACT.Sigmoid, scale=SBD ** -0.5)\
                        .then_inc(sb_sig, 1)
                act.wait_ge(sb_o, h * 8 + 16)
                act.activation(sbq[:, ds(h, 1), :].rearrange("p o t -> p (o t)"), mb[2][:, :], ACT.Copy)\
                    .then_inc(sb_o_out, 1)

            act.wait_ge(low_in, 32)
            act.activation(low_hi[:, :, :], low_f[:, :, :], ACT.Copy).then_inc(low_split, 1)
            act.wait_ge(low_z, 1)
            act.activation(lowT[:, :], mb[0][0:GR, :], ACT.Copy).then_inc(lowT_done, 1)
            for h in range(NH):
                act.wait_ge(la_z, h + 1)
                own.did(act.activation(la_sum[:, h, :], mb[h][:, :], ACT.Abs, bias=gate_bias[:, h:h + 1]))
                own.settle()
                own.did(act.activation(la_sum[:, h, :], la_sum[:, h, :], ACT.Exp, scale=-1.0))
                own.settle()
                act.activation(la_sum[:, h, :], la_sum[:, h, :], ACT.Ln, bias=one_col[:, 0:1]).then_inc(la_act, 1)
            split_hi(g_gla.chunk0, 0)
            split_hi(g_gla.chunk0 + 1, 1)
            units = ([(g_gla, 0, evac_f(gq_fm, ACT.Copy, scale=float(P) ** -0.5)), (g_gla, 1, evac_f(gk_fm, ACT.Copy)),
                      (g_gla, 2, lambda j: act.activation(gout_fm[:, j, :], gb[j][:, :], ACT.Silu)),
                      (g_gla, 3, lambda j: act.activation(gout_fm[:, 4 + j, :], gb[j][:, :], ACT.Silu))])
            for n, (g, u, put) in enumerate(units):
                c = g.chunk0 + 2 * u
                split_hi(c + 2, 0)
                evac_unit(c + 1, put)
                split_hi(c + 3, 1)
            for n in range(LEVELS):
                act.wait_ge(gl_dist, 2 * n + 2)
                act.activation(gl_e[:, :, :], gl_e[:, :, :], ACT.Exp, scale=1.0 / 16).then_inc(gl_exp, 1)
            act.wait_ge(gl_edge, 1)
            act.activation(gl_e[:, :, :], la_sum[:, :, :], ACT.Exp, scale=1.0 / 16).then_inc(gl_edge_exp, 1)
            act.activation(gl_qk[:, :, :], gl_qk[:, :, :], ACT.Exp, scale=1.0 / 16).then_inc(gl_edge_exp, 1)
            act.activation(decay[:, :, 0:NT], la_sum[:, :, P - 1:T:P], ACT.Exp, scale=1.0 / 16)\
                .then_inc(gl_edge_exp, 1)
            for t in range(NT):
                act.wait_ge(gkend_turned, t + 1)
                act.activation(gkend_tm[:, t, :], mb[t][:, :], ACT.Copy).then_inc(gkend_done, 1)
            for n in range(KT):
                h, o = n // 2, (go_a if n < 4 else go_b)
                act.wait_ge(gl_o, n + 1)
                act.activation(o[:, n % 4, :], mb[n % 2][:, :], ACT.Copy).then_inc(gl_o_out, 1)
                if n >= 4:
                    act.wait_ge(gl_ss, h - 1)
                act.activation(gsq[h % 2][:, n % 2, :], mb[n % 2][:, :], ACT.Square).then_inc(gl_sq, 1)
            act.wait_ge(gl_ss, NH)
            act.activation(rs_gla[:, :], mb[2][:, :], ACT.Sqrt, bias=eps_col[:, 0:1], scale=1.0 / DV)\
                .then_inc(gl_sd, 1)
            for u in range(4):
                dst = gs_fm if u < 2 else gg_fm
                c = g_gates.chunk0 + 2 * u
                if u < 3:
                    split_hi(c + 2, 0)
                evac_unit(c + 1, lambda j, u=u, dst=dst: act.activation(dst[:, 4 * (u % 2) + j, :], gb[j][:, :],
                                                                         ACT.Sigmoid))
                if u < 3:
                    split_hi(c + 3, 1)
            for h in range(4):
                act.activation(act_hi[:, h, :], sbq[:, h, :], ACT.Copy).then_inc(y_hi, 1)
            split_hi(g_psb.chunk0, 0)
            split_hi(g_psb.chunk0 + 1, 1)
            act.wait_ge(pe_tiles, 4 * g_psb.chunk1)
            for k in range(KT):
                o = go_a if k < 4 else go_b
                act.wait_ge(yg_done, k + 1)
                act.activation(act_hi[:, k, :], o[:, k % 4, :], ACT.Copy).then_inc(y_hi, 1)
            for u in range(2):
                split_hi(g_pgla.chunk0 + 2 * u, 0)
                split_hi(g_pgla.chunk0 + 2 * u + 1, 1)
            split_hi(g_out2.chunk0, 0)
            split_hi(g_out2.chunk0 + 1, 1)
            act.wait_ge(pe_tiles, 4 * g_pgla.chunk1)
            for k in range(KT):
                act.wait_ge(mixed, k + 1)
                act.activation(act_hi[:, k, :], gs_fm[:, k, :], ACT.Copy).then_inc(y_hi, 1)
            split_hi(g_out2.chunk0 + 2, 0)
            split_hi(g_out2.chunk0 + 3, 1)

            norm(5, lambda t: act.wait_ge(evacuated, all_out(g_out2)))

            def relu_unit(h, u, chunk):
                for j in range(4):
                    act.wait_ge(pe_tiles, chunk * 4 + j + 1)
                    seen = u * 4 + (j + 1) + (4 * up.units * h - 4)
                    if not (h == 0 and isinstance(u, int) and u == 0):
                        act.wait_ge(hid_sq, seen)
                    act.activation(relu_t[j][:, :], gb[j][:, :], ACT.Relu).then_inc(evacuated, 1)
                for j in range(4):
                    act.wait_ge(evacuated, (u * 4) + up.tile0 + 4 + j + 1)
                    if h:
                        act.wait_ge(pe_tiles, 4 * g_ff[h - 1][1].chunk1)
                    act.activation(at_tile(hid_hi, u, j), relu_t[j][:, :], ACT.Square).then_inc(hid_hi_done, 1)

            for h, (up, down) in enumerate(g_ff):
                split_hi(up.chunk0, 0)
                split_hi(up.chunk0 + 1, 1)
                split_hi(up.chunk0 + 2, 0)
                relu_unit(h, 0, up.chunk0 + 1)
                split_hi(up.chunk0 + 3, 1)
                with act.Fori(2, up.units) as u:
                    split_hi(u * 2 + up.chunk0, 0)
                    relu_unit(h, u - 1, u * 2 + (up.chunk0 - 1))
                    split_hi(u * 2 + up.chunk0 + 1, 1)
                split_hi(down.chunk0, 0)
                relu_unit(h, up.units - 1, up.chunk1 - 1)
                split_hi(down.chunk0 + 1, 1)
                with act.Fori(1, down.units * down.chunks // 2) as i:
                    for s in range(2):
                        split_hi(i * 2 + down.chunk0 + s, s)
            norm(6, lambda t: act.wait_ge(evacuated, all_out(g_ff[-1][1])))

        @block.vector
        def _(dve):
            own = Chain(dve, dve_own)

            def split_lo(c, s, ktiles=4):
                dve.wait_ge(w_hi_done, c + 1)
                dve.tensor_tensor(w_lo[s][:, 0:ktiles, :], w_stage[s][:, 0:ktiles, :],
                                  w_hi[s][:, 0:ktiles, :].bitcast(F32), ALU.subtract).then_inc(w_lo_done, 1)

            def split_los(g):
                n = g.units * g.chunks // 2
                if n == 1:
                    for s in range(2):
                        split_lo(g.chunk0 + s, s, g.ktiles)
                    return
                with dve.Fori(0, n) as i:
                    for s in range(2):
                        split_lo(i * 2 + g.chunk0 + s, s, g.ktiles)

            def rest(dst, src, hi):
                return dve.tensor_tensor(dst, src, hi.bitcast(F32), ALU.subtract)

            def norm(n):
                dve.wait_ge(n_sq, NT * (n + 1))
                dve.tensor_scalar(ssq[:, :], ssq[:, :], 1.0 / D, EPS, ALU.mult, ALU.add).then_inc(n_var, 1)
                dve.wait_ge(n_sd, n + 1)
                dve.reciprocal(rstd[:, :], rstd[:, :]).then_inc(n_rstd, 1)
                dve.wait_ge(n_rstd, n + 1)
                dve.wait_ge(gain_in, 16 * (n + 1))
                for t in range(NT):
                    dst = x if n == 3 else xn
                    dve.scalar_tensor_tensor(dst[:, t, :], x[:, t, :], rstd[:, t:t + 1], gain[:, :],
                                             ALU.mult, ALU.mult).then_inc(n_xn, 1)
                if n in ROWS_ONLY:
                    return
                for q in range(2 * NT):
                    t, b = q // 2, q % 2
                    dve.wait_ge(n_hi, turned_before(n) + q + 1)
                    rest(act_lo[:, 4 * b:4 * b + 4, t * P:(t + 1) * P],
                         mb[q % 4][:, :].rearrange("p (k t) -> p k t", k=4),
                         act_hi[:, 4 * b:4 * b + 4, t * P:(t + 1) * P]).then_inc(n_lo, 1)

            def evac_unit(last_chunk, put):
                for j in range(4):
                    dve.wait_ge(pe_tiles, last_chunk * 4 + j + 1)
                    put(j)

            dve.wait_ge(const_pool, 5)
            dve.wait_ge(pool_own, 5)
            dve.tensor_tensor(level_mask[:, 2, :], level_mask[:, 0, :], level_mask[:, 1, :],
                              ALU.bitwise_xor).then_inc(const_dve, 1)

            norm(0)
            dve.wait_ge(const_pool, 7)
            own.did(dve.tensor_copy(order_xor[:, :], level_mask[:, 2, :]))
            for n in range(LEVELS):
                own.settle()
                own.did(dve.tensor_scalar(level_mask[:, n, :], order_xor[:, :], n, None, ALU.arith_shift_right))
            own.settle()
            own.did(dve.tensor_scalar(level_mask[:, :, :], level_mask[:, :, :], 1, None, ALU.is_equal))
            split_lo(0, 0)
            split_lo(1, 1)
            dve.wait_ge(params_in, 16 * 8)
            dve.tensor_tensor(lb_neg[:, :], lb_par[:, 0, :], lb_par[:, 1, :], ALU.subtract).then_inc(lb_diff, 1)
            dve.wait_ge(lb_sig, 1)
            own.did(dve.tensor_scalar(lb_neg[:, :], lb[:, :], -1.0, None, ALU.add))
            dve.tensor_scalar(lb_not[:, :], lb[:, :], -1.0, 1.0, ALU.mult, ALU.add).then_inc(const_dve, 1)
            split_lo(2, 0)
            for t in range(NT):
                dve.wait_ge(evacuated, 4 + t + 1)
                own.did(dve.bn_stats(ln_stats[:, t, :], v_tm[:, t, :]))
            for t in range(NT):
                own.settle()
                if t < NT - 1:
                    own.did(dve.bn_aggr(ln_mv[:, t, :], ln_stats[:, t, :]))
                else:
                    dve.bn_aggr(ln_mv[:, t, :], ln_stats[:, t, :]).then_inc(ln_var, 1)
            split_lo(3, 1)
            dve.wait_ge(ln_sd, 1)
            own.did(dve.reciprocal(ln_rstd[:, :], ln_rstd[:, :]))
            own.settle()
            for t in range(NT):
                own.did(dve.tensor_scalar(v_tm[:, t, :], v_tm[:, t, :], ln_mv[:, t, 0:1], ln_rstd[:, t:t + 1],
                                          ALU.subtract, ALU.mult))
                own.settle()
                own.did(dve.tensor_tensor(v_tm[:, t, :], v_tm[:, t, :], ln_g[:, :], ALU.mult))
                own.settle()
                dve.tensor_tensor(v_tm[:, t, :], v_tm[:, t, :], ln_b[:, :], ALU.add).then_inc(v_normed, 1)
            split_los(g_fquo)
            split_lo(g_ga.chunk0, 0)
            dve.wait_ge(evacuated, g_fquo.tile0 + 4 + 12)
            for j in range(NH):
                dve.wait_ge(spatial_done, j + 1)
                dve.tensor_tensor(u_fm[:, j, :], u_fm[:, j, :], mb[j][:, :], ALU.mult).then_inc(ya_done, 1)
            split_lo(g_ga.chunk0 + 1, 1)
            for h in range(NH):
                dve.wait_ge(hg_log, h + 1)
                for c in range(T // HC):
                    dve.tensor_tensor_scan(kend_fm[:, h, c * HC:(c + 1) * HC], ones[:, 0:HC],
                                           b_fm[:, h, c * HC:(c + 1) * HC], 0.0, ALU.mult, ALU.add)\
                        .then_inc(hg_cum, 1)
            split_lo(g_ga.chunk0 + 2, 0)
            for h in range(NH):
                own.did(dve.tensor_scalar(f_fm[:, h, :], f_fm[:, h, :], lb_neg[:, h:h + 1], lb_not[:, h:h + 1],
                                          ALU.mult, ALU.add))
            split_lo(g_ga.chunk0 + 3, 1)
            dve.wait_ge(hg_exp, 2)
            own.settle()
            dve.tensor_tensor(q_fm[:, :, :], q_fm[:, :, :], eb_fm[:, :, :], ALU.mult).then_inc(hg_ready, 1)
            dve.tensor_tensor(f_fm[:, :, :], f_fm[:, :, :], b_fm[:, :, :], ALU.mult).then_inc(hg_ready, 1)
            own.did(dve.tensor_copy(decay[:, :, :], eb_fm[:, :, HC - 1:T:HC]))
            dve.wait_ge(hg_ready, 2)
            own.settle()
            last = decay[:, :, :].rearrange("p h (c o) -> p (h c) o", o=1).broadcast_to([P, NH * (T // HC), HC])
            dve.tensor_tensor(kend_fm[:, :, :].rearrange("p h (c t) -> p (h c) t", t=HC),
                              f_fm[:, :, :].rearrange("p h (c t) -> p (h c) t", t=HC), last,
                              ALU.mult).then_inc(hg_ready, 1)
            dve.wait_ge(hg_att, 2 * NT)
            dve.wait_ge(hg_ready, 3)
            q2 = q_fm[:, :, :].rearrange("p h (c t) -> p (h c) t", t=HC)
            k2 = kend_fm[:, :, :].rearrange("p h (c t) -> p (h c) t", t=HC)
            dl = decay[:, :, :].rearrange("p h (c o) -> p (h c) o", o=1)
            half = [P, NH * NT, HC]
            dve.tensor_tensor(k2[:, 0::2, :], k2[:, 0::2, :], dl[:, 1::2, :].broadcast_to(half), ALU.mult)\
                .then_inc(hg_scaled, 1)
            dve.tensor_tensor(q2[:, 1::2, :], q2[:, 1::2, :], dl[:, 0::2, :].broadcast_to(half), ALU.mult)\
                .then_inc(hg_scaled, 1)
            own.did(dve.tensor_tensor(ln_stats[:, :, 0:NH], decay[:, :, 0::2].rearrange("p h c -> p c h"),
                                      decay[:, :, 1::2].rearrange("p h c -> p c h"), ALU.mult))
            own.settle()
            for u in range(2):
                for s in range(2):
                    split_lo(g_gb.chunk0 + 2 * u + s, s)
            for t in range(NT - 1):
                for h in range(NH):
                    dve.wait_ge(hg_ds, t + 1)
                    ds_h = mb[t][:, h * P:(h + 1) * P]
                    if t == 0:
                        dve.tensor_copy(s_hg[:, 0, h, :], ds_h).then_inc(hg_state, 1)
                    else:
                        dve.wait_ge(hg_state, NH * (t - 1) + h + 1)
                        dve.scalar_tensor_tensor(s_hg[:, t, h, :], s_hg[:, t - 1, h, :], ln_stats[:, t, h:h + 1],
                                                 ds_h, ALU.mult, ALU.add).then_inc(hg_state, 1)
            for h in range(NH):
                dve.wait_ge(y_hi, h + 1)
                rest(act_lo[:, h, :], u_fm[:, h, :], act_hi[:, h, :]).then_inc(y_lo, 1)
            dve.wait_ge(hg_sd, 1)
            dve.reciprocal(rs_hg[:, :], rs_hg[:, :]).then_inc(hg_rs, 1)
            split_los(g_upa)
            for h in range(NH):
                dve.wait_ge(hg_rsb, h + 1)
                own.did(dve.scalar_tensor_tensor(o_fm[:, h, :], o_fm[:, h, :], hg_gain[:, h:h + 1], mb[h][:, :],
                                                 ALU.mult, ALU.mult))
                own.settle()
                dve.tensor_tensor(o_fm[:, h, :], o_fm[:, h, :], og_fm[:, h, :], ALU.mult).then_inc(yb_done, 1)
            for h in range(NH):
                dve.wait_ge(y_hi, NH + h + 1)
                rest(act_lo[:, 4 + h, :], o_fm[:, h, :], act_hi[:, 4 + h, :]).then_inc(y_lo, 1)

            def gate_tile(dst, k, j):
                return dve.tensor_tensor(dst[:, k, :], dst[:, k, :], gb[j][:, :], ALU.mult).then_inc(evacuated, 1)

            evac_unit(g_upa.chunk0, lambda j: gate_tile(ga_fm, j, j))
            split_lo(g_upb.chunk0, 0)
            evac_unit(g_upa.chunk0 + 1, lambda j: gate_tile(ga_fm, 4 + j, j))
            split_lo(g_upb.chunk0 + 1, 1)
            for u in range(2):
                def both(j, u=u):
                    gate_tile(gb_fm, 4 * u + j, j)
                    dve.wait_ge(evacuated, g_upb.tile0 + 4 + 4 * u + j + 1)
                    dve.tensor_tensor(ga_fm[:, 4 * u + j, :], ga_fm[:, 4 * u + j, :], gb_fm[:, 4 * u + j, :],
                                      ALU.add).then_inc(merged, 1)

                evac_unit(g_upb.chunk0 + u, both)
                split_lo(g_out.chunk0 + u, u)
            for k in range(KT):
                dve.wait_ge(y_hi, AT_MERGED + k + 1)
                rest(act_lo[:, k, :], ga_fm[:, k, :], act_hi[:, k, :]).then_inc(y_lo, 1)

            def add_tile(u, j, width=512):
                xt = x[:, j, u * 512:(u + 1) * 512]
                return dve.tensor_tensor(xt, xt, gb[j][:, :], ALU.add)

            split_lo(g_out.chunk0 + 2, 0)
            evac_unit(g_out.chunk0 + 1, lambda j: add_tile(0, j).then_inc(evacuated, 1))
            split_lo(g_out.chunk0 + 3, 1)
            evac_unit(g_out.chunk1 - 1, lambda j: add_tile(1, j).then_inc(evacuated, 1))

            norm(1)
            dve.wait_ge(rw_hi, 1)
            rest(route_lo[:, :, :], route_f[:, :, :], route_hi[:, :, :]).then_inc(rw_lo, 1)
            dve.wait_ge(lg_done, 1)
            own.did(dve.tensor_copy(logits[:, :, :], mb[1][:, 0:NT * ROUTED].rearrange("p (t e) -> p t e", t=NT)))
            own.settle()
            dve.wait_ge(r_pool, 2)
            grp = logits[:, :, 0:NG]

            def per_token(v, n):
                return v.rearrange("p (t o) -> p t o", o=1).broadcast_to([P, NT, n])

            def did(ins):
                own.did(ins)
                own.settle()

            def first_of_max(pick, values, best, index, n, spare):
                did(dve.tensor_tensor(pick, values, per_token(best, n), ALU.is_equal))
                did(dve.scalar_tensor_tensor(spare, pick, -64.0, index, ALU.mult, ALU.add))
                did(dve.tensor_reduce(r_first[:, :], spare, AX.X, ALU.min))
                did(dve.tensor_tensor(pick, spare, per_token(r_first[:, :], n), ALU.is_equal))

            did(dve.tensor_reduce(r_max[:, :], grp, AX.X, ALU.max))
            dve.tensor_tensor(r_grp[:, :, :], grp, per_token(r_max[:, :], NG), ALU.subtract).then_inc(r_shift, 1)
            dve.wait_ge(r_expd, 1)
            did(dve.tensor_reduce(r_pg[:, :], r_exp[:, :, :], AX.X, ALU.add))
            did(dve.reciprocal(r_pg[:, :], r_pg[:, :]))
            first_of_max(r_grp[:, :, :], grp, r_max[:, :], r_iota[:, :, 0:NG], NG, r_bias[:, :, :])
            did(dve.tensor_scalar(r_bias[:, :, :], r_grp[:, :, :], -1.0, HUGE, ALU.add, ALU.mult))
            by_group = [P, NT * NG, EG]
            did(dve.tensor_copy(r_sel[:, :, :], logits[:, :, NG:ROUTED]))
            sel = r_sel[:, :, :].rearrange("p t (g e) -> p (t g) e", g=NG)
            for op, m in ((ALU.mult, r_grp), (ALU.add, r_bias)):
                did(dve.tensor_tensor(sel, sel, m[:, :, :].rearrange("p t (g o) -> p (t g) o", o=1)
                                      .broadcast_to(by_group), op))
            for n in range(2):
                did(dve.tensor_reduce(r_top[n][:, :], r_sel[:, :, :], AX.X, ALU.max))
                first_of_max(r_pick[n][:, :, :], r_sel[:, :, :], r_top[n][:, :], r_iota[:, :, :], NE, r_tmp[:, :, :])
                if n == 0:
                    did(dve.scalar_tensor_tensor(r_sel[:, :, :], r_pick[0][:, :, :], -HUGE, r_sel[:, :, :],
                                                 ALU.mult, ALU.add))
            dve.tensor_tensor(r_any[:, :, :], r_pick[0][:, :, :], r_pick[1][:, :, :], ALU.add).then_inc(picked, 1)
            dve.tensor_tensor(r_top[1][:, :], r_top[1][:, :], r_top[0][:, :], ALU.subtract).then_inc(r_shift, 1)
            dve.wait_ge(r_expd, 2)
            did(dve.tensor_scalar(gate1[:, :], r_d[:, :], 1.0, None, ALU.add))
            did(dve.reciprocal(gate1[:, :], gate1[:, :]))
            did(dve.tensor_tensor(gate1[:, :], gate1[:, :], r_pg[:, :], ALU.mult))
            did(dve.tensor_tensor(gate2[:, :], gate1[:, :], r_d[:, :], ALU.mult))
            dve.wait_ge(ranked, 1)
            ranks = mb[2][:, 0:NT * NE].rearrange("p (t e) -> p t e", t=NT)
            totals = mb[3][:, 0:NT * NE].rearrange("p (t e) -> p t e", t=NT)
            did(dve.tensor_copy(r_rank[:, :, :], ranks))
            did(dve.tensor_copy(r_tot[:, :], totals[:, 0, :]))
            for t in range(1, NT):
                did(dve.tensor_tensor(r_rank[:, t, :], r_rank[:, t, :], r_tot[:, :], ALU.add))
                did(dve.tensor_tensor(r_tot[:, :], r_tot[:, :], totals[:, t, :], ALU.add))
            did(dve.tensor_reduce(r_max[:, 0:1], r_tot[:, :], AX.X, ALU.max))
            did(dve.tensor_copy(most[:, :], r_max[:, 0:1]))
            for n in range(2):
                for src, dst in ((r_rank[:, :, :], r_pos),
                                 (r_slot0[:, :].rearrange("p (o e) -> p o e", o=1).broadcast_to([P, NT, NE]), r_s0)):
                    did(dve.tensor_tensor(r_tmp[:, :, :], r_pick[n][:, :, :], src, ALU.mult))
                    did(dve.tensor_reduce(dst[:, n, :], r_tmp[:, :, :], AX.X, ALU.add))
            did(dve.tensor_copy(r_posi[:, :, :], r_pos[:, :, :]))
            did(dve.tensor_scalar(r_hi[:, :, :], r_posi[:, :, :], SLOTS.bit_length() - 1, None, ALU.arith_shift_right))
            did(dve.tensor_scalar(r_lo[:, :, :], r_posi[:, :, :], SLOTS - 1, None, ALU.bitwise_and))
            did(dve.scalar_tensor_tensor(r_s0[:, :, :], r_hi[:, :, :], float(P * PAIRS), r_s0[:, :, :],
                                         ALU.mult, ALU.add))
            did(dve.scalar_tensor_tensor(r_slot[:, :, :], r_lo[:, :, :], float(PAIRS), r_s0[:, :, :],
                                         ALU.mult, ALU.add))
            dve.sem_inc(routed, 1)

            def experts_dve(r):
                dve.wait_ge(slots_in, 16 if r is None else r * 16 + 16)
                dve.tensor_scalar(slot_token[:, :], slot_choice[:, :], T - 1, None, ALU.bitwise_and)\
                    .then_inc(tokens_done, 1)
                with dve.Fori(0, PAIRS // 2) as i:
                    for s in range(2):
                        n = pair_count(i, s, r)
                        dve.wait_ge(moe_act, 5 * (n + 2) + 3)
                        dve.wait_ge(moe_pe, 9 * (n + 2) + 6)
                        dve.tensor_tensor(gated[s][:, :], silu_h[s][:, :], mb[3][:, :], ALU.mult).then_inc(moe_dve, 1)
                        dve.wait_ge(moe_pe, 9 * (n + 2) + 7)
                        dve.tensor_copy(gatedT[s][:, :, :], gb[0][:, :].rearrange("p (k t) -> p k t", k=4))\
                            .then_inc(moe_dve, 1)

            dve.sem_inc(moe_dve, 4)
            experts_dve(None)
            main_round_done(dve)
            fullest = dve.value_load(most[0:1, 0:1], min_val=0, max_val=T)
            with dve.Fori(1, ROUNDS) as r:
                with dve.If(fullest > r * SLOTS):
                    experts_dve(r)
            for t in range(NT):
                dve.wait_ge(y_back[t], 32)
                own.did(dve.scalar_tensor_tensor(x[:, t, :], y_in[2 * t][:, :], gate1[:, t:t + 1], x[:, t, :],
                                                 ALU.mult, ALU.add))
                own.settle()
                dve.scalar_tensor_tensor(x[:, t, :], y_in[2 * t + 1][:, :], gate2[:, t:t + 1], x[:, t, :],
                                         ALU.mult, ALU.add).then_inc(x_moe, 1)

            norm(2)
            split_lo(g_pg.chunk0, 0)
            split_lo(g_pg.chunk0 + 1, 1)
            for b in range(2):
                dve.wait_ge(p_hi, b + 1)
                rest(pT_lo[:, b, :], mb[b][:, :], pT_hi[:, b, :]).then_inc(p_lo, 1)
            split_lo(g_pg.chunk0 + 2, 0)
            split_lo(g_pg.chunk0 + 3, 1)
            split_los(g_ple)
            dve.wait_ge(evacuated, all_out(g_pg))
            for u in range(2):
                for j in range(4):
                    dve.wait_ge(pe_tiles, 4 * (g_ple.chunk0 + u) + j + 1)
                    if u or j >= 2:
                        dve.wait_ge(x_ple, 4 * u + j - 1)
                    dve.tensor_tensor(ple_t[j % 2][:, :], gb[j][:, :], sg_tm[:, j, u * 512:(u + 1) * 512], ALU.mult)\
                        .then_inc(evacuated, 1)
                    dve.wait_ge(evacuated, g_ple.tile0 + 4 + 4 * u + j + 1)
                    xt = x[:, j, u * 512:(u + 1) * 512]
                    dve.tensor_tensor(xt, xt, ple_t[j % 2][:, :], ALU.add).then_inc(x_ple, 1)

            norm(3)
            norm(4)
            split_los(g_qk)
            split_los(g_vv)
            dve.wait_ge(sb_ones, 2)
            own.enter(None, 0)
            with dve.Fori(0, SBH // 2) as h:
                def turned_out(n):
                    s, t = n % 2, n % 4
                    dve.wait_ge(sb_turned, h * 8 + n + 1)
                    dve.tensor_copy(sb_wT[s][:, 0:t + 1, :],
                                    mb[s][:, 0:(t + 1) * P].rearrange("p (k t) -> p k t", t=P)).then_inc(sb_wT_done, 1)

                for n in range(8):
                    s, t = n % 2, n % 4
                    end = (t + 1) * P
                    dve.wait_ge(sb_past, h * 16 + 2 * n + 2)
                    dve.tensor_tensor_scan(sb_later[s][:, end - 2::-1], sb_fail[s][:, end - 1:0:-1],
                                           ones[:, 0:end - 1], 1.0, ALU.mult, ALU.mult).then_inc(sb_weight, 1)
                    dve.wait_ge(sb_weight, h * 16 + 2 * n + 1)
                    dve.tensor_tensor(sb_w[s][:, 0:end], sb_w[s][:, 0:end], sb_later[s][:, 0:end], ALU.mult)\
                        .then_inc(sb_weight, 1)
                    turned_out(n)
            dve.wait_ge(low_split, 1)
            rest(low_lo[:, :, :], low_f[:, :, :], low_hi[:, :, :]).then_inc(low_split, 1)
            for h in range(NH):
                dve.wait_ge(la_z, h + 1)
                dve.wait_ge(la_act, h + 1)
                own.did(dve.tensor_scalar(la_fm[:, h, :], mb[h][:, :], gate_bias[:, h:h + 1], 0.0, ALU.add, ALU.min))
                own.settle()
                dve.tensor_tensor(la_fm[:, h, :], la_fm[:, h, :], la_sum[:, h, :], ALU.subtract).then_inc(la_dve, 1)
            dve.wait_ge(la_dve, NH)
            for h in range(NH):
                for t in range(NT):
                    own.did(dve.tensor_tensor_scan(la_sum[:, h, t * P:(t + 1) * P], ones[:, 0:P],
                                                   la_fm[:, h, t * P:(t + 1) * P], 0.0, ALU.mult, ALU.add))
            own.settle()
            split_los(g_gla)
            split_lo(g_gates.chunk0, 0)
            split_lo(g_gates.chunk0 + 1, 1)
            dve.wait_ge(evacuated, g_gla.tile0 + 4 + 8)
            dve.wait_ge(g_att_zero, 1)

            def copy_scores(n):
                for t in range(NT):
                    dve.wait_ge(gl_mm, NT * n + t + 1)
                    mask = (level_mask[:, n, :] if n < LEVELS else ident[:, :].bitcast(I32))
                    dve.copy_predicated(g_att[:, t, :, :],
                                        mask.rearrange("p (o t) -> p o t", o=1).broadcast_to([P, NH, P]),
                                        mb[t][:, :].rearrange("p (h t) -> p h t", h=NH)).then_inc(gl_copied, 1)

            for n in range(LEVELS):
                m = 1 << n
                blocks = NH * T // (2 * m)
                def halves(a):
                    v = a[:, :, :].rearrange("p h (c t) -> p (h c) t", t=2 * m)
                    return v[:, :, 0:m], v[:, :, m:2 * m], v[:, :, m - 1:m].broadcast_to([P, blocks, m])
                (b0, b1, mid), (e0, e1, _), (k0, _, _), (_, q1, _), (qk0, qk1, _) = (
                    halves(a) for a in (la_sum, gl_e, gk_fm, gq_fm, gl_qk))
                if n:
                    dve.wait_ge(gl_prod, 2 * n)
                dve.tensor_tensor(e0, mid, b0, ALU.subtract).then_inc(gl_dist, 1)
                dve.tensor_tensor(e1, b1, mid, ALU.subtract).then_inc(gl_dist, 1)
                dve.wait_ge(gl_exp, n + 1)
                if n:
                    dve.wait_ge(gl_mm, NT * n)
                dve.tensor_tensor(qk0, e0, k0, ALU.mult).then_inc(gl_prod, 1)
                dve.tensor_tensor(qk1, e1, q1, ALU.mult).then_inc(gl_prod, 1)
                copy_scores(n)
            copy_scores(LEVELS)
            dve.wait_ge(gl_prod, 2 * LEVELS)
            by_tile = "p h (c t) -> p (h c) t"
            sums = la_sum[:, :, :].rearrange(by_tile, t=P)
            dve.tensor_tensor(gl_qk[:, :, :].rearrange(by_tile, t=P), sums[:, :, P - 1:P].broadcast_to([P, NH * NT, P]),
                              sums, ALU.subtract).then_inc(gl_edge, 1)
            dve.wait_ge(gl_edge_exp, 3)
            dve.tensor_tensor(gk_fm[:, :, :], gk_fm[:, :, :], gl_qk[:, :, :], ALU.mult).then_inc(gl_scaled, 1)
            dve.tensor_tensor(gq_fm[:, :, :], gq_fm[:, :, :], gl_e[:, :, :], ALU.mult).then_inc(gl_scaled, 1)
            for t in range(NT - 1):
                for h in range(NH):
                    dve.wait_ge(gl_ds, 2 * t + h // 2 + 1)
                    ds_h = mb[2 * (t % 2) + h // 2][:, (h % 2) * DV:(h % 2 + 1) * DV]
                    if t == 0:
                        dve.tensor_copy(s_gla[0][:, h, :], ds_h).then_inc(gl_state, 1)
                    else:
                        dve.wait_ge(gl_state, NH * (t - 1) + h + 1)
                        dve.scalar_tensor_tensor(s_gla[t][:, h, :], s_gla[t - 1][:, h, :], decay[:, h, t:t + 1],
                                                 ds_h, ALU.mult, ALU.add).then_inc(gl_state, 1)
            dve.wait_ge(gl_sd, 1)
            dve.reciprocal(rs_gla[:, :], rs_gla[:, :]).then_inc(gl_rs, 1)
            for k in range(KT):
                o = (go_a if k < 4 else go_b)[:, k % 4, :]
                dve.wait_ge(gl_rsb, k // 2 + 1)
                own.did(dve.scalar_tensor_tensor(o, o, gla_gain[:, k % 2:k % 2 + 1], mb[k // 2][:, :],
                                                 ALU.mult, ALU.mult))
                own.settle()
                dve.tensor_tensor(o, o, gout_fm[:, k, :], ALU.mult).then_inc(yg_done, 1)
            for c in range(2, 8):
                split_lo(g_gates.chunk0 + c, c % 2)
            for h in range(4):
                dve.wait_ge(y_hi, AT_YO + h + 1)
                rest(act_lo[:, h, :], sbq[:, h, :], act_hi[:, h, :]).then_inc(y_lo, 1)
            split_los(g_psb)
            dve.wait_ge(evacuated, all_out(g_gates))
            for u in range(2):
                evac_unit(g_psb.chunk0 + u, lambda j, u=u: gate_tile(gs_fm, 4 * u + j, j))
            for k in range(KT):
                dve.wait_ge(y_hi, AT_YG + k + 1)
                rest(act_lo[:, k, :], (go_a if k < 4 else go_b)[:, k % 4, :], act_hi[:, k, :]).then_inc(y_lo, 1)
            split_lo(g_pgla.chunk0, 0)
            split_lo(g_pgla.chunk0 + 1, 1)
            for u in range(2):
                def mix(j, u=u):
                    gate_tile(gg_fm, 4 * u + j, j)
                    dve.wait_ge(evacuated, g_pgla.tile0 + 4 + 4 * u + j + 1)
                    dve.tensor_tensor(gs_fm[:, 4 * u + j, :], gs_fm[:, 4 * u + j, :], gg_fm[:, 4 * u + j, :],
                                      ALU.add).then_inc(mixed, 1)

                split_lo(g_pgla.chunk0 + 2 + 2 * u, 0)
                evac_unit(g_pgla.chunk0 + 2 * u + 1, mix)
                split_lo(g_pgla.chunk0 + 3 + 2 * u, 1)
            for k in range(KT):
                dve.wait_ge(y_hi, AT_MIX + k + 1)
                rest(act_lo[:, k, :], gs_fm[:, k, :], act_hi[:, k, :]).then_inc(y_lo, 1)
            split_lo(g_out2.chunk0 + 2, 0)
            evac_unit(g_out2.chunk0 + 1, lambda j: add_tile(0, j).then_inc(evacuated, 1))
            split_lo(g_out2.chunk0 + 3, 1)
            evac_unit(g_out2.chunk1 - 1, lambda j: add_tile(1, j).then_inc(evacuated, 1))

            norm(5)

            def hidden_unit(h, u):
                for j in range(4):
                    seen = u * 4 + (4 * up.units * h + j + 1)
                    dve.wait_ge(evacuated, u * 4 + (up.tile0 + 4 + j + 1))
                    dve.tensor_tensor(relu_sq[j][:, :], relu_t[j][:, :], relu_t[j][:, :], ALU.mult)\
                        .then_inc(hid_sq, 1)
                for j in range(4):
                    seen = u * 4 + (4 * up.units * h + j + 1)
                    dve.wait_ge(hid_hi_done, seen)
                    dve.wait_ge(hid_sq, seen)
                    dst = [hidden[:, ds(u * 4 + j, 1), :].rearrange("p o t -> p (o t)") for hidden in (hid_lo, hid_hi)]
                    rest(dst[0], relu_sq[j][:, :], dst[1]).then_inc(hid_lo_done, 1)

            for h, (up, down) in enumerate(g_ff):
                split_lo(up.chunk0, 0)
                split_lo(up.chunk0 + 1, 1)
                with dve.Fori(1, up.units) as u:
                    split_lo(u * 2 + up.chunk0, 0)
                    hidden_unit(h, u - 1)
                    split_lo(u * 2 + up.chunk0 + 1, 1)
                split_lo(down.chunk0, 0)
                hidden_unit(h, up.units - 1)
                split_lo(down.chunk0 + 1, 1)
                for u in range(down.units):
                    for c in range(2 if u == 0 else 1, down.chunks):
                        split_lo(down.chunk0 + u * down.chunks + c, c % 2)
                    if u + 1 < down.units:
                        split_lo(down.chunk0 + (u + 1) * down.chunks, 0)
                    evac_unit(down.chunk0 + (u + 1) * down.chunks - 1,
                              lambda j, u=u: add_tile(u, j).then_inc(evacuated, 1))
            norm(6)

        @block.tensor
        def _(pe):
            def multiply(g, i, fm, a_hi, a_lo, per_body):
                for u in range(per_body):
                    for kc in range(g.chunks):
                        n = u * g.chunks + kc
                        s = n % 2
                        hi, lo = w_hi[s], w_lo[s]
                        pe.wait_ge(w_lo_done, i * (g.chunks * per_body) + (g.chunk0 + n + 1))
                        for j in range(4):
                            if kc == 0:
                                pe.wait_ge(evacuated, i * (4 * per_body) + (g.tile0 + 4 * u + j + 1))
                            cols = slice(j * P, (j + 1) * P)
                            for k in range(g.ktiles):
                                ka = kc * 4 + k
                                if fm:
                                    passes = ((hi[:, k, cols], a_hi[:, ka, :]), (hi[:, k, cols], a_lo[:, ka, :]),
                                              (lo[:, k, cols], a_hi[:, ka, :]))
                                else:
                                    passes = ((a_hi[:, ka, cols], hi[:, k, :]), (a_hi[:, ka, cols], lo[:, k, :]),
                                              (a_lo[:, ka, cols], hi[:, k, :]))
                                for n_pass, (left, right) in enumerate(passes):
                                    ins = pe.matmul(gb[j][:, :], left, right,
                                                    start=(kc == 0 and k == 0 and n_pass == 0),
                                                    stop=(kc == g.chunks - 1 and k == g.ktiles - 1 and n_pass == 2))
                            ins.then_inc(pe_tiles, 1)

            def gemm(g, fm, a_hi=act_hi, a_lo=act_lo):
                if g.other_taker:
                    pe.wait_ge(evacuated, g.tile0 + 4)
                per_body = 2 if g.chunks == 1 else 1
                if g.units == per_body:
                    multiply(g, 0, fm, a_hi, a_lo, per_body)
                    return
                with pe.Fori(0, g.units // per_body) as i:
                    multiply(g, i, fm, a_hi, a_lo, per_body)

            def turn(dst, src):
                return pe.transpose(dst, src, ident[:, :])

            def norm(n):
                for q in range(2 * NT):
                    t, b = q // 2, q % 2
                    if b == 0:
                        pe.wait_ge(n_xn, NT * n + t + 1)
                    if q >= 4:
                        pe.wait_ge(n_lo, turned_before(n) + q - 3)
                    for k in range(4):
                        ins = turn(mb[q % 4][:, k * P:(k + 1) * P], xn[:, t, (4 * b + k) * P:(4 * b + k + 1) * P])
                    ins.then_inc(n_tp, 1)
                pe.wait_ge(n_lo, turned_before(n) + 2 * NT)

            pe.sem_inc(evacuated, 4)
            pe.wait_ge(const_pool, 6)
            norm(0)
            gemm(g_vi, fm=False)
            gemm(g_fquo, fm=True)
            pe.wait_ge(wsp_masked, 1)
            for b in range(2):
                for g in range(4):
                    ins = turn(mb[b][:, g * P:(g + 1) * P], w_sp[:, 4 * b + g, :])
                ins.then_inc(wsp_turned, 1)
            pe.wait_ge(v_normed, NT)
            pe.wait_ge(wspT_done, 2)
            for j in range(NH):
                for t in range(NT):
                    cols = slice(t * P, (t + 1) * P)
                    ins = pe.matmul(mb[j][:, cols], group_sel[:, j * P:(j + 1) * P], b_sp[:, :], start=True, stop=False,
                                    skip_group_check=True)
                    for q in range(2):
                        g = 2 * j + q
                        ins = pe.matmul(mb[j][q * GD:(q + 1) * GD, cols], v_tm[:, t, g * GD:(g + 1) * GD],
                                        w_spT[:, g, :], start=False, stop=True, skip_group_check=True)
                ins.then_inc(spatial_done, 1)
            gemm(g_ga, fm=True)
            pe.wait_ge(hg_ready, 3)
            pe.wait_ge(ya_done, NH)
            for t in range(NT):
                cols = slice(t * P, (t + 1) * P)
                if t >= 2:
                    pe.wait_ge(hg_att_out, 3 * (t - 1))
                for h in range(NH):
                    ins = pe.matmul(mb[2 * (t % 2)][:, h * P:(h + 1) * P], f_fm[:, h, cols], q_fm[:, h, cols],
                                    start=True, stop=True, skip_group_check=True)
                ins.then_inc(hg_att, 1)
                for h in range(NH):
                    ins = pe.matmul(mb[2 * (t % 2) + 1][0:HC, h * P:(h + 1) * P], kend_fm[:, h, t * P:t * P + HC],
                                    q_fm[:, h, cols], start=True, stop=True, skip_group_check=True)
                ins.then_inc(hg_att, 1)
            pe.wait_ge(hg_scaled, 2)
            pe.wait_ge(hg_att_out, 3 * NT)
            for t in range(NT):
                for h in range(NH):
                    ins = turn(mb[t][:, h * P:(h + 1) * P], kend_fm[:, h, t * P:(t + 1) * P])
                ins.then_inc(kend_turned, 1)
            gemm(g_gb, fm=True)
            for t in range(NT - 1):
                pe.wait_ge(kend_done, NT)
                for h in range(NH):
                    cols = slice(h * P, (h + 1) * P)
                    ins = pe.matmul(mb[t][:, cols], kend_tm[:, t, cols], i_tm[:, t, cols], start=True, stop=True,
                                    skip_group_check=True)
                ins.then_inc(hg_ds, 1)
            pe.wait_ge(att_masked, NT)
            pe.wait_ge(hg_state, NH * (NT - 1))
            for h in range(NH):
                for t in range(NT):
                    cols = slice(t * P, (t + 1) * P)
                    ins = pe.matmul(mb[h][:, cols], i_tm[:, t, h * P:(h + 1) * P], attT[:, t, h, :], start=True,
                                    stop=(t == 0), skip_group_check=True)
                    if t:
                        ins = pe.matmul(mb[h][:, cols], s_hg[:, t - 1, h, :], q_fm[:, h, cols], start=False, stop=True,
                                        skip_group_check=True)
                ins.then_inc(hg_o, 1)
            pe.wait_ge(hg_sq, NH)
            for h in range(NH):
                ins = pe.matmul(mb[0][32 * h:32 * h + 32, :], ones[:, 0:32], sq_fm[:, h, :], start=True, stop=True,
                                skip_group_check=True)
            ins.then_inc(hg_ss, 1)
            pe.wait_ge(hg_rs, 1)
            pe.wait_ge(r_pool, 1)
            for h in range(NH):
                pe.matmul(mb[h][:, :], head_sel[:, h, :], rs_hg[:, :], start=True, stop=True).then_inc(hg_rsb, 1)
            pe.wait_ge(y_lo, NH)
            gemm(g_upa, fm=True)
            pe.wait_ge(y_lo, 2 * NH)
            gemm(g_upb, fm=True, a_hi=act_hi[:, 4:8, :], a_lo=act_lo[:, 4:8, :])
            pe.wait_ge(y_lo, AT_MERGED + KT)
            gemm(g_out, fm=False)

            norm(1)
            pe.wait_ge(rw_lo, 1)
            for k in range(KT):
                for n, (left, right) in enumerate(((route_hi, act_hi), (route_hi, act_lo), (route_lo, act_hi))):
                    ins = pe.matmul(mb[0][:, :], left[:, k, :], right[:, k, :], start=(k == 0 and n == 0),
                                    stop=(k == KT - 1 and n == 2))
            ins.then_inc(lgT_done, 1)
            pe.wait_ge(lgT_out, 1)
            for t in range(NT):
                ins = pe.transpose(mb[1][:, t * ROUTED:(t + 1) * ROUTED], logitT[0:ROUTED, t * P:(t + 1) * P],
                                   ident[0:ROUTED, 0:ROUTED])
            ins.then_inc(lg_done, 1)
            pe.wait_ge(picked, 1)
            any_flat = r_any[:, :, :].rearrange("p t e -> p (t e)")
            pe.matmul(mb[2][:, 0:NT * NE], earlier[:, :], any_flat, start=True, stop=True)
            pe.matmul(mb[3][:, 0:NT * NE], ones[:, 0:P], any_flat, start=True, stop=True).then_inc(ranked, 1)
            pe.wait_ge(routed, 1)

            def experts_pe(r):
                with pe.Fori(0, PAIRS // 2) as i:
                    for s in range(2):
                        n = pair_count(i, s, r)
                        half = i if r is None else i + r * (PAIRS // 2)
                        pe.wait_ge(gathered[s], half * 16 + 16)
                        pe.wait_ge(moe_act, 5 * (n + 1) + 2)
                        for b in range(2):
                            for k in range(4):
                                ins = turn(mb[b][:, k * P:(k + 1) * P], xg[s][:, (4 * b + k) * P:(4 * b + k + 1) * P])
                            ins.then_inc(moe_pe, 1)
                        pe.wait_ge(moe_act, 5 * (n + 2) + 2)
                        for w, dst in ((0, mb[2]), (1, mb[3])):
                            if w == 1:
                                pe.wait_ge(moe_dve, 2 * (n + 1) + 1)
                            for kh in range(2):
                                pe.wait_ge(ring_in[2 * w + kh], n * 32 + 32)
                                for k in range(4):
                                    for q in range(2):
                                        mine = slice(q * HALF, (q + 1) * HALF)
                                        ins = pe.matmul(dst[mine, :], xgT[s][:, 4 * kh + k, mine],
                                                        ring[4 * w + 2 * kh + q][:, k, :],
                                                        start=(kh == 0 and k == 0), stop=(kh == 1 and k == 3),
                                                        skip_group_check=True)
                                ins.then_inc(moe_pe, 1)
                        pe.wait_ge(moe_dve, 2 * (n + 2) + 1)
                        for k in range(4):
                            ins = turn(gb[0][:, k * P:(k + 1) * P], gated[s][:, k * P:(k + 1) * P])
                        ins.then_inc(moe_pe, 1)
                        pe.wait_ge(moe_dve, 2 * (n + 2) + 2)
                        pe.wait_ge(moe_act, 5 * (n + 1) + 5)
                        for nh in range(2):
                            pe.wait_ge(ring_in[4 + nh], n * 32 + 32)
                            for k in range(4):
                                for q in range(2):
                                    mine = slice(q * HALF, (q + 1) * HALF)
                                    ins = pe.matmul(gb[1 + nh][mine, :], gatedT[s][:, k, mine],
                                                    ring[8 + 2 * nh + q][:, k, :], start=(k == 0), stop=(k == 3),
                                                    skip_group_check=True)
                            ins.then_inc(moe_pe, 1)

            pe.sem_inc(moe_pe, 18)
            experts_pe(None)
            main_round_done(pe)
            fullest = pe.value_load(most[0:1, 0:1], min_val=0, max_val=T)
            with pe.Fori(1, ROUNDS) as r:
                with pe.If(fullest > r * SLOTS):
                    experts_pe(r)

            norm(2)
            pe.wait_ge(p_in, 16)
            for b in range(2):
                for t in range(NT):
                    ins = turn(mb[b][:, t * P:(t + 1) * P], p_tm[:, t, b * P:(b + 1) * P])
                ins.then_inc(p_turned, 1)
            gemm(g_pg, fm=False)
            pe.wait_ge(p_lo, 2)
            gemm(g_ple, fm=False, a_hi=pT_hi, a_lo=pT_lo)

            norm(4)
            gemm(g_qk, fm=True)
            gemm(g_vv, fm=False)
            pe.wait_ge(evacuated, all_out(g_vv))
            pe.sem_inc(sb_o, 8)
            pe.sem_inc(sb_sig, 2)
            pe.sem_inc(sb_wT_done, 1)
            pe.sem_inc(sb_o_out, 1)
            with pe.Fori(0, SBH // 2) as h:
                def scores(n):
                    s, t = n % 2, n % 4
                    rows = slice((n // 4) * SBD, (n // 4 + 1) * SBD)
                    if n == 0:
                        pe.wait_ge(sb_staged, h * 3 + 3)
                    pe.wait_ge(sb_sig, h * 16 + (2 * n if n >= 2 else 2))
                    pe.matmul(gb[s][:, 0:(t + 1) * P], sb_q[rows, t * P:(t + 1) * P], sb_k[rows, 0:(t + 1) * P],
                              start=True, stop=True).then_inc(sb_z, 1)

                scores(0)
                for n in range(8):
                    s, t = n % 2, n % 4
                    if n < 7:
                        scores(n + 1)
                    pe.wait_ge(sb_weight, h * 16 + 2 * n + 2)
                    pe.wait_ge(sb_wT_done, h * 8 + (n if n else 1))
                    for b in range(t + 1):
                        ins = turn(mb[s][:, b * P:(b + 1) * P], sb_w[s][:, b * P:(b + 1) * P])
                    ins.then_inc(sb_turned, 1)
                    pe.wait_ge(sb_wT_done, h * 8 + n + 2)
                    if n == 0:
                        pe.wait_ge(sb_o_out, h + 1)
                    rows = slice((n // 4) * SBD, (n // 4 + 1) * SBD)
                    for b in range(t + 1):
                        ins = pe.matmul(mb[2][rows, t * P:(t + 1) * P], sb_v[:, b, rows], sb_wT[s][:, b, :],
                                        start=(b == 0), stop=(b == t), skip_group_check=True)
                    ins.then_inc(sb_o, 1)
            pe.wait_ge(low_split, 2)
            for k in range(KT):
                for n, (left, right) in enumerate(((low_hi, act_hi), (low_hi, act_lo), (low_lo, act_hi))):
                    ins = pe.matmul(mb[0][:, :], left[:, k, :], right[:, k, :], start=(k == 0 and n == 0),
                                    stop=(k == KT - 1 and n == 2))
            ins.then_inc(low_z, 1)
            pe.wait_ge(lowT_done, 1)
            for h in range(NH):
                pe.matmul(mb[h][:, :], gate_up[:, h * P:(h + 1) * P], lowT[:, :], start=True, stop=True)\
                    .then_inc(la_z, 1)
            gemm(g_gla, fm=True)
            for n in range(LEVELS + 1):
                if n < LEVELS:
                    pe.wait_ge(gl_prod, 2 * n + 2)
                for t in range(NT):
                    cols = slice(t * P, (t + 1) * P)
                    if n:
                        pe.wait_ge(gl_copied, NT * (n - 1) + t + 1)
                    else:
                        pe.wait_ge(la_dve, NH)
                    for h in range(NH):
                        left, right = (gl_qk, gl_qk) if n < LEVELS else (gk_fm, gq_fm)
                        ins = pe.matmul(mb[t][:, h * P:(h + 1) * P], left[:, h, cols], right[:, h, cols],
                                        start=True, stop=True, skip_group_check=True)
                    ins.then_inc(gl_mm, 1)
            pe.wait_ge(gl_scaled, 2)
            pe.wait_ge(gl_copied, NT * (LEVELS + 1))
            for t in range(NT):
                for h in range(NH):
                    ins = turn(mb[t][:, h * P:(h + 1) * P], gk_fm[:, h, t * P:(t + 1) * P])
                ins.then_inc(gkend_turned, 1)
            pe.wait_ge(gkend_done, NT)
            for t in range(NT - 1):
                if t == 2:
                    pe.wait_ge(gl_state, NH)
                for h in range(NH):
                    ins = pe.matmul(mb[2 * (t % 2) + h // 2][:, (h % 2) * DV:(h % 2 + 1) * DV],
                                    gkend_tm[:, t, h * P:(h + 1) * P], gv_tm[:, t, h * DV:(h + 1) * DV],
                                    start=True, stop=True, skip_group_check=True)
                    if h % 2:
                        ins.then_inc(gl_ds, 1)
            pe.wait_ge(gl_state, NH * (NT - 1))
            for n in range(KT):
                h = n // 2
                if n >= 2:
                    pe.wait_ge(gl_sq, n - 1)
                for t in range(NT):
                    cols = slice(t * P, (t + 1) * P)
                    vals = slice((n % 2) * P, (n % 2 + 1) * P)
                    ins = pe.matmul(mb[n % 2][:, cols], gv_tm[:, t, n * P:(n + 1) * P], g_att[:, t, h, :], start=True,
                                    stop=(t == 0), skip_group_check=True)
                    if t:
                        ins = pe.matmul(mb[n % 2][:, cols], s_gla[t - 1][:, h, vals], gq_fm[:, h, cols], start=False,
                                        stop=True, skip_group_check=True)
                ins.then_inc(gl_o, 1)
                if n % 2:
                    pe.wait_ge(gl_sq, n + 1)
                    for v in range(2):
                        ins = pe.matmul(mb[2][32 * h:32 * h + 32, :], ones[:, 0:32], gsq[h % 2][:, v, :],
                                        start=(v == 0), stop=(v == 1), skip_group_check=True)
                    ins.then_inc(gl_ss, 1)
            pe.wait_ge(gl_rs, 1)
            pe.wait_ge(r_pool, 3)
            for h in range(NH):
                pe.matmul(mb[h][:, :], gsel[:, h, :], rs_gla[:, :], start=True, stop=True).then_inc(gl_rsb, 1)
            gemm(g_gates, fm=True)
            pe.wait_ge(y_lo, AT_YO + 4)
            gemm(g_psb, fm=True)
            pe.wait_ge(y_lo, AT_YG + KT)
            gemm(g_pgla, fm=True)
            pe.wait_ge(y_lo, AT_MIX + KT)
            gemm(g_out2, fm=False)

            norm(5)
            for h, (up, down) in enumerate(g_ff):
                gemm(up, fm=True)
                pe.wait_ge(hid_lo_done, (h + 1) * 4 * up.units)
                gemm(down, fm=False, a_hi=hid_hi, a_lo=hid_lo)


_INS = ["x", "p", "g_mix", "w_in", "gm_ln_g", "gm_ln_b", "gm_w_sp", "gm_b_sp", "w_up_a", "hg_lb_param",
        "hg_norm_g", "w_up_b", "w_out", "g_ffn", "w_grp", "w_exp", "w1", "w3", "w2", "g_ple", "w_pg",
        "w_ple", "g_final", "norm_mix_2", "w_in_2", "w_gate_up_2", "b_gate_up_2", "gla_norm_2",
        "w_proj_sb_2", "w_proj_gla_2", "w_out_2", "norm_mlp_2", "w_ff1_2", "w_ff2_2", "norm_final_2"]


def kernel(**inputs):
    import numpy as np
    import concourse.bacc as bacc
    from concourse.bass_utils import run_bass_kernel_spmd

    nc = bacc.Bacc("TRN2", target_bir_lowering=False, num_devices=1)
    arrays, aps = {}, {}
    for name in _INS:
        a = np.ascontiguousarray(inputs[name])
        arrays[f"in_{name}"] = a
        aps[name] = nc.dram_tensor(f"in_{name}", a.shape, mybir.dt.from_np(a.dtype), kind="ExternalInput").ap()
    out = nc.dram_tensor("out", inputs["x"].shape, F32, kind="ExternalOutput").ap()
    two_blocks(nc, aps, out)
    r = run_bass_kernel_spmd(nc, [arrays], core_ids=[0])
    return r.results[0]["out"]
```

```python
from contextlib import ExitStack

import concourse.bass as bass
from concourse import mybir

ALU = mybir.AluOpType
ACT = mybir.ActivationFunctionType
F32 = mybir.dt.float32
F32R = mybir.dt.float32r
I32 = mybir.dt.int32
U32 = mybir.dt.uint32
AX = mybir.AxisListType
ds = bass.ds

P = 128
EPS = 1e-6
HUGE = 3.0e38


class Gemm:

    def __init__(self, after, units, chunks, taker, ktiles=4):
        self.taker, self.other_taker = taker, bool(after) and after.taker != taker
        self.units, self.chunks, self.ktiles = units, chunks, ktiles
        self.chunk0 = after.chunk1 if after else 0
        self.tile0 = after.tile1 if after else 0
        self.chunk1 = self.chunk0 + units * chunks
        self.tile1 = self.tile0 + 4 * units


class Chain:

    def __init__(self, eng, sem):
        self.eng, self.sem, self.n = eng, sem, 0
        self.turn, self.per = None, 0

    def did(self, ins):
        ins.then_inc(self.sem, 1)
        self.n += 1

    def settle(self):
        self.eng.wait_ge(self.sem, self.n if self.turn is None else self.turn * self.per + self.n)

    def enter(self, turn, per):
        self.turn, self.per, self.start = turn, per, self.n

    def leave(self, turns):
        assert self.n - self.start == self.per, (self.n - self.start, self.per)
        self.n += (turns - 1) * self.per
        self.turn = None


def two_blocks(nc, A, out):
    T, D = A["x"].shape[1:]
    NT, KT = T // P, D // P
    GW = A["gm_ln_g"].shape[1]
    GG = A["gm_w_sp"].shape[1]
    GD = GW // GG
    HW = A["hg_norm_g"].shape[1]
    NH = HW // P
    HC = 64
    NE = A["w1"].shape[1]
    EG = 8
    NG = NE // EG
    FE = A["w1"].shape[3]
    PD = A["p"].shape[3]
    SBH, SBD = 8, 64
    GR = A["w_gate_up_2"].shape[1]
    DV = A["gla_norm_2"].shape[1]
    FF = A["w_ff1_2"].shape[2]
    SLOTS = 64
    ROUNDS = T // SLOTS
    PAIRS = NE // 2
    ROUTED = NG + NE
    LEVELS = 7
    assert (T, D, GW, HW, FE, DV) == (512, 1024, 512, 512, 512, 256)

    g_vi = Gemm(None, 2, 2, "act")
    g_fquo = Gemm(g_vi, 4, 2, "act")
    g_ga = Gemm(g_fquo, 2, 2, "act")
    g_gb = Gemm(g_ga, 2, 2, "act")
    g_upa = Gemm(g_gb, 2, 1, "dve")
    g_upb = Gemm(g_upa, 2, 1, "dve")
    g_out = Gemm(g_upb, 2, 2, "dve")
    g_pg = Gemm(g_out, 2, 2, "act")
    g_ple = Gemm(g_pg, 2, 1, "dve", ktiles=PD // P)
    g_qk = Gemm(g_ple, 2, 2, "act")
    g_sv = Gemm(g_qk, 1, 2, "act")
    g_gv = Gemm(g_sv, 2, 2, "act")
    g_gla = Gemm(g_gv, 4, 2, "act")
    g_gates = Gemm(g_gla, 4, 2, "act")
    g_psb = Gemm(g_gates, 2, 1, "dve")
    g_pgla = Gemm(g_psb, 2, 2, "dve")
    g_out2 = Gemm(g_pgla, 2, 2, "dve")
    HALVES = 2
    FH = FF // HALVES
    g_ff = []
    last = g_out2
    for _ in range(HALVES):
        up = Gemm(last, FH // 512, 2, "act")
        last = Gemm(up, 2, FH // 512, "dve")
        g_ff.append((up, last))

    h2_dram = nc.dram_tensor("moe_rows", [T, D], F32).ap()
    slot_dram = nc.dram_tensor("moe_slot_choice", [ROUNDS * P * PAIRS, 1], I32).ap()
    y_dram = nc.dram_tensor("moe_choice_out", [2 * T, D], F32).ap()

    gates_dram = nc.dram_tensor("branch_gates", [2 * KT, P, T], F32).ap()

    ctx = ExitStack()
    with ctx:
        PAGE = 2048
        base = (nc.sbuf_base + 63) // 64 * 64
        ctx.enter_context(nc.sbuf_tensor("fence", [P, 103 * 512], F32))

        def at(name, page, shape, dt=F32):
            return nc.alloc_sbuf_tensor_at(name, shape, dt, offset=base + int(page * PAGE))

        def sem(name):
            return ctx.enter_context(nc.semaphore(name))

        x = at("x_tm", 0, [P, NT, D])
        small_at = [8 * PAGE]

        def small(name, shape, dt=F32):
            n = 4
            for s in shape[1:]:
                n *= s
            t = nc.alloc_sbuf_tensor_at(name, shape, dt, offset=base + small_at[0])
            small_at[0] += (n + 31) // 32 * 32
            assert small_at[0] <= 13 * PAGE, small_at
            return t

        ident = small("ident", [P, P])
        ones = small("ones", [P, T])
        earlier = small("earlier", [P, P])
        level_mask = small("level_mask", [P, LEVELS, P], I32)
        eps_col = small("eps_col", [P, 1])
        one_col = small("one_col", [P, 1])
        lb_par = small("lb_par", [P, 2, NH])
        lb = small("lb", [P, NH])
        lb_not = small("lb_not", [P, NH])
        lb_neg = small("lb_neg", [P, NH])
        hg_gain = small("hg_gain", [P, NH])
        gate_bias = small("gate_bias", [P, NH])
        gla_gain = small("gla_gain", [P, DV // P])
        ssq = small("ssq", [P, NT])
        rstd = small("rstd", [P, NT])
        ln_stats = small("ln_stats", [P, NT, 6])
        ln_mv = small("ln_mv", [P, NT, 2])
        ln_rstd = small("ln_rstd", [P, NT])
        decay = small("decay", [P, NH, T // HC])
        b_sp = small("b_sp", [GG, P])
        gate1 = small("gate1", [P, NT])
        gate2 = small("gate2", [P, NT])
        most = small("most", [P, 1], I32)
        slot_choice = small("slot_choice", [P, PAIRS], I32)
        slot_token = small("slot_token", [P, PAIRS], I32)
        choice_now = [small(f"choice_now{s}", [P, 1], I32) for s in range(2)]
        token_now = [small(f"token_now{s}", [P, 1], I32) for s in range(2)]

        act_hi = at("act_hi", 13, [P, KT, T], F32R)
        act_lo = at("act_lo", 21, [P, KT, T], F32R)
        w_stage = [at(f"w_stage{s}", 29 + 4 * s, [P, 4, 512]) for s in range(2)]
        w_hi = [at(f"w_hi{s}", 37 + 4 * s, [P, 4, 512], F32R) for s in range(2)]
        w_lo = [at(f"w_lo{s}", 45 + 4 * s, [P, 4, 512], F32R) for s in range(2)]
        F = 53
        xn_at = {0: F + 8, 1: 45, 2: F + 36, 6: F + 40}
        xn_at = {n: at(f"xn_{n}", page, [P, NT, D]) for n, page in xn_at.items()}
        xn_at.update({n: xn_at[2] for n in (3, 4, 5)})
        gain = at("gain", F + 48, [P, D])
        gain_4 = at("gain_4", F + 44, [P, D])
        u_fm = at("u_fm", F + 0, [P, NH, T])
        v_tm = at("v_tm", F + 4, [P, NT, GW])
        q_fm = at("q_fm", F + 8, [P, NH, T])
        f_fm = at("f_fm", F + 12, [P, NH, T])
        i_tm = at("i_tm", F + 16, [P, NT, HW])
        og_fm = at("og_fm", F + 20, [P, NH, T])
        ga_fm = at("ga_fm", F + 24, [P, KT, T])
        gb_fm = at("gb_fm", F + 32, [P, KT, T])
        b_fm = at("b_fm", F + 40, [P, NH, T])
        kend_fm = at("kend_fm", F + 44, [P, NH, T])
        w_sp = at("w_sp", F + 40, [P, GG, P])
        w_spT = at("w_spT", F + 42, [P, GG, P])
        ln_g = at("ln_g", F + 44, [P, GW])
        ln_b = at("ln_b", F + 45, [P, GW])
        group_sel = at("group_sel", F + 32, [GG, GW])
        eb_fm = at("eb_fm", F + 32, [P, NH, T])
        order_xor = at("order_xor", F + 47, [P, P], I32)
        attT = at("attT", F + 4, [P, NT, NH, P])
        kend_tm = at("kend_tm", F + 40, [P, NT, HW])
        s_hg = at("s_hg", F + 12, [P, NT - 1, NH, P])
        o_fm = at("o_fm", F + 44, [P, NH, T])
        sq_fm = at("sq_fm", F + 8, [P, NH, T])
        rs_hg = at("rs_hg", F + 40, [P, T])
        head_sel = at("head_sel", F + 41, [P, NH, P])
        ring = [at(f"ring{j}", F + 4 * j, [P, 4, 512]) for j in range(12)]
        xg = [at(f"xg{s}", 13 + 2 * s, [P, D]) for s in range(2)]
        xgT = [at(f"xgT{s}", 17 + 2 * s, [P, KT, P]) for s in range(2)]
        silu_h = [at(f"silu_h{s}", 21 + s, [P, FE]) for s in range(2)]
        gated = [at(f"gated{s}", 23 + s, [P, FE]) for s in range(2)]
        gatedT = [at(f"gatedT{s}", 25 + s, [P, FE // P, P]) for s in range(2)]
        y_sb = [at(f"y_sb{s}", 45 + 2 * s, [P, D]) for s in range(2)]
        route_f = at("route_f", 33, [P, KT, P])
        route_hi = at("route_hi", 41, [P, KT, P], F32R)
        route_lo = at("route_lo", 43, [P, KT, P], F32R)
        logitT = at("logitT", 27, [P, T])
        routes_at = [37 * PAGE]

        def routes(name, shape, dt=F32):
            n = 4
            for s in shape[1:]:
                n *= s
            t = nc.alloc_sbuf_tensor_at(name, shape, dt, offset=base + routes_at[0])
            routes_at[0] += (n + 31) // 32 * 32
            assert routes_at[0] <= 41 * PAGE, routes_at
            return t

        logits = routes("logits", [P, NT, ROUTED])
        r_iota = routes("r_iota", [P, NT, NE])
        r_slot0 = routes("r_slot0", [P, NE])
        r_max = routes("r_max", [P, NT])
        r_grp = routes("r_grp", [P, NT, NG])
        r_exp = routes("r_exp", [P, NT, NG])
        r_pg = routes("r_pg", [P, NT])
        r_first = routes("r_first", [P, NT])
        r_bias = routes("r_bias", [P, NT, NG])
        r_sel = routes("r_sel", [P, NT, NE])
        r_pick = [routes(f"r_pick{n}", [P, NT, NE]) for n in range(2)]
        r_tmp = routes("r_tmp", [P, NT, NE])
        r_any = routes("r_any", [P, NT, NE])
        r_rank = routes("r_rank", [P, NT, NE])
        r_top = [routes(f"r_top{n}", [P, NT]) for n in range(2)]
        r_d = routes("r_d", [P, NT])
        r_pos = routes("r_pos", [P, 2, NT])
        r_s0 = routes("r_s0", [P, 2, NT])
        r_posi = routes("r_posi", [P, 2, NT], I32)
        r_hi = routes("r_hi", [P, 2, NT], I32)
        r_lo = routes("r_lo", [P, 2, NT], I32)
        r_slot = routes("r_slot", [P, 2, NT], I32)
        r_choice = routes("r_choice", [P, 2, NT], I32)
        r_none = routes("r_none", [P, P], I32)
        r_tot = routes("r_tot", [P, NE])
        y_in = [at(f"y_in{n}", F + 2 * n, [P, D]) for n in range(2 * NT)]
        sg_tm = at("sg_tm", F + 16, [P, NT, D])
        p_tm = at("p_tm", F + 24, [P, NT, PD])
        pT_hi = at("pT_hi", F + 26, [P, PD // P, T], F32R)
        pT_lo = at("pT_lo", F + 28, [P, PD // P, T], F32R)
        ple_t = [at(f"ple_t{s}", F + 30 + s, [P, 512]) for s in range(2)]
        sbq = at("sbq", F + 0, [P, 4, T])
        sbk = at("sbk", F + 4, [P, 4, T])
        sbv = at("sbv", F + 8, [P, NT, 512])
        gv_tm = at("gv_tm", F + 12, [P, NT, D])
        g_all = at("g_all", F + 20, [P, 4 * NH, T])
        gq_fm = g_all[:, 0:NH, :]
        gk_fm = g_all[:, NH:2 * NH, :]
        gout_fm = g_all[:, 2 * NH:4 * NH, :]
        sb_q = at("sb_q", F + 36, [P, T])
        sb_v = at("sb_v", F + 37, [P, NT, P])
        sb_fail = [at(f"sb_fail{s}", F + 38 + s, [P, T]) for s in range(2)]
        sb_w = [at(f"sb_w{s}", F + 40 + s, [P, T]) for s in range(2)]
        sb_later = [at(f"sb_later{s}", F + 42 + s, [P, T]) for s in range(2)]
        sb_wT = at("sb_wT", F + 44, [P, NT, P])
        sb_k = at("sb_k", F + 45, [P, T])
        low_f = at("low_f", F + 20, [P, KT, P])
        low_hi = at("low_hi", F + 22, [P, KT, P], F32R)
        low_lo = at("low_lo", F + 24, [P, KT, P], F32R)
        lowT = at("lowT", F + 26, [GR, T])
        gate_up = at("gate_up", F + 27, [GR, HW])
        la_fm = at("la_fm", F + 28, [P, NH, T])
        la_tmp = at("la_tmp", F + 32, [P, NH, T])
        la_sum = at("la_sum", F + 46, [P, NH, T])
        gl_e = at("gl_e", F + 36, [P, NH, T])
        gl_qk = at("gl_qk", F + 40, [P, NH, T])
        gate_out = [at(f"gate_out{s}", F + 44 + s, [P, T]) for s in range(2)]
        g_att = at("g_att", F + 4, [P, NT, NH, P])
        gkend_tm = at("gkend_tm", F + 40, [P, NT, HW])
        s_gla = [at(f"s_gla{n}", F + 8 + 2 * n, [P, NH, DV]) for n in range(2)]
        s_gla.append(at("s_gla2", F + 36, [P, NH, DV]))
        go_all = at("go", F + 20, [P, KT, T])
        go = [go_all[:, (n + KT // 2) % KT, :] for n in range(KT)]
        gsq = [at(f"gsq{s}", F + 40 + 2 * s, [P, 2, T]) for s in range(2)]
        rs_gla = at("rs_gla", F + 38, [P, T])
        gsel = at("gsel", F + 39, [P, NH, P])
        gs_fm = at("gs_fm", F + 12, [P, KT, T])
        gg_fm = at("gg_fm", F + 4, [P, KT, T])
        mix_hi = at("mix_hi", F + 20, [P, KT, T], F32R)
        mix_lo = at("mix_lo", F + 28, [P, KT, T], F32R)
        hid_hi = at("hid_hi", F + 0, [P, FH // P, T], F32R)
        hid_lo = at("hid_lo", F + 16, [P, FH // P, T], F32R)
        relu_t = [at(f"relu_t{s}", F + 32 + s, [P, T]) for s in range(4)]
        relu_sq = [at(f"relu_sq{s}", F + 36 + s, [P, T]) for s in range(4)]

        bank = [ctx.enter_context(nc.psum_tensor(f"bank{b}", [P, 512], F32)) for b in range(8)]
        gb, mb = bank[:4], bank[4:]

        x_in = [sem(f"x_in{t}") for t in range(NT)]
        w_loaded = [sem(f"w_loaded{s}") for s in range(2)]
        w_hi_done, w_lo_done = sem("w_hi_done"), sem("w_lo_done")
        pe_tiles = sem("pe_tiles")
        evacuated = sem("evacuated")
        n_sd = sem("n_sd")
        n_xn, n_tp, n_hi, n_lo = sem("n_xn"), sem("n_tp"), sem("n_hi"), sem("n_lo")
        gain_in, gain_4_in = sem("gain_in"), sem("gain_4_in")
        const_pool, const_dve, params_in = sem("const_pool"), sem("const_dve"), sem("params_in")
        dve_own, act_own, pool_own = sem("dve_own"), sem("act_own"), sem("pool_own")
        lb_diff, lb_sig = sem("lb_diff"), sem("lb_sig")
        wsp_masked, wsp_turned, wspT_done = sem("wsp_masked"), sem("wsp_turned"), sem("wspT_done")
        ln_var, ln_sd, v_normed = sem("ln_var"), sem("ln_sd"), sem("v_normed")
        spatial_done, ya_done = sem("spatial_done"), sem("ya_done")
        hg_log, hg_k, hg_cum, hg_exp = sem("hg_log"), sem("hg_k"), sem("hg_cum"), sem("hg_exp")
        hg_ready, hg_att, hg_att_out = sem("hg_ready"), sem("hg_att"), sem("hg_att_out")
        att_zero, att_masked = sem("att_zero"), sem("att_masked")
        hg_scaled, kend_turned, kend_done = sem("hg_scaled"), sem("kend_turned"), sem("kend_done")
        hg_ds, hg_state = sem("hg_ds"), sem("hg_state")
        hg_o, hg_o_out, hg_sq = sem("hg_o"), sem("hg_o_out"), sem("hg_sq")
        hg_ss, hg_sd, hg_rs, hg_rsb, yb_done = (sem("hg_ss"), sem("hg_sd"), sem("hg_rs"),
                                                sem("hg_rsb"), sem("yb_done"))
        y_hi, y_lo = sem("y_hi"), sem("y_lo")
        AT_MERGED = 2 * NH
        AT_YO = AT_MERGED + KT
        AT_YG = AT_YO + NH
        AT_MIX = AT_YG + KT
        merged = sem("merged")
        route_in, route_pad, rw_hi, rw_lo = (sem("route_in"), sem("route_pad"), sem("rw_hi"),
                                             sem("rw_lo"))
        lgT_done, lgT_out, lg_done = sem("lgT_done"), sem("lgT_out"), sem("lg_done")
        r_expd = sem("r_expd")
        r_shift, r_pool = sem("r_shift"), sem("r_pool")
        picked, ranked, routed = sem("picked"), sem("ranked"), sem("routed")
        h2_stored, slots_cleared, slots_sent = sem("h2_stored"), sem("slots_cleared"), sem("slots_sent")

        moe_pe, moe_act, moe_dve = sem("moe_pe"), sem("moe_act"), sem("moe_dve")
        slots_in, tokens_done = sem("slots_in"), sem("tokens_done")
        token_copied, choice_copied, y_free = sem("token_copied"), sem("choice_copied"), sem("y_free")
        gathered = [sem(f"gathered{s}") for s in range(2)]
        ring_in = [sem(f"ring_in{j}") for j in range(6)]
        y_stored = [sem(f"y_stored{s}") for s in range(2)]
        round_done, pool_turn = sem("round_done"), sem("pool_turn")
        y_back, x_moe = [sem(f"y_back{t}") for t in range(NT)], sem("x_moe")
        p_in, p_turned, p_hi, p_lo = sem("p_in"), sem("p_turned"), sem("p_hi"), sem("p_lo")
        x_ple = sem("x_ple")
        sb_qk_in, sb_v_in = sem("sb_qk_in"), sem("sb_v_in")
        sb_z, sb_sig, sb_past = sem("sb_z"), sem("sb_sig"), sem("sb_past")
        sb_weight, sb_turned, sb_wT_done = sem("sb_weight"), sem("sb_turned"), sem("sb_wT_done")
        sb_o, sb_o_out, sb_ones = sem("sb_o"), sem("sb_o_out"), sem("sb_ones")
        low_in, low_pad, low_split, low_z = sem("low_in"), sem("low_pad"), sem("low_split"), sem("low_z")
        lowT_done, la_z, la_act, la_cum = sem("lowT_done"), sem("la_z"), sem("la_act"), sem("la_cum")
        gla_q, gout_done, gates_in, moe_done = sem("gla_q"), sem("gout_done"), sem("gates_in"), sem("moe_done")
        gates_stored = [sem(f"gates_stored{s}") for s in range(2)]
        gl_dist, gl_exp, gl_prod, gl_mm, gl_copied = (sem("gl_dist"), sem("gl_exp"), sem("gl_prod"),
                                                      sem("gl_mm"), sem("gl_copied"))
        g_att_zero, gl_edge, gl_edge_exp, gl_scaled = (sem("g_att_zero"), sem("gl_edge"),
                                                       sem("gl_edge_exp"), sem("gl_scaled"))
        gkend_turned, gkend_done = sem("gkend_turned"), sem("gkend_done")
        gl_ds, gl_state, gl_o, gl_o_out, gl_sq = (sem("gl_ds"), sem("gl_state"), sem("gl_o"),
                                                  sem("gl_o_out"), sem("gl_sq"))
        gl_ss, gl_sd, gl_rs, gl_rsb, yg_done = (sem("gl_ss"), sem("gl_sd"), sem("gl_rs"),
                                                sem("gl_rsb"), sem("yg_done"))
        mixed = sem("mixed")
        hid_hi_done, hid_sq, hid_lo_done = sem("hid_hi_done"), sem("hid_sq"), sem("hid_lo_done")
        out_stored = sem("out_stored")

        block = ctx.enter_context(nc.Block())
        HALF = SLOTS

        ROWS_ONLY = (3, 6)

        def turned_before(n):
            return 2 * NT * (n - sum(m < n for m in ROWS_ONLY))

        def all_out(g):
            return g.tile1 + 4

        def pair_count(turn, s, round_turn):
            pair = turn * 2 + s
            return pair if round_turn is None else pair + round_turn * PAIRS

        def main_round_done(eng):
            for s in range(2):
                eng.wait_ge(y_stored[s], 16 * PAIRS // 2)

        @block.sync
        def _(sp):
            def load_chunk(c, s, w, cols, kc, ktiles=4):
                if isinstance(c, int):
                    if c >= 2:
                        sp.wait_ge(w_lo_done, c - 1)
                else:
                    sp.wait_ge(w_lo_done, c - 1)
                src = w[kc * 512:kc * 512 + ktiles * P, cols].rearrange("(k p) n -> p k n", p=P)
                sp.dma_start(w_stage[s][:, 0:ktiles, :], src).then_inc(w_loaded[s], 16)

            def load_unit(g, u, w, col):
                for kc in range(g.chunks):
                    c = g.chunk0 + u * g.chunks + kc
                    load_chunk(c, c % 2, w, slice(col, col + 512), kc, g.ktiles)

            def load_units(g, w, col, k0=0):
                if g.units * g.chunks == 2:
                    for u in range(g.units):
                        load_unit(g, u, w, col + 512 * u)
                    return
                with sp.Fori(0, g.units) as u:
                    for kc in range(g.chunks):
                        load_chunk(g.chunk0 + g.chunks * u + kc, kc % 2, w,
                                   ds(u * 512 + col, 512), k0 + kc, g.ktiles)

            def load_gain(n, g):
                if n == 4:
                    sp.dma_start(gain_4[:, :], g.rearrange("(o d) -> o d", o=1).broadcast_to([P, D]))\
                        .then_inc(gain_4_in, 16)
                    return
                if n == 5:
                    sp.wait_ge(y_lo, AT_YG + KT)
                elif n:
                    sp.wait_ge(n_xn, NT * n)
                sp.dma_start(gain[:, :], g.rearrange("(o d) -> o d", o=1).broadcast_to([P, D]))\
                    .then_inc(gain_in, 16)

            x_dram = A["x"][0].rearrange("(t p) d -> t p d", p=P)
            for t in range(NT):
                sp.dma_start(x[:, t, :], x_dram[t]).then_inc(x_in[t], 16)
            load_gain(0, A["g_mix"][0])
            w_in = A["w_in"][0]
            load_unit(g_vi, 0, w_in, 1 * 512)
            load_unit(g_vi, 1, w_in, 4 * 512)
            for u, col in enumerate((3, 2, 0, 5)):
                load_unit(g_fquo, u, w_in, col * 512)
            load_units(g_ga, w_in, 6 * 512)
            load_units(g_gb, w_in, 8 * 512)
            load_units(g_upa, A["w_up_a"][0], 0)
            load_units(g_upb, A["w_up_b"][0], 0)
            load_units(g_out, A["w_out"][0], 0)
            load_gain(1, A["g_ffn"][0])

            sp.wait_ge(w_lo_done, g_out.chunk1)
            sp.wait_ge(route_pad, 1)
            sp.dma_start(route_f[:, :, 0:NG], A["w_grp"][0].rearrange("(k p) n -> p k n", p=P))\
                .then_inc(route_in, 16)
            sp.dma_start(route_f[:, :, NG:ROUTED], A["w_exp"][0].rearrange("(k p) n -> p k n", p=P))\
                .then_inc(route_in, 16)

            PIECE_USED = [3, 3, 4, 4, 5, 5, 6, 6, 8, 8, 9, 9]

            def load_piece(j, e0, free):
                q = j % 2
                if free is not None:
                    sp.wait_ge(moe_pe, free)
                e = e0 + q
                h = (j // 2) % 2
                if j < 8:
                    w = A["w1"] if j < 4 else A["w3"]
                    src = w[0, ds(e, 1), h * 512:(h + 1) * 512, :].rearrange("e (k p) n -> p (e k) n", p=P)
                else:
                    src = A["w2"][0, ds(e, 1), :, h * 512:(h + 1) * 512]\
                        .rearrange("e (k p) n -> p (e k) n", p=P)
                sp.dma_start(ring[j][:, :, :], src).then_inc(ring_in[j // 2], 16)

            sp.wait_ge(y_lo, AT_MERGED + KT)
            for j in range(12):
                load_piece(j, 0, None)
            for t in range(NT):
                sp.wait_ge(n_xn, NT + t + 1)
                sp.dma_start(h2_dram[t * P:(t + 1) * P, :], xn_at[1][:, t, :]).then_inc(h2_stored, 16)
            load_gain(2, A["g_ple"][0])

            sp.wait_ge(rw_lo, 1)
            load_unit(g_pg, 0, A["w_pg"][0], 0)

            with sp.Fori(0, PAIRS - 1) as i:
                for j in range(12):
                    load_piece(j, i * 2 + 2, i * 9 + (18 + PIECE_USED[j]))
            main_round_done(sp)
            sp.wait_ge(routed, 1)
            fullest = sp.value_load(most[0:1, 0:1], min_val=0, max_val=T)
            with sp.Fori(1, ROUNDS) as r:
                with sp.If(fullest > r * SLOTS):
                    with sp.Fori(0, PAIRS) as i:
                        for j in range(12):
                            load_piece(j, i * 2, i * 9 + r * (9 * PAIRS) + (9 + PIECE_USED[j]))
                    for s in range(2):
                        sp.wait_ge(y_stored[s], r * (16 * PAIRS // 2) + 16 * PAIRS // 2)
                    sp.sem_inc(round_done, 1)
            sp.sem_inc(moe_done, 1)
            sp.dma_start(p_tm[:, :, :], A["p"][0, 0].rearrange("(t p) d -> p t d", p=P)).then_inc(p_in, 16)
            for t in range(NT):
                for c in range(2):
                    sp.dma_start(y_in[2 * t + c][:, :], y_dram[c * T + t * P:c * T + (t + 1) * P, :])\
                        .then_inc(y_back[t], 16)
            load_unit(g_pg, 1, A["w_pg"][0], 512)
            load_gain(3, A["g_final"])
            load_gain(4, A["norm_mix_2"][0])
            load_units(g_ple, A["w_ple"][0], 0)
            w_in2 = A["w_in_2"][0]
            load_unit(g_qk, 0, w_in2, 0)
            sp.wait_ge(low_pad, 1)
            sp.dma_start(low_f[:, :, 0:GR], w_in2[:, 9 * 512:9 * 512 + GR]
                         .rearrange("(k p) n -> p k n", p=P)).then_inc(low_in, 16)
            sp.dma_start(gate_up[:, :], A["w_gate_up_2"][0]).then_inc(low_in, 16)
            load_unit(g_qk, 1, w_in2, 512)
            load_unit(g_sv, 0, w_in2, 2 * 512)
            load_units(g_gv, w_in2, 5 * 512)
            for u, col in enumerate((3, 4, 7, 8)):
                load_unit(g_gla, u, w_in2, col * 512)
            load_units(g_gates, w_in2, 9 * 512 + GR)
            load_units(g_psb, A["w_proj_sb_2"][0], 0)
            for s in range(2):
                sp.wait_ge(gates_stored[s], 16 * KT)
            sp.wait_ge(gl_o, KT)
            for gates, half in ((gs_fm, gates_dram[0:KT]), (gg_fm, gates_dram[KT:2 * KT])):
                sp.dma_start(gates[:, :, :], half.rearrange("k p t -> p k t")).then_inc(gates_in, 16)
            load_units(g_pgla, A["w_proj_gla_2"][0], 0)
            load_units(g_out2, A["w_out_2"][0], 0)
            load_gain(5, A["norm_mlp_2"][0])
            for h, (up, down) in enumerate(g_ff):
                load_units(up, A["w_ff1_2"][0], h * FH)
                load_units(down, A["w_ff2_2"][0], 0, k0=h * FH // 512)
            load_gain(6, A["norm_final_2"])
            out_dram = out[0].rearrange("(t p) d -> t p d", p=P)
            for t in range(NT):
                sp.wait_ge(n_xn, 6 * NT + t + 1)
                sp.dma_start(out_dram[t], xn_at[6][:, t, :]).then_inc(out_stored, 16)
            sp.wait_ge(out_stored, 16 * NT)

        @block.gpsimd
        def _(pool):
            own = Chain(pool, pool_own)

            own.did(pool.memset(ident[:, :], 0.0))
            own.did(pool.memset(earlier[:, :], 1.0))
            own.did(pool.memset(group_sel[:, :], 1.0))
            own.did(pool.iota(level_mask[:, 0, :], pattern=[[0, P]], base=0, channel_multiplier=1))
            own.did(pool.iota(level_mask[:, 1, :], pattern=[[1, P]], base=0, channel_multiplier=0))
            own.settle()
            pool.affine_select(out=ident[:, :], in_=ident[:, :], compare_op=ALU.not_equal, fill=1.0,
                               base=0, pattern=[[-1, P]], channel_multiplier=1).then_inc(const_pool, 1)
            pool.affine_select(out=earlier[:, :], in_=earlier[:, :], compare_op=ALU.is_gt, fill=0.0,
                               base=0, pattern=[[1, P]], channel_multiplier=-1).then_inc(const_pool, 1)
            pool.memset(ones[:, :], 1.0).then_inc(const_pool, 1)
            pool.memset(eps_col[:, :], EPS).then_inc(const_pool, 1)
            pool.memset(one_col[:, :], 1.0).then_inc(const_pool, 1)
            own.did(pool.affine_select(out=group_sel[:, :], in_=group_sel[:, :], compare_op=ALU.is_ge,
                                       fill=0.0, base=0, pattern=[[1, GW]], channel_multiplier=-GD))
            own.settle()
            pool.affine_select(out=group_sel[:, :], in_=group_sel[:, :], compare_op=ALU.is_ge, fill=0.0,
                               base=GD - 1, pattern=[[-1, GW]], channel_multiplier=GD)\
                .then_inc(const_pool, 1)
            pool.dma_start(lb_par[:, :, :], A["hg_lb_param"].rearrange("l (h p) -> p l h", p=P),
                           allow_slow_non_contiguous=True).then_inc(params_in, 16)
            pool.dma_start(hg_gain[:, :], A["hg_norm_g"][0].rearrange("(h p) -> p h", p=P),
                           allow_slow_non_contiguous=True).then_inc(params_in, 16)
            pool.dma_start(gate_bias[:, :], A["b_gate_up_2"][0].rearrange("(h p) -> p h", p=P),
                           allow_slow_non_contiguous=True).then_inc(params_in, 16)
            pool.dma_start(gla_gain[:, :], A["gla_norm_2"][0].rearrange("(h p) -> p h", p=P),
                           allow_slow_non_contiguous=True).then_inc(params_in, 16)
            pool.dma_start(w_sp[:, :, :], A["gm_w_sp"][0].rearrange("g t s -> t g s")).then_inc(params_in, 16)
            pool.dma_start(b_sp[:, :], A["gm_b_sp"][0]).then_inc(params_in, 16)
            for t, name in ((ln_g, "gm_ln_g"), (ln_b, "gm_ln_b")):
                pool.dma_start(t[:, :], A[name].broadcast_to([P, GW])).then_inc(params_in, 16)

            pool.wait_ge(const_dve, 1)
            pool.affine_select(out=level_mask[:, 2, :], in_=level_mask[:, 2, :], compare_op=ALU.is_gt,
                               fill=0.0, base=0, pattern=[[1, P]], channel_multiplier=-1)\
                .then_inc(const_pool, 1)
            pool.wait_ge(params_in, 16 * 8)
            pool.affine_select(out=w_sp[:, :, :], in_=w_sp[:, :, :], compare_op=ALU.is_ge, fill=0.0,
                               base=0, pattern=[[0, GG], [-1, P]], channel_multiplier=1)\
                .then_inc(wsp_masked, 1)

            pool.wait_ge(ya_done, NH)
            pool.memset(attT[:, :, :, :], 0.0).then_inc(att_zero, 1)
            for t in range(NT):
                pool.wait_ge(hg_att_out, 3 * (t + 1))
                pool.affine_select(out=attT[:, t, :, :], in_=attT[:, t, :, :], compare_op=ALU.is_ge,
                                   fill=0.0, base=0, pattern=[[0, NH], [1, P]], channel_multiplier=-1)\
                    .then_inc(att_masked, 1)
            pool.wait_ge(hg_state, NH * (NT - 1))
            own.did(pool.memset(head_sel[:, :, :], 0.0))
            own.settle()
            own.did(pool.affine_select(out=head_sel[:, :, :], in_=head_sel[:, :, :],
                                       compare_op=ALU.not_equal, fill=1.0, base=0,
                                       pattern=[[-32, NH], [0, P]], channel_multiplier=1))
            own.settle()
            pool.sem_inc(r_pool, 1)

            pool.wait_ge(w_lo_done, g_out.chunk1)
            pool.memset(route_f[:, :, :], 0.0).then_inc(route_pad, 1)
            pool.wait_ge(pe_tiles, 4 * g_out.chunk1)
            opts = dict(allow_small_or_imprecise_dtypes=True)
            own.did(pool.iota(r_iota[:, :, :], pattern=[[0, NT], [1, NE]], base=0, channel_multiplier=0, **opts))
            own.did(pool.iota(r_slot0[:, :], pattern=[[1, PAIRS], [SLOTS * PAIRS, 2]], base=0,
                              channel_multiplier=0, **opts))
            own.did(pool.iota(r_choice[:, :, :], pattern=[[T, 2], [P, NT]], base=0, channel_multiplier=1))
            own.did(pool.iota(r_none[:, :], pattern=[[0, P]], base=2 * T, channel_multiplier=0))
            own.settle()
            pool.sem_inc(r_pool, 1)
            pool.dma_start(slot_dram.rearrange("(a b) o -> a (b o)", a=P), r_none[:, :])\
                .then_inc(slots_cleared, 16)
            pool.wait_ge(slots_cleared, 16)

            pool.wait_ge(routed, 1)
            for c in range(2):
                for t in range(NT):
                    pool.indirect_dma_start(slot_dram, bass.IndirectOffsetOnAxis(r_slot[:, c, t:t + 1], 0),
                                            r_choice[:, c, t:t + 1], None).then_inc(slots_sent, 16)
            pool.wait_ge(slots_sent, 16 * 2 * NT)
            pool.wait_ge(h2_stored, 16 * NT)

            def at_col(c):
                return slice(c, c + 1) if isinstance(c, int) else ds(c, 1)

            def gather_round(r):
                first = 0 if r is None else r * (P * PAIRS)
                table = slot_dram[ds(first, P * PAIRS), :] if r is not None else slot_dram[0:P * PAIRS, :]
                pool.dma_start(slot_choice[:, :], table.rearrange("(p a) o -> p (a o)", p=P))\
                    .then_inc(slots_in, 16)
                pool.wait_ge(tokens_done, 1 if r is None else r + 1)
                pool.sem_inc(pool_turn, 1)

                def half_count(i):
                    return i if r is None else i + r * (PAIRS // 2)

                def gather(i, s):
                    n = pair_count(i, s, r)
                    if not (r is None and isinstance(i, int) and i == 0):
                        pool.wait_ge(gathered[s], half_count(i) * 16)
                        pool.sem_inc(pool_turn, 1)
                    pool.tensor_copy(token_now[s][:, :], slot_token[:, at_col(i * 2 + s)]).then_inc(token_copied, 1)
                    pool.wait_ge(token_copied, n + 1)
                    pool.wait_ge(moe_pe, n * 9 + 2)
                    pool.sem_inc(pool_turn, 1)
                    pool.indirect_dma_start(xg[s][:, :], None, h2_dram,
                                            bass.IndirectOffsetOnAxis(token_now[s][:, :], 0))\
                        .then_inc(gathered[s], 16)

                def scatter(i, s):
                    n = pair_count(i, s, r)
                    if not (r is None and isinstance(i, int) and i == 0):
                        pool.wait_ge(y_stored[s], half_count(i) * 16)
                    pool.sem_inc(y_free, 1)
                    pool.tensor_copy(choice_now[s][:, :], slot_choice[:, at_col(i * 2 + s)])\
                        .then_inc(choice_copied, 1)
                    pool.wait_ge(choice_copied, n + 1)
                    pool.wait_ge(moe_act, n * 5 + 15)
                    pool.sem_inc(pool_turn, 1)
                    pool.indirect_dma_start(y_dram, bass.IndirectOffsetOnAxis(choice_now[s][:, :], 0),
                                            y_sb[s][:, :], None, bounds_check=2 * T - 1, oob_is_err=False)\
                        .then_inc(y_stored[s], 16)

                for s in range(2):
                    gather(0, s)
                first_turn = 0
                if r is None:
                    first_turn = 1
                    for s in range(2):
                        scatter(0, s)
                        gather(1, s)
                with pool.Fori(first_turn, PAIRS // 2 - 1) as i:
                    for s in range(2):
                        scatter(i, s)
                        gather(i + 1, s)
                for s in range(2):
                    scatter(PAIRS // 2 - 1, s)
                for s in range(2):
                    pool.wait_ge(y_stored[s], half_count(PAIRS // 2) * 16)
                pool.sem_inc(round_done, 1)

            gather_round(None)
            main_round_done(pool)
            fullest = pool.value_load(most[0:1, 0:1], min_val=0, max_val=T)
            with pool.Fori(1, ROUNDS) as r:
                with pool.If(fullest > r * SLOTS):
                    gather_round(r)
            pool.wait_ge(x_ple, 2 * NT)
            pool.memset(low_f[:, :, :], 0.0).then_inc(low_pad, 1)

            def copy_qk(h):
                for staged, whole in ((sb_q, sbq), (sb_k, sbk)):
                    pool.tensor_copy(staged[:, :], whole[:, ds(h, 1), :].rearrange("p o t -> p (o t)"))\
                        .then_inc(sb_qk_in, 1)

            def sb_turn(h, last):
                for n in range(2 * NT):
                    s, t = n % 2, n % 4
                    a, b = t * P, (t + 1) * P
                    pool.wait_ge(sb_sig, h * 16 + 2 * n + 4)
                    pool.sem_inc(pool_turn, 1)
                    pool.affine_select(out=sb_fail[s][:, a:b], in_=sb_fail[s][:, a:b], compare_op=ALU.is_gt,
                                       fill=1.0, base=0, pattern=[[-1, P]], channel_multiplier=1)\
                        .then_inc(sb_past, 1)
                    pool.affine_select(out=sb_w[s][:, a:b], in_=sb_w[s][:, a:b], compare_op=ALU.is_gt,
                                       fill=0.0, base=0, pattern=[[-1, P]], channel_multiplier=1)\
                        .then_inc(sb_past, 1)
                    if n == 0:
                        pool.wait_ge(sb_o, h * 8 + 8)
                        pool.tensor_copy(sb_v[:, :, :], sbv[:, :, ds(h * P, P)]).then_inc(sb_v_in, 1)
                    if n == 2 * NT - 1 and not last:
                        copy_qk(h + 1)

            pool.wait_ge(evacuated, all_out(g_sv))
            for s in range(2):
                pool.memset(sb_later[s][:, :], 1.0).then_inc(sb_ones, 1)
            copy_qk(0)
            with pool.Fori(0, SBH // 2 - 1) as h:
                sb_turn(h, False)
            sb_turn(SBH // 2 - 1, True)
            pool.wait_ge(sb_z, 8 * (SBH // 2))
            pool.memset(g_att[:, :, :, :], 0.0).then_inc(g_att_zero, 1)
            with pool.Fori(0, KT) as i:
                for s in range(2):
                    pool.wait_ge(evacuated, i * 2 + (g_gates.tile0 + 4 + s + 1))
                    pool.sem_inc(pool_turn, 1)
                    pool.dma_start(gates_dram[ds(i * 2 + s, 1)].rearrange("o p t -> p (o t)"), gate_out[s][:, :])\
                        .then_inc(gates_stored[s], 16)
            pool.wait_ge(gl_state, NH * (NT - 1))
            own.did(pool.memset(gsel[:, :, :], 0.0))
            own.settle()
            own.did(pool.affine_select(out=gsel[:, :, :], in_=gsel[:, :, :],
                                       compare_op=ALU.not_equal, fill=1.0, base=0,
                                       pattern=[[-32, NH], [0, P]], channel_multiplier=1))
            own.settle()
            pool.sem_inc(r_pool, 1)

        @block.scalar
        def _(act):
            own = Chain(act, act_own)

            def split_hi(c, s, ktiles=4):
                act.wait_ge(w_loaded[s], (c // 2 + 1) * 16 if isinstance(c, int) else c * 8 + (16 - 8 * s))
                if not isinstance(c, int) or c >= 2:
                    act.wait_ge(pe_tiles, (c - 1) * 4)
                act.activation(w_hi[s][:, 0:ktiles, :], w_stage[s][:, 0:ktiles, :], ACT.Copy)\
                    .then_inc(w_hi_done, 1)

            def evac_unit(last_chunk, put):
                for j in range(4):
                    act.wait_ge(pe_tiles, last_chunk * 4 + j + 1)
                    put(j).then_inc(evacuated, 1)

            def evac_f(dst, func, scale=1.0):
                return lambda j: act.activation(dst[:, j, :], gb[j][:, :], func, scale=scale)

            def at_tile(dst, u, j):
                return dst[:, ds(u * 4 + j, 1), :].rearrange("p o t -> p (o t)")

            def norm(n, ready):
                def root(t):
                    ready(t)
                    own.did(act.activation(xn_at[n][:, t, :], x[:, t, :], ACT.Square, accum_out=ssq[:, t:t + 1]))
                    own.settle()
                    act.activation(rstd[:, t:t + 1], ssq[:, t:t + 1], ACT.Sqrt, bias=eps_col[:, 0:1],
                                   scale=1.0 / D).then_inc(n_sd, 1)

                def high(t):
                    if n in ROWS_ONLY:
                        return
                    for b in range(2):
                        q = 2 * t + b
                        act.wait_ge(n_tp, turned_before(n) + q + 1)
                        act.activation(act_hi[:, 4 * b:4 * b + 4, t * P:(t + 1) * P],
                                       mb[q % 4][:, :].rearrange("p (k t) -> p k t", k=4), ACT.Copy)\
                            .then_inc(n_hi, 1)

                root(0)
                for t in range(1, NT):
                    root(t)
                    high(t - 1)
                high(NT - 1)

            def rows_added(g, t):
                act.wait_ge(evacuated, all_out(g) - NT + t + 1)
                if g is g_out and t >= NT // 2:
                    act.wait_ge(pe_tiles, 4 * g.chunk1)

            act.wait_ge(const_pool, 5)
            norm(0, lambda t: act.wait_ge(x_in[t], 16))

            c = g_vi.chunk0
            split_hi(c, 0)
            split_hi(c + 1, 1)
            act.wait_ge(lb_diff, 1)
            act.activation(lb[:, :], lb_neg[:, :], ACT.Sigmoid).then_inc(lb_sig, 1)
            split_hi(c + 2, 0)
            evac_unit(c + 1, evac_f(v_tm, ACT.Gelu_apprx_tanh))
            split_hi(c + 3, 1)
            act.wait_ge(ln_var, 1)
            act.activation(ln_rstd[:, :], ln_mv[:, :, 1], ACT.Sqrt, bias=eps_col[:, 0:1]).then_inc(ln_sd, 1)
            for u, (dst, func) in enumerate(((f_fm, ACT.Sigmoid), (q_fm, ACT.Silu),
                                             (u_fm, ACT.Gelu_apprx_tanh), (og_fm, ACT.Sigmoid))):
                split_hi(g_fquo.chunk0 + 2 * u, 0)
                if u == 0:
                    evac_unit(g_vi.chunk1 - 1, evac_f(i_tm, ACT.Copy))
                else:
                    evac_unit(g_fquo.chunk0 + 2 * u - 1, evac_f(*prev))
                split_hi(g_fquo.chunk0 + 2 * u + 1, 1)
                prev = (dst, func)
            for b in range(2):
                act.wait_ge(wsp_turned, b + 1)
                act.activation(w_spT[:, 4 * b:4 * b + 4, :],
                               mb[b][:, :].rearrange("p (g t) -> p g t", g=4), ACT.Copy).then_inc(wspT_done, 1)
            split_hi(g_ga.chunk0, 0)
            evac_unit(g_fquo.chunk1 - 1, evac_f(og_fm, ACT.Sigmoid))
            split_hi(g_ga.chunk0 + 1, 1)
            act.wait_ge(ya_done, NH)
            act.wait_ge(const_dve, 2)
            for h in range(NH):
                act.activation(b_fm[:, h, :], f_fm[:, h, :], ACT.Ln, bias=lb[:, h:h + 1],
                               scale=lb_not[:, h:h + 1]).then_inc(hg_log, 1)
            split_hi(g_ga.chunk0 + 2, 0)
            evac_unit(g_ga.chunk0 + 1, evac_f(ga_fm, ACT.Sigmoid))
            split_hi(g_ga.chunk0 + 3, 1)
            act.wait_ge(hg_cum, NH * (T // HC))
            act.activation(eb_fm[:, :, :], kend_fm[:, :, :], ACT.Exp).then_inc(hg_exp, 1)
            act.activation(b_fm[:, :, :], kend_fm[:, :, :], ACT.Exp, scale=-1.0).then_inc(hg_exp, 1)
            for t in range(NT):
                act.wait_ge(att_zero, 1)
                act.wait_ge(hg_att, 2 * t + 1)
                diag = mb[2 * (t % 2)][:, :].rearrange("p (h t) -> p h t", h=NH)
                act.activation(attT[0:HC, t, :, 0:HC], diag[0:HC, :, 0:HC], ACT.Copy).then_inc(hg_att_out, 1)
                act.activation(attT[HC:P, t, :, HC:P], diag[HC:P, :, HC:P], ACT.Copy).then_inc(hg_att_out, 1)
                act.wait_ge(hg_att, 2 * t + 2)
                low = mb[2 * (t % 2) + 1][:, :].rearrange("p (h t) -> p h t", h=NH)
                act.activation(attT[0:HC, t, :, HC:P], low[0:HC, :, HC:P], ACT.Copy).then_inc(hg_att_out, 1)
            for t in range(NT):
                act.wait_ge(kend_turned, t + 1)
                act.activation(kend_tm[:, t, :], mb[t][:, :], ACT.Copy).then_inc(kend_done, 1)
            for u in range(2):
                split_hi(g_gb.chunk0 + 2 * u, 0)
                if u == 0:
                    evac_unit(g_ga.chunk1 - 1, lambda j: act.activation(ga_fm[:, 4 + j, :], gb[j][:, :], ACT.Sigmoid))
                else:
                    evac_unit(g_gb.chunk0 + 1, evac_f(gb_fm, ACT.Sigmoid))
                split_hi(g_gb.chunk0 + 2 * u + 1, 1)
            for h in range(NH):
                act.wait_ge(hg_o, h + 1)
                act.activation(o_fm[:, h, :], mb[h][:, :], ACT.Copy).then_inc(hg_o_out, 1)
                act.activation(sq_fm[:, h, :], mb[h][:, :], ACT.Square).then_inc(hg_sq, 1)
            evac_unit(g_gb.chunk1 - 1, lambda j: act.activation(gb_fm[:, 4 + j, :], gb[j][:, :], ACT.Sigmoid))
            act.wait_ge(ya_done, NH)
            for h in range(NH):
                act.activation(act_hi[:, h, :], u_fm[:, h, :], ACT.Copy).then_inc(y_hi, 1)
            act.wait_ge(hg_ss, 1)
            act.activation(rs_hg[:, :], mb[0][:, :], ACT.Sqrt, bias=eps_col[:, 0:1], scale=1.0 / P)\
                .then_inc(hg_sd, 1)
            split_hi(g_upa.chunk0, 0)
            split_hi(g_upa.chunk0 + 1, 1)
            split_hi(g_upb.chunk0, 0)
            for h in range(NH):
                act.wait_ge(yb_done, h + 1)
                act.activation(act_hi[:, 4 + h, :], o_fm[:, h, :], ACT.Copy).then_inc(y_hi, 1)
            split_hi(g_upb.chunk0 + 1, 1)
            for u in range(2):
                split_hi(g_out.chunk0 + u, u)
                act.wait_ge(pe_tiles, 4 * (g_upa if u == 0 else g_upb).chunk1)
                for k in range(4 * u, 4 * u + 4):
                    act.wait_ge(merged, k + 1)
                    act.activation(act_hi[:, k, :], ga_fm[:, k, :], ACT.Copy).then_inc(y_hi, 1)
            split_hi(g_out.chunk0 + 2, 0)
            split_hi(g_out.chunk0 + 3, 1)

            norm(1, lambda t: rows_added(g_out, t))
            act.wait_ge(route_in, 32)
            act.activation(route_hi[:, :, :], route_f[:, :, :], ACT.Copy).then_inc(rw_hi, 1)
            act.wait_ge(lgT_done, 1)
            act.activation(logitT[:, :], mb[0][:, :], ACT.Copy).then_inc(lgT_out, 1)
            act.wait_ge(r_shift, 1)
            act.activation(r_exp[:, :, :], r_grp[:, :, :], ACT.Exp).then_inc(r_expd, 1)
            act.wait_ge(r_shift, 2)
            act.activation(r_d[:, :], r_top[1][:, :], ACT.Exp).then_inc(r_expd, 1)

            def experts_act(r):
                with act.Fori(0, PAIRS // 2) as i:
                    for s in range(2):
                        n = pair_count(i, s, r)
                        for b in range(2):
                            act.wait_ge(moe_pe, 9 * (n + 2) + b + 1)
                            act.activation(xgT[s][:, 4 * b:4 * b + 4, :],
                                           mb[b][:, :].rearrange("p (k t) -> p k t", k=4), ACT.Copy)\
                                .then_inc(moe_act, 1)
                        act.wait_ge(moe_pe, 9 * (n + 2) + 4)
                        act.activation(silu_h[s][:, :], mb[2][:, :], ACT.Silu).then_inc(moe_act, 1)
                        act.wait_ge(y_free, n + 1)
                        for b in range(2):
                            act.wait_ge(moe_pe, 9 * (n + 2) + 8 + b)
                            act.activation(y_sb[s][:, b * 512:(b + 1) * 512], gb[1 + b][:, :], ACT.Copy)\
                                .then_inc(moe_act, 1)

            act.sem_inc(moe_act, 10)
            experts_act(None)
            main_round_done(act)
            fullest = act.value_load(most[0:1, 0:1], min_val=0, max_val=T)
            with act.Fori(1, ROUNDS) as r:
                with act.If(fullest > r * SLOTS):
                    experts_act(r)

            split_hi(g_pg.chunk0, 0)
            split_hi(g_pg.chunk0 + 1, 1)
            for b in range(2):
                act.wait_ge(p_turned, b + 1)
                act.activation(pT_hi[:, b, :], mb[b][:, :], ACT.Copy).then_inc(p_hi, 1)
            norm(2, lambda t: act.wait_ge(x_moe, t + 1))
            split_hi(g_pg.chunk0 + 2, 0)
            evac_unit(g_pg.chunk0 + 1, lambda j: act.activation(sg_tm[:, j, 0:512], gb[j][:, :], ACT.Sigmoid))
            split_hi(g_pg.chunk0 + 3, 1)
            split_hi(g_ple.chunk0, 0, g_ple.ktiles)
            evac_unit(g_pg.chunk1 - 1, lambda j: act.activation(sg_tm[:, j, 512:D], gb[j][:, :], ACT.Sigmoid))
            split_hi(g_ple.chunk0 + 1, 1, g_ple.ktiles)

            norm(3, lambda t: (rows_added(g_ple, t), act.wait_ge(x_ple, NT + t + 1)))
            split_hi(g_qk.chunk0, 0)
            norm(4, lambda t: act.wait_ge(n_xn, 3 * NT + t + 1))
            split_hi(g_qk.chunk0 + 1, 1)
            act.wait_ge(low_in, 32)
            act.activation(low_hi[:, :, :], low_f[:, :, :], ACT.Copy).then_inc(low_split, 1)

            def unit(c, put, next_two=True):
                split_hi(c + 2, 0)
                evac_unit(c + 1, put)
                if next_two:
                    split_hi(c + 3, 1)

            unit(g_qk.chunk0, evac_f(sbq, ACT.Copy))
            unit(g_qk.chunk0 + 2, evac_f(sbk, ACT.Copy))
            act.wait_ge(low_z, 1)
            act.activation(lowT[:, :], mb[0][0:GR, :], ACT.Copy).then_inc(lowT_done, 1)
            unit(g_sv.chunk0, evac_f(sbv, ACT.Copy))
            for h in range(NH):
                act.wait_ge(la_z, h + 1)
                act.activation(la_tmp[:, h, :], mb[h][:, :], ACT.Abs, bias=gate_bias[:, h:h + 1]).then_inc(la_act, 1)
            act.wait_ge(la_act, NH)
            own.did(act.activation(la_tmp[:, :, :], la_tmp[:, :, :], ACT.Exp, scale=-1.0))
            own.settle()
            act.activation(la_tmp[:, :, :], la_tmp[:, :, :], ACT.Ln, bias=one_col[:, 0:1]).then_inc(la_act, 1)
            unit(g_gv.chunk0, lambda j: act.activation(gv_tm[:, j, 0:512], gb[j][:, :], ACT.Copy))
            unit(g_gv.chunk0 + 2, lambda j: act.activation(gv_tm[:, j, 512:D], gb[j][:, :], ACT.Copy), False)

            def gla_out(h, j):
                act.wait_ge(pe_tiles, h * 8 + (4 * (g_gla.chunk0 + 1) + j + 1))
                act.activation(at_tile(g_all, h, j), gb[j][:, :], ACT.Copy).then_inc(evacuated, 1)

            def turn_end(h):
                for j in (2, 3):
                    gla_out(h, j)
                act.wait_ge(sb_o, h * 8 + 16)
                act.activation(sbq[:, ds(h, 1), :].rearrange("p o t -> p (o t)"), mb[3][:, :], ACT.Copy)\
                    .then_inc(sb_o_out, 1)

            def sb_turn(h, first):
                for n in range(2 * NT):
                    s, t = n % 2, n % 4
                    end = (t + 1) * P
                    act.wait_ge(sb_z, h * 8 + n + 1)
                    if n >= 2 or not first:
                        act.wait_ge(sb_turned, h * 8 + n - 1)
                    act.activation(sb_fail[s][:, 0:end], mb[s][:, 0:end], ACT.Sigmoid, scale=-SBD ** -0.5)\
                        .then_inc(sb_sig, 1)
                    act.activation(sb_w[s][:, 0:end], mb[s][:, 0:end], ACT.Sigmoid, scale=SBD ** -0.5)\
                        .then_inc(sb_sig, 1)
                    if n == 0 and not first:
                        turn_end(h - 1)
                    if n == 1:
                        split_hi(h * 2 + (g_gla.chunk0 + 1), 1)
                    if n == 5:
                        split_hi(h * 2 + (g_gla.chunk0 + 2), 0)
                    if n >= 6:
                        gla_out(h, n - 6)

            act.wait_ge(la_cum, NH * NT)
            sb_turn(0, True)
            with act.Fori(1, SBH // 2) as h:
                sb_turn(h, False)
            turn_end(SBH // 2 - 1)

            act.wait_ge(evacuated, all_out(g_gla))
            act.activation(gq_fm[:, :, :], gq_fm[:, :, :], ACT.Copy, scale=float(P) ** -0.5).then_inc(gla_q, 1)

            def gate_unit(u):
                for j in range(4):
                    n = 4 * u + j
                    act.wait_ge(pe_tiles, 4 * (g_gates.chunk0 + 2 * u + 1) + j + 1)
                    if n >= 2:
                        act.wait_ge(gates_stored[n % 2], 16 * (n // 2))
                    act.activation(gate_out[n % 2][:, :], gb[j][:, :], ACT.Sigmoid).then_inc(evacuated, 1)

            for n in range(LEVELS):
                act.wait_ge(gl_dist, 2 * n + 2)
                act.activation(gl_e[:, :, :], gl_e[:, :, :], ACT.Exp, scale=1.0 / 16).then_inc(gl_exp, 1)
                if n and n % 2 == 0:
                    gate_unit(n // 2 - 1)
                split_hi(g_gates.chunk0 + n + 1, (n + 1) % 2)
            act.wait_ge(gl_edge, 1)
            act.activation(gl_e[:, :, :], la_sum[:, :, :], ACT.Exp, scale=1.0 / 16).then_inc(gl_edge_exp, 1)
            act.activation(gl_qk[:, :, :], gl_qk[:, :, :], ACT.Exp, scale=1.0 / 16).then_inc(gl_edge_exp, 1)
            act.activation(decay[:, :, 0:NT], la_sum[:, :, P - 1:T:P], ACT.Exp, scale=1.0 / 16)\
                .then_inc(gl_edge_exp, 1)
            split_hi(g_psb.chunk0, 0)
            gate_unit(3)
            split_hi(g_psb.chunk0 + 1, 1)
            for t in range(NT):
                act.wait_ge(gkend_turned, t + 1)
                act.activation(gkend_tm[:, t, :], mb[t][:, :], ACT.Copy).then_inc(gkend_done, 1)
            for h in range(NH):
                act.activation(act_hi[:, h, :], sbq[:, h, :], ACT.Copy).then_inc(y_hi, 1)
            act.activation(gout_fm[:, :, :], gout_fm[:, :, :], ACT.Silu).then_inc(gout_done, 1)
            for n in range(KT):
                h = n // 2
                act.wait_ge(gl_o, n + 1)
                act.activation(go[n], mb[n % 2][:, :], ACT.Copy).then_inc(gl_o_out, 1)
                if n >= 4:
                    act.wait_ge(gl_ss, h - 1)
                act.activation(gsq[h % 2][:, n % 2, :], mb[n % 2][:, :], ACT.Square).then_inc(gl_sq, 1)
            act.wait_ge(gl_ss, NH)
            act.activation(rs_gla[:, :], mb[2][:, :], ACT.Sqrt, bias=eps_col[:, 0:1], scale=1.0 / DV)\
                .then_inc(gl_sd, 1)
            split_hi(g_pgla.chunk0, 0)
            for u in range(2):
                if u:
                    split_hi(g_pgla.chunk0 + 1, 1)
                    act.wait_ge(pe_tiles, 4 * g_psb.chunk1)
                for k in range(4 * u, 4 * u + 4):
                    act.wait_ge(yg_done, k + 1)
                    act.activation(act_hi[:, (k + 4) % KT, :], go[k], ACT.Copy).then_inc(y_hi, 1)
            split_hi(g_pgla.chunk0 + 2, 0)
            split_hi(g_pgla.chunk0 + 3, 1)
            for u in range(2):
                for k in range(4 * u, 4 * u + 4):
                    act.wait_ge(mixed, k + 1)
                    act.activation(mix_hi[:, k, :], gs_fm[:, k, :], ACT.Copy).then_inc(y_hi, 1)
                if u == 0:
                    split_hi(g_out2.chunk0, 0)
                    split_hi(g_out2.chunk0 + 1, 1)
            split_hi(g_out2.chunk0 + 2, 0)
            split_hi(g_out2.chunk0 + 3, 1)

            split_hi(g_ff[0][0].chunk0, 0)
            norm(5, lambda t: rows_added(g_out2, t))

            def relu_unit(h, u, chunk):
                for j in range(4):
                    act.wait_ge(pe_tiles, chunk * 4 + j + 1)
                    seen = u * 4 + (j + 1) + (4 * up.units * h - 4)
                    if not (h == 0 and isinstance(u, int) and u == 0):
                        act.wait_ge(hid_sq, seen)
                    act.activation(relu_t[j][:, :], gb[j][:, :], ACT.Relu).then_inc(evacuated, 1)
                for j in range(4):
                    act.wait_ge(evacuated, (u * 4) + up.tile0 + 4 + j + 1)
                    if h:
                        act.wait_ge(pe_tiles, 4 * g_ff[h - 1][1].chunk1)
                    act.activation(at_tile(hid_hi, u, j), relu_t[j][:, :], ACT.Square).then_inc(hid_hi_done, 1)

            for h, (up, down) in enumerate(g_ff):
                if h:
                    split_hi(up.chunk0, 0)
                split_hi(up.chunk0 + 1, 1)
                split_hi(up.chunk0 + 2, 0)
                relu_unit(h, 0, up.chunk0 + 1)
                split_hi(up.chunk0 + 3, 1)
                with act.Fori(2, up.units) as u:
                    split_hi(u * 2 + up.chunk0, 0)
                    relu_unit(h, u - 1, u * 2 + (up.chunk0 - 1))
                    split_hi(u * 2 + up.chunk0 + 1, 1)
                split_hi(down.chunk0, 0)
                relu_unit(h, up.units - 1, up.chunk1 - 1)
                split_hi(down.chunk0 + 1, 1)
                with act.Fori(1, down.units * down.chunks // 2) as i:
                    for s in range(2):
                        split_hi(i * 2 + down.chunk0 + s, s)
            norm(6, lambda t: rows_added(g_ff[-1][1], t))

        @block.vector
        def _(dve):
            own = Chain(dve, dve_own)

            def split_lo(c, s, ktiles=4):
                dve.wait_ge(w_hi_done, c + 1)
                dve.tensor_tensor(w_lo[s][:, 0:ktiles, :], w_stage[s][:, 0:ktiles, :],
                                  w_hi[s][:, 0:ktiles, :].bitcast(F32), ALU.subtract).then_inc(w_lo_done, 1)

            def split_los(g):
                n = g.units * g.chunks // 2
                if n == 1:
                    for s in range(2):
                        split_lo(g.chunk0 + s, s, g.ktiles)
                    return
                with dve.Fori(0, n) as i:
                    for s in range(2):
                        split_lo(i * 2 + g.chunk0 + s, s, g.ktiles)

            def rest(dst, src, hi):
                return dve.tensor_tensor(dst, src, hi.bitcast(F32), ALU.subtract)

            def norm(n, before=lambda t: None):
                dve.wait_ge(gain_4_in if n == 4 else gain_in, 16 * (1 if n == 4 else n + 1 if n < 4 else n))

                def scale(t):
                    before(t)
                    dve.wait_ge(n_sd, NT * n + t + 1)
                    own.did(dve.reciprocal(rstd[:, t:t + 1], rstd[:, t:t + 1]))
                    own.settle()
                    dst = x if n == 3 else xn_at[n]
                    gains = gain_4 if n == 4 else gain
                    dve.scalar_tensor_tensor(dst[:, t, :], x[:, t, :], rstd[:, t:t + 1], gains[:, :],
                                             ALU.mult, ALU.mult).then_inc(n_xn, 1)

                def low(t):
                    if n in ROWS_ONLY:
                        return
                    for b in range(2):
                        q = 2 * t + b
                        dve.wait_ge(n_hi, turned_before(n) + q + 1)
                        rest(act_lo[:, 4 * b:4 * b + 4, t * P:(t + 1) * P],
                             mb[q % 4][:, :].rearrange("p (k t) -> p k t", k=4),
                             act_hi[:, 4 * b:4 * b + 4, t * P:(t + 1) * P]).then_inc(n_lo, 1)

                scale(0)
                for t in range(1, NT):
                    scale(t)
                    low(t - 1)
                low(NT - 1)

            def evac_unit(last_chunk, put):
                for j in range(4):
                    dve.wait_ge(pe_tiles, last_chunk * 4 + j + 1)
                    put(j)

            dve.wait_ge(const_pool, 5)
            dve.wait_ge(pool_own, 5)
            dve.tensor_tensor(level_mask[:, 2, :], level_mask[:, 0, :], level_mask[:, 1, :],
                              ALU.bitwise_xor).then_inc(const_dve, 1)

            norm(0)
            dve.wait_ge(const_pool, 7)
            own.did(dve.tensor_copy(order_xor[:, :], level_mask[:, 2, :]))
            for n in range(LEVELS):
                own.settle()
                own.did(dve.tensor_scalar(level_mask[:, n, :], order_xor[:, :], n, None, ALU.arith_shift_right))
            own.settle()
            own.did(dve.tensor_scalar(level_mask[:, :, :], level_mask[:, :, :], 1, None, ALU.is_equal))
            split_lo(0, 0)
            split_lo(1, 1)
            dve.wait_ge(params_in, 16 * 8)
            dve.tensor_tensor(lb_neg[:, :], lb_par[:, 0, :], lb_par[:, 1, :], ALU.subtract).then_inc(lb_diff, 1)
            dve.wait_ge(lb_sig, 1)
            own.did(dve.tensor_scalar(lb_neg[:, :], lb[:, :], -1.0, None, ALU.add))
            dve.tensor_scalar(lb_not[:, :], lb[:, :], -1.0, 1.0, ALU.mult, ALU.add).then_inc(const_dve, 1)
            split_lo(2, 0)
            for t in range(NT):
                dve.wait_ge(evacuated, 4 + t + 1)
                own.did(dve.bn_stats(ln_stats[:, t, :], v_tm[:, t, :]))
            for t in range(NT):
                own.settle()
                if t < NT - 1:
                    own.did(dve.bn_aggr(ln_mv[:, t, :], ln_stats[:, t, :]))
                else:
                    dve.bn_aggr(ln_mv[:, t, :], ln_stats[:, t, :]).then_inc(ln_var, 1)
            split_lo(3, 1)
            dve.wait_ge(ln_sd, 1)
            own.did(dve.reciprocal(ln_rstd[:, :], ln_rstd[:, :]))
            own.settle()
            for t in range(NT):
                own.did(dve.tensor_scalar(v_tm[:, t, :], v_tm[:, t, :], ln_mv[:, t, 0:1], ln_rstd[:, t:t + 1],
                                          ALU.subtract, ALU.mult))
                own.settle()
                own.did(dve.tensor_tensor(v_tm[:, t, :], v_tm[:, t, :], ln_g[:, :], ALU.mult))
                own.settle()
                dve.tensor_tensor(v_tm[:, t, :], v_tm[:, t, :], ln_b[:, :], ALU.add).then_inc(v_normed, 1)
            split_los(g_fquo)
            split_lo(g_ga.chunk0, 0)
            dve.wait_ge(evacuated, g_fquo.tile0 + 4 + 12)
            for j in range(NH):
                dve.wait_ge(spatial_done, j + 1)
                dve.tensor_tensor(u_fm[:, j, :], u_fm[:, j, :], mb[j][:, :], ALU.mult).then_inc(ya_done, 1)
            split_lo(g_ga.chunk0 + 1, 1)
            for h in range(NH):
                dve.wait_ge(hg_log, h + 1)
                for c in range(T // HC):
                    dve.tensor_tensor_scan(kend_fm[:, h, c * HC:(c + 1) * HC], ones[:, 0:HC],
                                           b_fm[:, h, c * HC:(c + 1) * HC], 0.0, ALU.mult, ALU.add)\
                        .then_inc(hg_cum, 1)
            split_lo(g_ga.chunk0 + 2, 0)
            for h in range(NH):
                own.did(dve.tensor_scalar(f_fm[:, h, :], f_fm[:, h, :], lb_neg[:, h:h + 1], lb_not[:, h:h + 1],
                                          ALU.mult, ALU.add))
            split_lo(g_ga.chunk0 + 3, 1)
            dve.wait_ge(hg_exp, 2)
            own.settle()
            dve.tensor_tensor(q_fm[:, :, :], q_fm[:, :, :], eb_fm[:, :, :], ALU.mult).then_inc(hg_ready, 1)
            dve.tensor_tensor(f_fm[:, :, :], f_fm[:, :, :], b_fm[:, :, :], ALU.mult).then_inc(hg_ready, 1)
            own.did(dve.tensor_copy(decay[:, :, :], eb_fm[:, :, HC - 1:T:HC]))
            dve.wait_ge(hg_ready, 2)
            own.settle()
            last = decay[:, :, :].rearrange("p h (c o) -> p (h c) o", o=1).broadcast_to([P, NH * (T // HC), HC])
            dve.tensor_tensor(kend_fm[:, :, :].rearrange("p h (c t) -> p (h c) t", t=HC),
                              f_fm[:, :, :].rearrange("p h (c t) -> p (h c) t", t=HC), last,
                              ALU.mult).then_inc(hg_ready, 1)
            dve.wait_ge(hg_att, 2 * NT)
            dve.wait_ge(hg_ready, 3)
            q2 = q_fm[:, :, :].rearrange("p h (c t) -> p (h c) t", t=HC)
            k2 = kend_fm[:, :, :].rearrange("p h (c t) -> p (h c) t", t=HC)
            dl = decay[:, :, :].rearrange("p h (c o) -> p (h c) o", o=1)
            half = [P, NH * NT, HC]
            dve.tensor_tensor(k2[:, 0::2, :], k2[:, 0::2, :], dl[:, 1::2, :].broadcast_to(half), ALU.mult)\
                .then_inc(hg_scaled, 1)
            dve.tensor_tensor(q2[:, 1::2, :], q2[:, 1::2, :], dl[:, 0::2, :].broadcast_to(half), ALU.mult)\
                .then_inc(hg_scaled, 1)
            own.did(dve.tensor_tensor(ln_stats[:, :, 0:NH], decay[:, :, 0::2].rearrange("p h c -> p c h"),
                                      decay[:, :, 1::2].rearrange("p h c -> p c h"), ALU.mult))
            own.settle()
            for u in range(2):
                for s in range(2):
                    split_lo(g_gb.chunk0 + 2 * u + s, s)
            for t in range(NT - 1):
                for h in range(NH):
                    dve.wait_ge(hg_ds, t + 1)
                    ds_h = mb[t][:, h * P:(h + 1) * P]
                    if t == 0:
                        dve.tensor_copy(s_hg[:, 0, h, :], ds_h).then_inc(hg_state, 1)
                    else:
                        dve.wait_ge(hg_state, NH * (t - 1) + h + 1)
                        dve.scalar_tensor_tensor(s_hg[:, t, h, :], s_hg[:, t - 1, h, :], ln_stats[:, t, h:h + 1],
                                                 ds_h, ALU.mult, ALU.add).then_inc(hg_state, 1)
            for h in range(NH):
                dve.wait_ge(y_hi, h + 1)
                rest(act_lo[:, h, :], u_fm[:, h, :], act_hi[:, h, :]).then_inc(y_lo, 1)
            def gate_tile(dst, k, j):
                return dve.tensor_tensor(dst[:, k, :], dst[:, k, :], gb[j][:, :], ALU.mult).then_inc(evacuated, 1)

            split_lo(g_upa.chunk0, 0)
            dve.wait_ge(hg_sd, 1)
            dve.reciprocal(rs_hg[:, :], rs_hg[:, :]).then_inc(hg_rs, 1)
            split_lo(g_upa.chunk0 + 1, 1)
            evac_unit(g_upa.chunk0, lambda j: gate_tile(ga_fm, j, j))
            for h in range(NH):
                dve.wait_ge(hg_rsb, h + 1)
                own.did(dve.scalar_tensor_tensor(o_fm[:, h, :], o_fm[:, h, :], hg_gain[:, h:h + 1], mb[h][:, :],
                                                 ALU.mult, ALU.mult))
                own.settle()
                dve.tensor_tensor(o_fm[:, h, :], o_fm[:, h, :], og_fm[:, h, :], ALU.mult).then_inc(yb_done, 1)
            split_lo(g_upb.chunk0, 0)
            for h in range(NH):
                dve.wait_ge(y_hi, NH + h + 1)
                rest(act_lo[:, 4 + h, :], o_fm[:, h, :], act_hi[:, 4 + h, :]).then_inc(y_lo, 1)
            evac_unit(g_upa.chunk0 + 1, lambda j: gate_tile(ga_fm, 4 + j, j))
            split_lo(g_upb.chunk0 + 1, 1)
            for u in range(2):
                def both(j, u=u):
                    gate_tile(gb_fm, 4 * u + j, j)
                    dve.wait_ge(evacuated, g_upb.tile0 + 4 + 4 * u + j + 1)
                    dve.tensor_tensor(ga_fm[:, 4 * u + j, :], ga_fm[:, 4 * u + j, :], gb_fm[:, 4 * u + j, :],
                                      ALU.add).then_inc(merged, 1)

                evac_unit(g_upb.chunk0 + u, both)
                split_lo(g_out.chunk0 + u, u)
                for k in range(4 * u, 4 * u + 4):
                    dve.wait_ge(y_hi, AT_MERGED + k + 1)
                    rest(act_lo[:, k, :], ga_fm[:, k, :], act_hi[:, k, :]).then_inc(y_lo, 1)

            def add_tile(u, j, width=512):
                xt = x[:, j, u * 512:(u + 1) * 512]
                return dve.tensor_tensor(xt, xt, gb[j][:, :], ALU.add)

            split_lo(g_out.chunk0 + 2, 0)
            evac_unit(g_out.chunk0 + 1, lambda j: add_tile(0, j).then_inc(evacuated, 1))
            split_lo(g_out.chunk0 + 3, 1)
            evac_unit(g_out.chunk1 - 1, lambda j: add_tile(1, j).then_inc(evacuated, 1))

            norm(1)
            dve.wait_ge(rw_hi, 1)
            rest(route_lo[:, :, :], route_f[:, :, :], route_hi[:, :, :]).then_inc(rw_lo, 1)
            dve.wait_ge(lg_done, 1)
            own.did(dve.tensor_copy(logits[:, :, :], mb[1][:, 0:NT * ROUTED].rearrange("p (t e) -> p t e", t=NT)))
            own.settle()
            dve.wait_ge(r_pool, 2)
            grp = logits[:, :, 0:NG]

            def per_token(v, n):
                return v.rearrange("p (t o) -> p t o", o=1).broadcast_to([P, NT, n])

            def did(ins):
                own.did(ins)
                own.settle()

            def first_of_max(pick, values, best, index, n, spare):
                did(dve.tensor_tensor(pick, values, per_token(best, n), ALU.is_equal))
                did(dve.scalar_tensor_tensor(spare, pick, -64.0, index, ALU.mult, ALU.add))
                did(dve.tensor_reduce(r_first[:, :], spare, AX.X, ALU.min))
                did(dve.tensor_tensor(pick, spare, per_token(r_first[:, :], n), ALU.is_equal))

            did(dve.tensor_reduce(r_max[:, :], grp, AX.X, ALU.max))
            dve.tensor_tensor(r_grp[:, :, :], grp, per_token(r_max[:, :], NG), ALU.subtract).then_inc(r_shift, 1)
            dve.wait_ge(r_expd, 1)
            did(dve.tensor_reduce(r_pg[:, :], r_exp[:, :, :], AX.X, ALU.add))
            did(dve.reciprocal(r_pg[:, :], r_pg[:, :]))
            first_of_max(r_grp[:, :, :], grp, r_max[:, :], r_iota[:, :, 0:NG], NG, r_bias[:, :, :])
            did(dve.tensor_scalar(r_bias[:, :, :], r_grp[:, :, :], -1.0, HUGE, ALU.add, ALU.mult))
            by_group = [P, NT * NG, EG]
            did(dve.tensor_copy(r_sel[:, :, :], logits[:, :, NG:ROUTED]))
            sel = r_sel[:, :, :].rearrange("p t (g e) -> p (t g) e", g=NG)
            for op, m in ((ALU.mult, r_grp), (ALU.add, r_bias)):
                did(dve.tensor_tensor(sel, sel, m[:, :, :].rearrange("p t (g o) -> p (t g) o", o=1)
                                      .broadcast_to(by_group), op))
            for n in range(2):
                did(dve.tensor_reduce(r_top[n][:, :], r_sel[:, :, :], AX.X, ALU.max))
                first_of_max(r_pick[n][:, :, :], r_sel[:, :, :], r_top[n][:, :], r_iota[:, :, :], NE, r_tmp[:, :, :])
                if n == 0:
                    did(dve.scalar_tensor_tensor(r_sel[:, :, :], r_pick[0][:, :, :], -HUGE, r_sel[:, :, :],
                                                 ALU.mult, ALU.add))
            dve.tensor_tensor(r_any[:, :, :], r_pick[0][:, :, :], r_pick[1][:, :, :], ALU.add).then_inc(picked, 1)
            dve.tensor_tensor(r_top[1][:, :], r_top[1][:, :], r_top[0][:, :], ALU.subtract).then_inc(r_shift, 1)
            dve.wait_ge(r_expd, 2)
            did(dve.tensor_scalar(gate1[:, :], r_d[:, :], 1.0, None, ALU.add))
            did(dve.reciprocal(gate1[:, :], gate1[:, :]))
            did(dve.tensor_tensor(gate1[:, :], gate1[:, :], r_pg[:, :], ALU.mult))
            did(dve.tensor_tensor(gate2[:, :], gate1[:, :], r_d[:, :], ALU.mult))
            dve.wait_ge(ranked, 1)
            ranks = mb[2][:, 0:NT * NE].rearrange("p (t e) -> p t e", t=NT)
            totals = mb[3][:, 0:NT * NE].rearrange("p (t e) -> p t e", t=NT)
            did(dve.tensor_copy(r_rank[:, :, :], ranks))
            did(dve.tensor_copy(r_tot[:, :], totals[:, 0, :]))
            for t in range(1, NT):
                did(dve.tensor_tensor(r_rank[:, t, :], r_rank[:, t, :], r_tot[:, :], ALU.add))
                did(dve.tensor_tensor(r_tot[:, :], r_tot[:, :], totals[:, t, :], ALU.add))
            did(dve.tensor_reduce(r_max[:, 0:1], r_tot[:, :], AX.X, ALU.max))
            did(dve.tensor_copy(most[:, :], r_max[:, 0:1]))
            for n in range(2):
                for src, dst in ((r_rank[:, :, :], r_pos),
                                 (r_slot0[:, :].rearrange("p (o e) -> p o e", o=1).broadcast_to([P, NT, NE]), r_s0)):
                    did(dve.tensor_tensor(r_tmp[:, :, :], r_pick[n][:, :, :], src, ALU.mult))
                    did(dve.tensor_reduce(dst[:, n, :], r_tmp[:, :, :], AX.X, ALU.add))
            did(dve.tensor_copy(r_posi[:, :, :], r_pos[:, :, :]))
            did(dve.tensor_scalar(r_hi[:, :, :], r_posi[:, :, :], SLOTS.bit_length() - 1, None, ALU.arith_shift_right))
            did(dve.tensor_scalar(r_lo[:, :, :], r_posi[:, :, :], SLOTS - 1, None, ALU.bitwise_and))
            did(dve.scalar_tensor_tensor(r_s0[:, :, :], r_hi[:, :, :], float(P * PAIRS), r_s0[:, :, :],
                                         ALU.mult, ALU.add))
            did(dve.scalar_tensor_tensor(r_slot[:, :, :], r_lo[:, :, :], float(PAIRS), r_s0[:, :, :],
                                         ALU.mult, ALU.add))
            dve.sem_inc(routed, 1)

            def experts_dve(r):
                dve.wait_ge(slots_in, 16 if r is None else r * 16 + 16)
                dve.tensor_scalar(slot_token[:, :], slot_choice[:, :], T - 1, None, ALU.bitwise_and)\
                    .then_inc(tokens_done, 1)
                with dve.Fori(0, PAIRS // 2) as i:
                    for s in range(2):
                        n = pair_count(i, s, r)
                        dve.wait_ge(moe_act, 5 * (n + 2) + 3)
                        dve.wait_ge(moe_pe, 9 * (n + 2) + 6)
                        dve.tensor_tensor(gated[s][:, :], silu_h[s][:, :], mb[3][:, :], ALU.mult).then_inc(moe_dve, 1)
                        dve.wait_ge(moe_pe, 9 * (n + 2) + 7)
                        dve.tensor_copy(gatedT[s][:, :, :], gb[0][:, :].rearrange("p (k t) -> p k t", k=4))\
                            .then_inc(moe_dve, 1)

            dve.sem_inc(moe_dve, 4)
            experts_dve(None)
            main_round_done(dve)
            fullest = dve.value_load(most[0:1, 0:1], min_val=0, max_val=T)
            with dve.Fori(1, ROUNDS) as r:
                with dve.If(fullest > r * SLOTS):
                    experts_dve(r)
            def combine(t):
                dve.wait_ge(y_back[t], 32)
                own.did(dve.scalar_tensor_tensor(x[:, t, :], y_in[2 * t][:, :], gate1[:, t:t + 1], x[:, t, :],
                                                 ALU.mult, ALU.add))
                own.settle()
                dve.scalar_tensor_tensor(x[:, t, :], y_in[2 * t + 1][:, :], gate2[:, t:t + 1], x[:, t, :],
                                         ALU.mult, ALU.add).then_inc(x_moe, 1)

            for b in range(2):
                dve.wait_ge(p_hi, b + 1)
                rest(pT_lo[:, b, :], mb[b][:, :], pT_hi[:, b, :]).then_inc(p_lo, 1)
            dve.wait_ge(moe_done, 1)
            split_lo(g_pg.chunk0, 0)
            split_lo(g_pg.chunk0 + 1, 1)
            norm(2, combine)
            split_lo(g_pg.chunk0 + 2, 0)
            split_lo(g_pg.chunk0 + 3, 1)
            split_los(g_ple)
            dve.wait_ge(evacuated, all_out(g_pg))
            for u in range(2):
                for j in range(4):
                    dve.wait_ge(pe_tiles, 4 * (g_ple.chunk0 + u) + j + 1)
                    if u or j >= 2:
                        dve.wait_ge(x_ple, 4 * u + j - 1)
                    dve.tensor_tensor(ple_t[j % 2][:, :], gb[j][:, :], sg_tm[:, j, u * 512:(u + 1) * 512], ALU.mult)\
                        .then_inc(evacuated, 1)
                    dve.wait_ge(evacuated, g_ple.tile0 + 4 + 4 * u + j + 1)
                    xt = x[:, j, u * 512:(u + 1) * 512]
                    dve.tensor_tensor(xt, xt, ple_t[j % 2][:, :], ALU.add).then_inc(x_ple, 1)

            norm(3)
            split_lo(g_qk.chunk0, 0)
            norm(4)
            split_lo(g_qk.chunk0 + 1, 1)
            dve.wait_ge(low_split, 1)
            rest(low_lo[:, :, :], low_f[:, :, :], low_hi[:, :, :]).then_inc(low_split, 1)
            for c in range(2, 6):
                split_lo(g_qk.chunk0 + c, c % 2)
            split_lo(g_gv.chunk0, 0)
            split_lo(g_gv.chunk0 + 1, 1)
            for h in range(NH):
                dve.wait_ge(la_act, h + 1)
                own.did(dve.tensor_scalar(la_fm[:, h, :], mb[h][:, :], gate_bias[:, h:h + 1], 0.0, ALU.add, ALU.min))
            own.settle()
            dve.wait_ge(la_act, NH + 1)
            own.did(dve.tensor_tensor(la_fm[:, :, :], la_fm[:, :, :], la_tmp[:, :, :], ALU.subtract))
            own.settle()
            for h in range(NH):
                for t in range(NT):
                    dve.tensor_tensor_scan(la_sum[:, h, t * P:(t + 1) * P], ones[:, 0:P],
                                           la_fm[:, h, t * P:(t + 1) * P], 0.0, ALU.mult, ALU.add)\
                        .then_inc(la_cum, 1)
            split_lo(g_gv.chunk0 + 2, 0)
            split_lo(g_gv.chunk0 + 3, 1)
            split_lo(g_gla.chunk0, 0)
            dve.wait_ge(sb_ones, 2)
            with dve.Fori(0, SBH // 2) as h:
                for n in range(2 * NT):
                    s, t = n % 2, n % 4
                    end = (t + 1) * P
                    dve.wait_ge(sb_past, h * 16 + 2 * n + 2)
                    dve.tensor_tensor_scan(sb_later[s][:, end - 2::-1], sb_fail[s][:, end - 1:0:-1],
                                           ones[:, 0:end - 1], 1.0, ALU.mult, ALU.mult).then_inc(sb_weight, 1)
                    dve.wait_ge(sb_weight, h * 16 + 2 * n + 1)
                    dve.tensor_tensor(sb_w[s][:, 0:end], sb_w[s][:, 0:end], sb_later[s][:, 0:end], ALU.mult)\
                        .then_inc(sb_weight, 1)
                    dve.wait_ge(sb_turned, h * 8 + n + 1)
                    dve.tensor_copy(sb_wT[:, 0:t + 1, :],
                                    mb[2][:, 0:(t + 1) * P].rearrange("p (k t) -> p k t", t=P)).then_inc(sb_wT_done, 1)
                    if n == 1:
                        split_lo(h * 2 + (g_gla.chunk0 + 1), 1)
                    if n == 5:
                        split_lo(h * 2 + (g_gla.chunk0 + 2), 0)
            dve.wait_ge(la_cum, NH * NT)
            dve.wait_ge(sb_o, 8 * (SBH // 2) + 8)

            def copy_scores(n):
                for t in range(NT):
                    dve.wait_ge(gl_mm, NT * n + t + 1)
                    mask = (level_mask[:, n, :] if n < LEVELS else ident[:, :].bitcast(I32))
                    dve.copy_predicated(g_att[:, t, :, :],
                                        mask.rearrange("p (o t) -> p o t", o=1).broadcast_to([P, NH, P]),
                                        mb[t][:, :].rearrange("p (h t) -> p h t", h=NH)).then_inc(gl_copied, 1)

            def halves(a, m):
                v = a[:, :, :].rearrange("p h (c t) -> p (h c) t", t=2 * m)
                return v[:, :, 0:m], v[:, :, m:2 * m], v[:, :, m - 1:m].broadcast_to([P, NH * T // (2 * m), m])

            def distances(n):
                b0, b1, mid = halves(la_sum, 1 << n)
                e0, e1, _ = halves(gl_e, 1 << n)
                dve.tensor_tensor(e0, mid, b0, ALU.subtract).then_inc(gl_dist, 1)
                dve.tensor_tensor(e1, b1, mid, ALU.subtract).then_inc(gl_dist, 1)

            distances(0)
            dve.wait_ge(gla_q, 1)
            dve.wait_ge(g_att_zero, 1)
            for n in range(LEVELS):
                (e0, e1, _), (k0, _, _), (_, q1, _), (qk0, qk1, _) = (
                    halves(a, 1 << n) for a in (gl_e, gk_fm, gq_fm, gl_qk))
                dve.wait_ge(gl_exp, n + 1)
                if n:
                    dve.wait_ge(gl_mm, NT * n)
                dve.tensor_tensor(qk0, e0, k0, ALU.mult).then_inc(gl_prod, 1)
                dve.tensor_tensor(qk1, e1, q1, ALU.mult).then_inc(gl_prod, 1)
                if n < LEVELS - 1:
                    dve.wait_ge(gl_prod, 2 * n + 2)
                    distances(n + 1)
                copy_scores(n)
                split_lo(g_gates.chunk0 + n + 1, (n + 1) % 2)
            by_tile = "p h (c t) -> p (h c) t"
            sums = la_sum[:, :, :].rearrange(by_tile, t=P)
            dve.wait_ge(gl_prod, 2 * LEVELS)
            dve.tensor_tensor(gl_qk[:, :, :].rearrange(by_tile, t=P), sums[:, :, P - 1:P].broadcast_to([P, NH * NT, P]),
                              sums, ALU.subtract).then_inc(gl_edge, 1)
            copy_scores(LEVELS)
            dve.wait_ge(gl_edge_exp, 3)
            dve.tensor_tensor(gk_fm[:, :, :], gk_fm[:, :, :], gl_qk[:, :, :], ALU.mult).then_inc(gl_scaled, 1)
            dve.tensor_tensor(gq_fm[:, :, :], gq_fm[:, :, :], gl_e[:, :, :], ALU.mult).then_inc(gl_scaled, 1)
            split_lo(g_psb.chunk0, 0)
            split_lo(g_psb.chunk0 + 1, 1)
            for t in range(NT - 1):
                for h in range(NH):
                    dve.wait_ge(gl_ds, 2 * t + h // 2 + 1)
                    ds_h = mb[2 * (t % 2) + h // 2][:, (h % 2) * DV:(h % 2 + 1) * DV]
                    if t == 0:
                        dve.tensor_copy(s_gla[0][:, h, :], ds_h).then_inc(gl_state, 1)
                    else:
                        dve.wait_ge(gl_state, NH * (t - 1) + h + 1)
                        dve.scalar_tensor_tensor(s_gla[t][:, h, :], s_gla[t - 1][:, h, :], decay[:, h, t:t + 1],
                                                 ds_h, ALU.mult, ALU.add).then_inc(gl_state, 1)
            for h in range(NH):
                dve.wait_ge(y_hi, AT_YO + h + 1)
                rest(act_lo[:, h, :], sbq[:, h, :], act_hi[:, h, :]).then_inc(y_lo, 1)
            dve.wait_ge(gl_sd, 1)
            dve.reciprocal(rs_gla[:, :], rs_gla[:, :]).then_inc(gl_rs, 1)
            dve.wait_ge(gates_in, 32)
            dve.wait_ge(gout_done, 1)
            for u in range(2):
                evac_unit(g_psb.chunk0 + u, lambda j, u=u: gate_tile(gs_fm, 4 * u + j, j))
                split_lo(g_pgla.chunk0 + u, u)
                for k in range(4 * u, 4 * u + 4):
                    dve.wait_ge(gl_rsb, k // 2 + 1)
                    own.did(dve.scalar_tensor_tensor(go[k], go[k], gla_gain[:, k % 2:k % 2 + 1], mb[k // 2][:, :],
                                                     ALU.mult, ALU.mult))
                    own.settle()
                    dve.tensor_tensor(go[k], go[k], gout_fm[:, k, :], ALU.mult).then_inc(yg_done, 1)
                for k in range(4 * u, 4 * u + 4):
                    dve.wait_ge(y_hi, AT_YG + k + 1)
                    rest(act_lo[:, (k + 4) % KT, :], go[k], act_hi[:, (k + 4) % KT, :]).then_inc(y_lo, 1)
            split_lo(g_pgla.chunk0 + 2, 0)
            for u in range(2):
                def mix(j, u=u):
                    gate_tile(gg_fm, 4 * u + j, j)
                    dve.wait_ge(evacuated, g_pgla.tile0 + 4 + 4 * u + j + 1)
                    dve.tensor_tensor(gs_fm[:, 4 * u + j, :], gs_fm[:, 4 * u + j, :], gg_fm[:, 4 * u + j, :],
                                      ALU.add).then_inc(mixed, 1)

                evac_unit(g_pgla.chunk0 + 2 * u + 1, mix)
                if u == 0:
                    split_lo(g_pgla.chunk0 + 3, 1)
                else:
                    split_lo(g_out2.chunk0 + 1, 1)
                for k in range(4 * u, 4 * u + 4):
                    dve.wait_ge(y_hi, AT_MIX + k + 1)
                    rest(mix_lo[:, k, :], gs_fm[:, k, :], mix_hi[:, k, :]).then_inc(y_lo, 1)
                if u == 0:
                    split_lo(g_out2.chunk0, 0)
            split_lo(g_out2.chunk0 + 2, 0)
            evac_unit(g_out2.chunk0 + 1, lambda j: add_tile(0, j).then_inc(evacuated, 1))
            split_lo(g_out2.chunk0 + 3, 1)
            split_lo(g_ff[0][0].chunk0, 0)
            evac_unit(g_out2.chunk1 - 1, lambda j: add_tile(1, j).then_inc(evacuated, 1))

            norm(5)

            def hidden_unit(h, u):
                for j in range(4):
                    seen = u * 4 + (4 * up.units * h + j + 1)
                    dve.wait_ge(evacuated, u * 4 + (up.tile0 + 4 + j + 1))
                    dve.tensor_tensor(relu_sq[j][:, :], relu_t[j][:, :], relu_t[j][:, :], ALU.mult)\
                        .then_inc(hid_sq, 1)
                for j in range(4):
                    seen = u * 4 + (4 * up.units * h + j + 1)
                    dve.wait_ge(hid_hi_done, seen)
                    dve.wait_ge(hid_sq, seen)
                    dst = [hidden[:, ds(u * 4 + j, 1), :].rearrange("p o t -> p (o t)") for hidden in (hid_lo, hid_hi)]
                    rest(dst[0], relu_sq[j][:, :], dst[1]).then_inc(hid_lo_done, 1)

            for h, (up, down) in enumerate(g_ff):
                if h:
                    split_lo(up.chunk0, 0)
                split_lo(up.chunk0 + 1, 1)
                with dve.Fori(1, up.units) as u:
                    split_lo(u * 2 + up.chunk0, 0)
                    hidden_unit(h, u - 1)
                    split_lo(u * 2 + up.chunk0 + 1, 1)
                split_lo(down.chunk0, 0)
                hidden_unit(h, up.units - 1)
                split_lo(down.chunk0 + 1, 1)
                for u in range(down.units):
                    for c in range(2 if u == 0 else 1, down.chunks):
                        split_lo(down.chunk0 + u * down.chunks + c, c % 2)
                    if u + 1 < down.units:
                        split_lo(down.chunk0 + (u + 1) * down.chunks, 0)
                    evac_unit(down.chunk0 + (u + 1) * down.chunks - 1,
                              lambda j, u=u: add_tile(u, j).then_inc(evacuated, 1))
            norm(6)

        @block.tensor
        def _(pe):
            def tile_passes(g, chunk, tile, s, kc, j, fm, a_hi=act_hi, a_lo=act_lo, base=(0, 4, 8, 12)):
                hi, lo = w_hi[s], w_lo[s]
                if j == 0:
                    pe.wait_ge(w_lo_done, chunk + 1)
                if kc == 0:
                    pe.wait_ge(evacuated, tile + 1)
                cols = slice(j * P, (j + 1) * P)
                for k in range(g.ktiles):
                    ka = base[kc] + k
                    if fm:
                        passes = ((hi[:, k, cols], a_hi[:, ka, :]), (hi[:, k, cols], a_lo[:, ka, :]),
                                  (lo[:, k, cols], a_hi[:, ka, :]))
                    else:
                        passes = ((a_hi[:, ka, cols], hi[:, k, :]), (a_hi[:, ka, cols], lo[:, k, :]),
                                  (a_lo[:, ka, cols], hi[:, k, :]))
                    for n_pass, (left, right) in enumerate(passes):
                        ins = pe.matmul(gb[j][:, :], left, right, start=(kc == 0 and k == 0 and n_pass == 0),
                                        stop=(kc == g.chunks - 1 and k == g.ktiles - 1 and n_pass == 2))
                ins.then_inc(pe_tiles, 1)

            def multiply(g, i, per_body, ready, after, **operand):
                for u in range(per_body):
                    for kc in range(g.chunks):
                        n = u * g.chunks + kc
                        for j in range(4):
                            ready(kc, j)
                            tile_passes(g, i * (g.chunks * per_body) + (g.chunk0 + n),
                                        i * (4 * per_body) + (g.tile0 + 4 * u + j), n % 2, kc, j, **operand)
                    after(u)

            def gemm(g, ready=lambda kc, j: None, after=lambda u: None, **operand):
                if g.other_taker:
                    pe.wait_ge(evacuated, g.tile0 + 4)
                per_body = 2 if g.chunks == 1 else 1
                if g.units == per_body:
                    multiply(g, 0, per_body, ready, after, **operand)
                    return
                with pe.Fori(0, g.units // per_body) as i:
                    multiply(g, i, per_body, ready, after, **operand)

            def turn(dst, src):
                return pe.transpose(dst, src, ident[:, :])

            def norm(n):
                for q in range(2 * NT):
                    t, b = q // 2, q % 2
                    if b == 0:
                        pe.wait_ge(n_xn, NT * n + t + 1)
                    if q >= 4:
                        pe.wait_ge(n_lo, turned_before(n) + q - 3)
                    for k in range(4):
                        ins = turn(mb[q % 4][:, k * P:(k + 1) * P], xn_at[n][:, t, (4 * b + k) * P:(4 * b + k + 1) * P])
                    ins.then_inc(n_tp, 1)

            def rows_split(n):
                return lambda kc, j: kc == 0 and pe.wait_ge(n_lo, turned_before(n) + 2 * (j + 1))

            def all_split(n):
                pe.wait_ge(n_lo, turned_before(n) + 2 * NT)

            def half_split(count):
                return lambda kc, j: j == 0 and pe.wait_ge(y_lo, count + 4 * (kc + 1))

            pe.sem_inc(evacuated, 4)
            pe.wait_ge(const_pool, 6)
            norm(0)
            gemm(g_vi, fm=False, ready=rows_split(0))
            gemm(g_fquo, fm=True)
            pe.wait_ge(wsp_masked, 1)
            for b in range(2):
                for g in range(4):
                    ins = turn(mb[b][:, g * P:(g + 1) * P], w_sp[:, 4 * b + g, :])
                ins.then_inc(wsp_turned, 1)
            pe.wait_ge(v_normed, NT)
            pe.wait_ge(wspT_done, 2)
            for j in range(NH):
                for t in range(NT):
                    cols = slice(t * P, (t + 1) * P)
                    ins = pe.matmul(mb[j][:, cols], group_sel[:, j * P:(j + 1) * P], b_sp[:, :], start=True, stop=False,
                                    skip_group_check=True)
                    for q in range(2):
                        g = 2 * j + q
                        ins = pe.matmul(mb[j][q * GD:(q + 1) * GD, cols], v_tm[:, t, g * GD:(g + 1) * GD],
                                        w_spT[:, g, :], start=False, stop=True, skip_group_check=True)
                ins.then_inc(spatial_done, 1)
            gemm(g_ga, fm=True)
            pe.wait_ge(hg_ready, 3)
            pe.wait_ge(ya_done, NH)
            for t in range(NT):
                cols = slice(t * P, (t + 1) * P)
                if t >= 2:
                    pe.wait_ge(hg_att_out, 3 * (t - 1))
                for h in range(NH):
                    ins = pe.matmul(mb[2 * (t % 2)][:, h * P:(h + 1) * P], f_fm[:, h, cols], q_fm[:, h, cols],
                                    start=True, stop=True, skip_group_check=True)
                ins.then_inc(hg_att, 1)
                for h in range(NH):
                    ins = pe.matmul(mb[2 * (t % 2) + 1][0:HC, h * P:(h + 1) * P], kend_fm[:, h, t * P:t * P + HC],
                                    q_fm[:, h, cols], start=True, stop=True, skip_group_check=True)
                ins.then_inc(hg_att, 1)
            pe.wait_ge(hg_scaled, 2)
            pe.wait_ge(hg_att_out, 3 * NT)
            for t in range(NT):
                for h in range(NH):
                    ins = turn(mb[t][:, h * P:(h + 1) * P], kend_fm[:, h, t * P:(t + 1) * P])
                ins.then_inc(kend_turned, 1)
            gemm(g_gb, fm=True)
            for t in range(NT - 1):
                pe.wait_ge(kend_done, NT)
                for h in range(NH):
                    cols = slice(h * P, (h + 1) * P)
                    ins = pe.matmul(mb[t][:, cols], kend_tm[:, t, cols], i_tm[:, t, cols], start=True, stop=True,
                                    skip_group_check=True)
                ins.then_inc(hg_ds, 1)
            pe.wait_ge(att_masked, NT)
            pe.wait_ge(hg_state, NH * (NT - 1))
            for h in range(NH):
                for t in range(NT):
                    cols = slice(t * P, (t + 1) * P)
                    ins = pe.matmul(mb[h][:, cols], i_tm[:, t, h * P:(h + 1) * P], attT[:, t, h, :], start=True,
                                    stop=(t == 0), skip_group_check=True)
                    if t:
                        ins = pe.matmul(mb[h][:, cols], s_hg[:, t - 1, h, :], q_fm[:, h, cols], start=False, stop=True,
                                        skip_group_check=True)
                ins.then_inc(hg_o, 1)
            pe.wait_ge(hg_sq, NH)
            for h in range(NH):
                ins = pe.matmul(mb[0][32 * h:32 * h + 32, :], ones[:, 0:32], sq_fm[:, h, :], start=True, stop=True,
                                skip_group_check=True)
            ins.then_inc(hg_ss, 1)
            pe.wait_ge(y_lo, NH)

            def spread_roots(u):
                if u == 0:
                    pe.wait_ge(hg_rs, 1)
                    pe.wait_ge(r_pool, 1)
                    for h in range(NH):
                        pe.matmul(mb[h][:, :], head_sel[:, h, :], rs_hg[:, :], start=True, stop=True)\
                            .then_inc(hg_rsb, 1)

            gemm(g_upa, fm=True, after=spread_roots)
            pe.wait_ge(y_lo, 2 * NH)
            gemm(g_upb, fm=True, a_hi=act_hi[:, 4:8, :], a_lo=act_lo[:, 4:8, :])
            gemm(g_out, fm=False, ready=half_split(AT_MERGED))

            norm(1)
            all_split(1)
            pe.wait_ge(rw_lo, 1)
            for k in range(KT):
                for n, (left, right) in enumerate(((route_hi, act_hi), (route_hi, act_lo), (route_lo, act_hi))):
                    ins = pe.matmul(mb[0][:, :], left[:, k, :], right[:, k, :], start=(k == 0 and n == 0),
                                    stop=(k == KT - 1 and n == 2))
            ins.then_inc(lgT_done, 1)
            pe.wait_ge(lgT_out, 1)
            for t in range(NT):
                ins = pe.transpose(mb[1][:, t * ROUTED:(t + 1) * ROUTED], logitT[0:ROUTED, t * P:(t + 1) * P],
                                   ident[0:ROUTED, 0:ROUTED])
            ins.then_inc(lg_done, 1)
            pe.wait_ge(picked, 1)
            any_flat = r_any[:, :, :].rearrange("p t e -> p (t e)")
            pe.matmul(mb[2][:, 0:NT * NE], earlier[:, :], any_flat, start=True, stop=True)
            pe.matmul(mb[3][:, 0:NT * NE], ones[:, 0:P], any_flat, start=True, stop=True).then_inc(ranked, 1)
            pe.wait_ge(routed, 1)

            def experts_pe(r):
                with pe.Fori(0, PAIRS // 2) as i:
                    for s in range(2):
                        n = pair_count(i, s, r)
                        half = i if r is None else i + r * (PAIRS // 2)
                        pe.wait_ge(gathered[s], half * 16 + 16)
                        pe.wait_ge(moe_act, 5 * (n + 1) + 2)
                        for b in range(2):
                            for k in range(4):
                                ins = turn(mb[b][:, k * P:(k + 1) * P], xg[s][:, (4 * b + k) * P:(4 * b + k + 1) * P])
                            ins.then_inc(moe_pe, 1)
                        pe.wait_ge(moe_act, 5 * (n + 2) + 2)
                        for w, dst in ((0, mb[2]), (1, mb[3])):
                            if w == 1:
                                pe.wait_ge(moe_dve, 2 * (n + 1) + 1)
                            for kh in range(2):
                                pe.wait_ge(ring_in[2 * w + kh], n * 32 + 32)
                                for k in range(4):
                                    for q in range(2):
                                        mine = slice(q * HALF, (q + 1) * HALF)
                                        ins = pe.matmul(dst[mine, :], xgT[s][:, 4 * kh + k, mine],
                                                        ring[4 * w + 2 * kh + q][:, k, :],
                                                        start=(kh == 0 and k == 0), stop=(kh == 1 and k == 3),
                                                        skip_group_check=True)
                                ins.then_inc(moe_pe, 1)
                        pe.wait_ge(moe_dve, 2 * (n + 2) + 1)
                        for k in range(4):
                            ins = turn(gb[0][:, k * P:(k + 1) * P], gated[s][:, k * P:(k + 1) * P])
                        ins.then_inc(moe_pe, 1)
                        pe.wait_ge(moe_dve, 2 * (n + 2) + 2)
                        pe.wait_ge(moe_act, 5 * (n + 1) + 5)
                        for nh in range(2):
                            pe.wait_ge(ring_in[4 + nh], n * 32 + 32)
                            for k in range(4):
                                for q in range(2):
                                    mine = slice(q * HALF, (q + 1) * HALF)
                                    ins = pe.matmul(gb[1 + nh][mine, :], gatedT[s][:, k, mine],
                                                    ring[8 + 2 * nh + q][:, k, :], start=(k == 0), stop=(k == 3),
                                                    skip_group_check=True)
                            ins.then_inc(moe_pe, 1)

            pe.sem_inc(moe_pe, 18)
            experts_pe(None)
            main_round_done(pe)
            fullest = pe.value_load(most[0:1, 0:1], min_val=0, max_val=T)
            with pe.Fori(1, ROUNDS) as r:
                with pe.If(fullest > r * SLOTS):
                    experts_pe(r)

            pe.wait_ge(p_in, 16)
            for b in range(2):
                for t in range(NT):
                    ins = turn(mb[b][:, t * P:(t + 1) * P], p_tm[:, t, b * P:(b + 1) * P])
                ins.then_inc(p_turned, 1)
            pe.wait_ge(p_lo, 2)
            norm(2)
            gemm(g_pg, fm=False, ready=rows_split(2))
            gemm(g_ple, fm=False, a_hi=pT_hi, a_lo=pT_lo)

            norm(4)
            all_split(4)
            gemm(g_qk, fm=True)
            pe.wait_ge(low_split, 2)
            for k in range(KT):
                for n, (left, right) in enumerate(((low_hi, act_hi), (low_hi, act_lo), (low_lo, act_hi))):
                    ins = pe.matmul(mb[0][:, :], left[:, k, :], right[:, k, :], start=(k == 0 and n == 0),
                                    stop=(k == KT - 1 and n == 2))
            ins.then_inc(low_z, 1)
            gemm(g_sv, fm=False)
            pe.wait_ge(lowT_done, 1)
            for h in range(NH):
                pe.matmul(mb[h][:, :], gate_up[:, h * P:(h + 1) * P], lowT[:, :], start=True, stop=True)\
                    .then_inc(la_z, 1)
            gemm(g_gv, fm=False)
            pe.wait_ge(evacuated, all_out(g_qk))
            pe.wait_ge(la_cum, NH * NT)
            pe.sem_inc(sb_o, 8)
            pe.sem_inc(sb_sig, 2)
            pe.sem_inc(sb_wT_done, 1)
            pe.sem_inc(sb_o_out, 1)

            def scores(h, n):
                s, t = n % 2, n % 4
                rows = slice((n // 4) * SBD, (n // 4 + 1) * SBD)
                if n == 0:
                    pe.wait_ge(sb_qk_in, h * 2 + 2)
                if n or not isinstance(h, int):
                    pe.wait_ge(sb_sig, h * 16 + 2 * n)
                pe.matmul(mb[s][:, 0:(t + 1) * P], sb_q[rows, t * P:(t + 1) * P], sb_k[rows, 0:(t + 1) * P],
                          start=True, stop=True).then_inc(sb_z, 1)

            def sb_turn(h, last):
                for n in range(2 * NT):
                    s, t = n % 2, n % 4
                    if n < 2 * NT - 1:
                        scores(h, n + 1)
                    elif not last:
                        scores(h + 1, 0)
                    pe.wait_ge(sb_weight, h * 16 + 2 * n + 2)
                    pe.wait_ge(sb_wT_done, h * 8 + n + 1)
                    for b in range(t + 1):
                        ins = turn(mb[2][:, b * P:(b + 1) * P], sb_w[s][:, b * P:(b + 1) * P])
                    ins.then_inc(sb_turned, 1)
                    kc, j = n // 4, n % 4
                    tile_passes(g_gla, h * 2 + (g_gla.chunk0 + kc), h * 4 + (g_gla.tile0 + j), kc, kc, j, fm=True)
                    pe.wait_ge(sb_wT_done, h * 8 + n + 2)
                    if n == 0:
                        pe.wait_ge(sb_o_out, h + 1)
                        pe.wait_ge(sb_v_in, h + 1)
                    rows = slice((n // 4) * SBD, (n // 4 + 1) * SBD)
                    for b in range(t + 1):
                        ins = pe.matmul(mb[3][rows, t * P:(t + 1) * P], sb_v[:, b, rows], sb_wT[:, b, :],
                                        start=(b == 0), stop=(b == t), skip_group_check=True)
                    ins.then_inc(sb_o, 1)

            scores(0, 0)
            with pe.Fori(0, SBH // 2 - 1) as h:
                sb_turn(h, False)
            sb_turn(SBH // 2 - 1, True)
            pe.wait_ge(sb_o_out, SBH // 2 + 1)

            def gates_chunk(n):
                for j in range(4):
                    tile_passes(g_gates, g_gates.chunk0 + n, g_gates.tile0 + 4 * (n // 2) + j, n % 2, n % 2, j, fm=True)

            for n in range(LEVELS + 1):
                if n < LEVELS:
                    pe.wait_ge(gl_prod, 2 * n + 2)
                for t in range(NT):
                    cols = slice(t * P, (t + 1) * P)
                    if n:
                        pe.wait_ge(gl_copied, NT * (n - 1) + t + 1)
                    for h in range(NH):
                        left, right = (gl_qk, gl_qk) if n < LEVELS else (gk_fm, gq_fm)
                        ins = pe.matmul(mb[t][:, h * P:(h + 1) * P], left[:, h, cols], right[:, h, cols],
                                        start=True, stop=True, skip_group_check=True)
                    ins.then_inc(gl_mm, 1)
                gates_chunk(n)
            pe.wait_ge(gl_scaled, 2)
            pe.wait_ge(gl_copied, NT * (LEVELS + 1))
            for t in range(NT):
                for h in range(NH):
                    ins = turn(mb[t][:, h * P:(h + 1) * P], gk_fm[:, h, t * P:(t + 1) * P])
                ins.then_inc(gkend_turned, 1)
            pe.wait_ge(gkend_done, NT)
            for t in range(NT - 1):
                if t == 2:
                    pe.wait_ge(gl_state, NH)
                for h in range(NH):
                    ins = pe.matmul(mb[2 * (t % 2) + h // 2][:, (h % 2) * DV:(h % 2 + 1) * DV],
                                    gkend_tm[:, t, h * P:(h + 1) * P], gv_tm[:, t, h * DV:(h + 1) * DV],
                                    start=True, stop=True, skip_group_check=True)
                    if h % 2:
                        ins.then_inc(gl_ds, 1)
            pe.wait_ge(gl_state, NH * (NT - 1))
            for n in range(KT):
                h = n // 2
                if n >= 2:
                    pe.wait_ge(gl_sq, n - 1)
                for t in range(NT):
                    cols = slice(t * P, (t + 1) * P)
                    vals = slice((n % 2) * P, (n % 2 + 1) * P)
                    ins = pe.matmul(mb[n % 2][:, cols], gv_tm[:, t, n * P:(n + 1) * P], g_att[:, t, h, :], start=True,
                                    stop=(t == 0), skip_group_check=True)
                    if t:
                        ins = pe.matmul(mb[n % 2][:, cols], s_gla[t - 1][:, h, vals], gq_fm[:, h, cols], start=False,
                                        stop=True, skip_group_check=True)
                ins.then_inc(gl_o, 1)
                if n % 2:
                    pe.wait_ge(gl_sq, n + 1)
                    for v in range(2):
                        ins = pe.matmul(mb[2][32 * h:32 * h + 32, :], ones[:, 0:32], gsq[h % 2][:, v, :],
                                        start=(v == 0), stop=(v == 1), skip_group_check=True)
                    ins.then_inc(gl_ss, 1)
            pe.wait_ge(y_lo, AT_YO + NH)

            def spread_gla(u):
                if u == 0:
                    pe.wait_ge(gl_rs, 1)
                    pe.wait_ge(r_pool, 3)
                    for h in range(NH):
                        pe.matmul(mb[h][:, :], gsel[:, h, :], rs_gla[:, :], start=True, stop=True)\
                            .then_inc(gl_rsb, 1)

            gemm(g_psb, fm=True, after=spread_gla)
            gemm(g_pgla, fm=True, base=(4, 0), ready=half_split(AT_YG))
            gemm(g_out2, fm=False, a_hi=mix_hi, a_lo=mix_lo, ready=half_split(AT_MIX))

            norm(5)
            all_split(5)
            for h, (up, down) in enumerate(g_ff):
                gemm(up, fm=True)
                pe.wait_ge(hid_lo_done, (h + 1) * 4 * up.units)
                gemm(down, fm=False, a_hi=hid_hi, a_lo=hid_lo, base=tuple(range(0, FH // P, 4)))


_INS = ["x", "p", "g_mix", "w_in", "gm_ln_g", "gm_ln_b", "gm_w_sp", "gm_b_sp", "w_up_a", "hg_lb_param",
        "hg_norm_g", "w_up_b", "w_out", "g_ffn", "w_grp", "w_exp", "w1", "w3", "w2", "g_ple", "w_pg",
        "w_ple", "g_final", "norm_mix_2", "w_in_2", "w_gate_up_2", "b_gate_up_2", "gla_norm_2",
        "w_proj_sb_2", "w_proj_gla_2", "w_out_2", "norm_mlp_2", "w_ff1_2", "w_ff2_2", "norm_final_2"]


def kernel(**inputs):
    import numpy as np
    import concourse.bacc as bacc
    from concourse.bass_utils import run_bass_kernel_spmd

    nc = bacc.Bacc("TRN2", target_bir_lowering=False, num_devices=1)
    arrays, aps = {}, {}
    for name in _INS:
        a = np.ascontiguousarray(inputs[name])
        arrays[f"in_{name}"] = a
        aps[name] = nc.dram_tensor(f"in_{name}", a.shape, mybir.dt.from_np(a.dtype), kind="ExternalInput").ap()
    out = nc.dram_tensor("out", inputs["x"].shape, F32, kind="ExternalOutput").ap()
    two_blocks(nc, aps, out)
    r = run_bass_kernel_spmd(nc, [arrays], core_ids=[0])
    return r.results[0]["out"]
```

```python
from contextlib import ExitStack

import concourse.bass as bass
from concourse import mybir

ALU = mybir.AluOpType
ACT = mybir.ActivationFunctionType
F32 = mybir.dt.float32
F32R = mybir.dt.float32r
I32 = mybir.dt.int32
AX = mybir.AxisListType
ds = bass.ds

P = 128
EPS = 1e-6
HUGE = 3.0e38


class Gemm:

    def __init__(self, after, units, chunks, taker, ktiles=4):
        self.taker, self.after = taker, after
        self.units, self.chunks, self.ktiles = units, chunks, ktiles
        self.chunk0 = after.chunk1 if after else 0
        self.out = dict(after.out) if after else {"act": 0, "dve": 0}
        self.tile0 = self.out[taker]
        self.chunk1 = self.chunk0 + units * chunks
        self.tile1 = self.out[taker] = self.tile0 + 4 * units


class Chain:

    def __init__(self, eng, sem):
        self.eng, self.sem, self.n = eng, sem, 0
        self.turn, self.per = None, 0

    def did(self, ins):
        ins.then_inc(self.sem, 1)
        self.n += 1

    def settle(self):
        self.eng.wait_ge(self.sem, self.n if self.turn is None else self.turn * self.per + self.n)

    def enter(self, turn, per):
        self.turn, self.per, self.start = turn, per, self.n

    def leave(self, turns):
        assert self.n - self.start == self.per, (self.n - self.start, self.per)
        self.n += (turns - 1) * self.per
        self.turn = None


def two_blocks(nc, A, out):
    T, D = A["x"].shape[1:]
    NT, KT = T // P, D // P
    GW = A["gm_ln_g"].shape[1]
    GG = A["gm_w_sp"].shape[1]
    GD = GW // GG
    HW = A["hg_norm_g"].shape[1]
    NH = HW // P
    HC = 64
    NE = A["w1"].shape[1]
    EG = 8
    NG = NE // EG
    FE = A["w1"].shape[3]
    PD = A["p"].shape[3]
    SBH, SBD = 8, 64
    GR = A["w_gate_up_2"].shape[1]
    DV = A["gla_norm_2"].shape[1]
    FF = A["w_ff1_2"].shape[2]
    SLOTS = 64
    ROUNDS = T // SLOTS
    PAIRS = NE // 2
    ROUTED = NG + NE
    FAR = 4096
    FIRST_PLACE = -2 * ROUNDS * FAR
    LEVELS = 7
    assert (T, D, GW, HW, FE, DV) == (512, 1024, 512, 512, 512, 256)

    g_vi = Gemm(None, 2, 2, "act")
    g_fquo = Gemm(g_vi, 4, 2, "act")
    g_ga = Gemm(g_fquo, 2, 2, "act")
    g_gb = Gemm(g_ga, 2, 2, "act")
    g_upa = Gemm(g_gb, 2, 1, "dve")
    g_upb = Gemm(g_upa, 2, 1, "dve")
    g_out = Gemm(g_upb, 2, 2, "dve")
    g_pg = Gemm(g_out, 2, 2, "act")
    g_ple = Gemm(g_pg, 2, 1, "dve", ktiles=PD // P)
    g_sv = Gemm(g_ple, 1, 2, "act")
    g_gv = Gemm(g_sv, 2, 2, "act")
    g_qk = Gemm(g_gv, 2, 2, "act")
    g_gla = Gemm(g_qk, 4, 2, "act")
    g_gates = Gemm(g_gla, 4, 2, "act")
    g_psb = Gemm(g_gates, 2, 1, "dve")
    g_pgla = Gemm(g_psb, 2, 2, "dve")
    g_out2 = Gemm(g_pgla, 2, 2, "dve")
    HALVES = 2
    FH = FF // HALVES
    g_ff = []
    last = g_out2
    for _ in range(HALVES):
        up = Gemm(last, FH // 512, 2, "act")
        last = Gemm(up, 2, FH // 512, "dve")
        g_ff.append((up, last))

    gates_dram = nc.dram_tensor("branch_gates", [2 * KT, P, T], F32).ap()

    ctx = ExitStack()
    with ctx:
        PAGE = 2048
        base = (nc.sbuf_base + 63) // 64 * 64
        ctx.enter_context(nc.sbuf_tensor("fence", [P, 103 * 512], F32))

        def at(name, page, shape, dt=F32):
            return nc.alloc_sbuf_tensor_at(name, shape, dt, offset=base + int(page * PAGE))

        def sem(name):
            return ctx.enter_context(nc.semaphore(name))

        x = at("x_tm", 0, [P, NT, D])
        small_at = [8 * PAGE]

        def small(name, shape, dt=F32):
            n = 4
            for s in shape[1:]:
                n *= s
            t = nc.alloc_sbuf_tensor_at(name, shape, dt, offset=base + small_at[0])
            small_at[0] += (n + 31) // 32 * 32
            assert small_at[0] <= 13 * PAGE, small_at
            return t

        ident = small("ident", [P, P])
        ones = small("ones", [P, T])
        earlier = small("earlier", [P, P])
        level_mask = small("level_mask", [P, LEVELS, P], I32)
        eps_col = small("eps_col", [P, 1])
        one_col = small("one_col", [P, 1])
        lb_par = small("lb_par", [P, 2, NH])
        lb = small("lb", [P, NH])
        lb_not = small("lb_not", [P, NH])
        lb_neg = small("lb_neg", [P, NH])
        hg_gain = small("hg_gain", [P, NH])
        gate_bias = small("gate_bias", [P, NH])
        gla_gain = small("gla_gain", [P, DV // P])
        ssq = small("ssq", [P, NT])
        rstd = small("rstd", [P, NT])
        ln_stats = small("ln_stats", [P, NT, 6])
        ln_mv = small("ln_mv", [P, NT, 2])
        ln_rstd = small("ln_rstd", [P, NT])
        decay = small("decay", [P, NH, T // HC])
        b_sp = small("b_sp", [GG, P])
        most = small("most", [P, 1], I32)
        choice_gates = small("choice_gates", [P, 2 * NT])
        slot_gate = small("slot_gate", [P, PAIRS])
        iota_row = small("iota_row", [P, P])
        place_in = small("place_in", [P, 2 * NT, PAIRS])
        r_place = small("r_place", [P, 2 * NT])
        iota_place = small("iota_place", [P, P])
        first_place = small("first_place", [P, NE])
        pair_gate = small("pair_gate", [P, 2 * NT, PAIRS])

        act_hi = at("act_hi", 13, [P, KT, T], F32R)
        act_lo = at("act_lo", 21, [P, KT, T], F32R)
        w_stage = [at(f"w_stage{s}", 29 + 4 * s, [P, 4, 512]) for s in range(2)]
        w_hi = [at(f"w_hi{s}", 41 - 4 * s, [P, 4, 512], F32R) for s in range(2)]
        w_lo = [at(f"w_lo{s}", 45 + 4 * s, [P, 4, 512], F32R) for s in range(2)]
        F = 53
        xn_at = {0: F + 8, 1: 41, 2: F + 36, 6: F + 40}
        xn_at = {n: at(f"xn_{n}", page, [P, NT, D]) for n, page in xn_at.items()}
        xn_at.update({n: xn_at[2] for n in (3, 4, 5)})
        gain = at("gain", F + 48, [P, D])
        gain_4 = at("gain_4", F + 44, [P, D])
        u_fm = at("u_fm", F + 0, [P, NH, T])
        v_tm = at("v_tm", F + 4, [P, NT, GW])
        q_fm = at("q_fm", F + 8, [P, NH, T])
        f_fm = at("f_fm", F + 12, [P, NH, T])
        i_tm = at("i_tm", F + 16, [P, NT, HW])
        og_fm = at("og_fm", F + 20, [P, NH, T])
        ga_fm = at("ga_fm", F + 24, [P, KT, T])
        gb_fm = at("gb_fm", F + 32, [P, KT, T])
        b_fm = at("b_fm", F + 40, [P, NH, T])
        kend_fm = at("kend_fm", F + 44, [P, NH, T])
        w_sp = at("w_sp", F + 40, [P, GG, P])
        w_spT = at("w_spT", F + 42, [P, GG, P])
        ln_g = at("ln_g", F + 44, [P, GW])
        ln_b = at("ln_b", F + 45, [P, GW])
        group_sel = at("group_sel", F + 32, [GG, GW])
        eb_fm = at("eb_fm", F + 32, [P, NH, T])
        order_xor = at("order_xor", F + 47, [P, P], I32)
        attT = at("attT", F + 4, [P, NT, NH, P])
        kend_tm = at("kend_tm", F + 40, [P, NT, HW])
        s_hg = at("s_hg", F + 12, [P, NT - 1, NH, P])
        o_fm = at("o_fm", F + 44, [P, NH, T])
        sq_fm = at("sq_fm", F + 8, [P, NH, T])
        rs_hg = at("rs_hg", F + 40, [P, T])
        head_sel = at("head_sel", F + 41, [P, NH, P])
        ring = [at(f"ring{j}", F + 4 * j, [P, 4, 512]) for j in range(12)]
        xn_hi = at("xn_hi", 21, [P, NT, D], F32R)
        xn_lo = at("xn_lo", 41, [P, NT, D], F32R)
        xgT = at("xgT", 13, [P, KT, P])
        sel = at("sel", 15, [P, NT, P], F32R)
        selT = at("selT", 16, [P, T], F32R)
        gated = at("gated", 17, [P, FE])
        gatedT = at("gatedT", 18, [P, FE // P, P])
        xg = at("xg", F + 48, [P, D])
        y_hi_sb = at("y_hi_sb", F + 48, [P, D], F32R)
        y_lo_sb = at("y_lo_sb", 19, [P, D], F32R)
        place_1h = at("place_1h", 19, [P, 2 * NT, P])
        EXTRA = 4
        extra = [at(f"extra{j}", page, [P, 4, 512]) for j, page in enumerate((29, 33, 37, 49))]
        assert len(extra) == EXTRA
        logitT = at("logitT", 36, [ROUTED, T])
        route_f = at("route_f", 33, [P, KT, ROUTED])
        route_lo = at("route_lo", 33, [P, KT, ROUTED], F32R)
        route_hi = at("route_hi", 35, [P, KT, ROUTED], F32R)
        routes_at = [16 * PAGE]

        def routes(name, shape, dt=F32):
            n = 4
            for s in shape[1:]:
                n *= s
            t = nc.alloc_sbuf_tensor_at(name, shape, dt, offset=base + routes_at[0])
            routes_at[0] += (n + 31) // 32 * 32
            assert routes_at[0] <= 19 * PAGE, routes_at
            return t

        logits = routes("logits", [P, NT, ROUTED])
        r_max = routes("r_max", [P, NT])
        r_gpick = routes("r_gpick", [P, NT, NG])
        r_grp = routes("r_grp", [P, NT, NG])
        r_exp = routes("r_exp", [P, NT, NG])
        r_pg = routes("r_pg", [P, NT])
        r_first = routes("r_first", [P, NT])
        r_bias = routes("r_bias", [P, NT, NG])
        r_sel = routes("r_sel", [P, NT, NE])
        r_picks = routes("r_picks", [P, 2 * NT, NE])
        r_pick = [r_picks[:, n * NT:(n + 1) * NT, :] for n in range(2)]
        r_tmp = routes("r_tmp", [P, NT, NE])
        r_tmps = routes("r_tmps", [P, 2 * NT, NE])
        r_any = routes("r_any", [P, NT, NE])
        r_rank = routes("r_rank", [P, NT, NE])
        r_top = [routes(f"r_top{n}", [P, NT]) for n in range(2)]
        r_d = routes("r_d", [P, NT])
        r_hi = routes("r_hi", [P, NT, NE], I32)
        gain_2 = at("gain_2", F + 0, [P, D])
        sg_tm = at("sg_tm", F + 16, [P, NT, D])
        p_tm = at("p_tm", F + 24, [P, NT, PD])
        pT_hi = at("pT_hi", F + 26, [P, PD // P, T], F32R)
        pT_lo = at("pT_lo", F + 28, [P, PD // P, T], F32R)
        ple_t = [at(f"ple_t{s}", F + 30 + s, [P, 512]) for s in range(2)]
        sbq = at("sbq", F + 0, [P, 4, T])
        sbk = at("sbk", F + 4, [P, 4, T])
        sbv = at("sbv", F + 8, [P, NT, 512])
        gv_tm = at("gv_tm", F + 12, [P, NT, D])
        g_all = at("g_all", F + 20, [P, 4 * NH, T])
        gq_fm = g_all[:, 0:NH, :]
        gk_fm = g_all[:, NH:2 * NH, :]
        gout_fm = g_all[:, 2 * NH:4 * NH, :]
        sb_q = at("sb_q", F + 36, [P, T])
        sb_v = at("sb_v", F + 37, [P, NT, P])
        sb_fail = [at(f"sb_fail{s}", F + 38 + s, [P, T]) for s in range(2)]
        sb_w = [at(f"sb_w{s}", F + 40 + s, [P, T]) for s in range(2)]
        sb_later = [at(f"sb_later{s}", F + 42 + s, [P, T]) for s in range(2)]
        sb_wT = at("sb_wT", F + 44, [P, NT, P])
        sb_k = at("sb_k", F + 45, [P, T])
        low_f = at("low_f", F + 20, [P, KT, P])
        low_hi = at("low_hi", F + 22, [P, KT, P], F32R)
        low_lo = at("low_lo", F + 24, [P, KT, P], F32R)
        lowT = at("lowT", F + 26, [GR, T])
        gate_up = at("gate_up", F + 27, [GR, HW])
        la_fm = at("la_fm", F + 28, [P, NH, T])
        la_tmp = at("la_tmp", F + 32, [P, NH, T])
        la_sum = at("la_sum", F + 46, [P, NH, T])
        gl_e = at("gl_e", F + 36, [P, NH, T])
        gl_qk = at("gl_qk", F + 40, [P, NH, T])
        gate_out = [at(f"gate_out{s}", F + 44 + s, [P, T]) for s in range(2)]
        g_att = at("g_att", F + 4, [P, NT, NH, P])
        gkend_tm = at("gkend_tm", F + 40, [P, NT, HW])
        s_gla = [at(f"s_gla{n}", F + 8 + 2 * n, [P, NH, DV]) for n in range(2)]
        s_gla.append(at("s_gla2", F + 36, [P, NH, DV]))
        go_all = at("go", F + 20, [P, KT, T])
        go = [go_all[:, (n + KT // 2) % KT, :] for n in range(KT)]
        gsq = [at(f"gsq{s}", F + 40 + 2 * s, [P, 2, T]) for s in range(2)]
        rs_gla = at("rs_gla", F + 38, [P, T])
        gsel = at("gsel", F + 39, [P, NH, P])
        gs_fm = at("gs_fm", F + 12, [P, KT, T])
        gg_fm = at("gg_fm", F + 4, [P, KT, T])
        mix_hi = at("mix_hi", F + 20, [P, KT, T], F32R)
        mix_lo = at("mix_lo", F + 28, [P, KT, T], F32R)
        hid_hi = at("hid_hi", F + 0, [P, FH // P, T], F32R)
        hid_lo = at("hid_lo", F + 16, [P, FH // P, T], F32R)
        relu_t = [at(f"relu_t{s}", F + 32 + s, [P, T]) for s in range(4)]
        relu_sq = [at(f"relu_sq{s}", F + 36 + s, [P, T]) for s in range(4)]

        bank = [ctx.enter_context(nc.psum_tensor(f"bank{b}", [P, 512], F32)) for b in range(8)]
        gb, mb = bank[:4], bank[4:]

        x_in = [sem(f"x_in{t}") for t in range(NT)]
        w_loaded = [sem(f"w_loaded{s}") for s in range(2)]
        w_hi_done, w_lo_done = sem("w_hi_done"), sem("w_lo_done")
        pe_tiles = sem("pe_tiles")
        out_act, out_dve = sem("out_act"), sem("out_dve")
        n_sd = sem("n_sd")
        n_xn, n_tp, n_hi, n_lo = sem("n_xn"), sem("n_tp"), sem("n_hi"), sem("n_lo")
        gain_in, gain_2_in, gain_4_in = sem("gain_in"), sem("gain_2_in"), sem("gain_4_in")
        const_pool, const_dve, params_in = sem("const_pool"), sem("const_dve"), sem("params_in")
        dve_own, act_own, pool_own = sem("dve_own"), sem("act_own"), sem("pool_own")
        lb_diff, lb_sig = sem("lb_diff"), sem("lb_sig")
        wsp_masked, wsp_turned, wspT_done = sem("wsp_masked"), sem("wsp_turned"), sem("wspT_done")
        ln_var, ln_sd, v_normed = sem("ln_var"), sem("ln_sd"), sem("v_normed")
        spatial_done, ya_done = sem("spatial_done"), sem("ya_done")
        hg_log, hg_cum, hg_exp = sem("hg_log"), sem("hg_cum"), sem("hg_exp")
        hg_ready, hg_att, hg_att_out = sem("hg_ready"), sem("hg_att"), sem("hg_att_out")
        att_zero, att_masked = sem("att_zero"), sem("att_masked")
        hg_scaled, kend_turned, kend_done = sem("hg_scaled"), sem("kend_turned"), sem("kend_done")
        hg_ds, hg_state = sem("hg_ds"), sem("hg_state")
        hg_o, hg_sq = sem("hg_o"), sem("hg_sq")
        hg_ss, hg_sd, hg_rs, hg_rsb, yb_done = (sem("hg_ss"), sem("hg_sd"), sem("hg_rs"),
                                                sem("hg_rsb"), sem("yb_done"))
        y_hi, y_lo = sem("y_hi"), sem("y_lo")
        AT_MERGED = 2 * NH
        AT_YO = AT_MERGED + KT
        AT_YG = AT_YO + NH
        AT_MIX = AT_YG + KT
        merged = sem("merged")
        route_in, rw_hi, rw_lo, logits_done = sem("route_in"), sem("rw_hi"), sem("rw_lo"), sem("logits_done")
        logitT_done, logitT_out = sem("logitT_done"), sem("logitT_out")
        r_expd = sem("r_expd")
        r_shift, r_pool = sem("r_shift"), sem("r_pool")
        picked, ranked, routed = sem("picked"), sem("ranked"), sem("routed")
        xn_hi_done, xn_lo_done = sem("xn_hi_done"), sem("xn_lo_done")

        placed, tabled, valued, next_round = sem("placed"), sem("tabled"), sem("valued"), sem("next_round")
        sel_made, sel_turned, selT_out = sem("sel_made"), sem("sel_turned"), sem("selT_out")
        rows_in, xg_out, rows_turned, rows_out = sem("rows_in"), sem("xg_out"), sem("rows_turned"), sem("rows_out")
        up_done, down_done = sem("up_done"), sem("down_done")
        silu_done, gated_done = sem("silu_done"), sem("gated_done")
        gated_turned, gatedT_out = sem("gated_turned"), sem("gatedT_out")
        y_hi_out, y_lo_out = sem("y_hi_out"), sem("y_lo_out")
        spread_done, moe_added = sem("spread_done"), sem("moe_added")
        extra_in = sem("extra_in")
        ring_in = [sem(f"ring_in{j}") for j in range(6)]
        wait_carrier = sem("wait_carrier")
        p_in, p_turned, p_hi, p_lo = sem("p_in"), sem("p_turned"), sem("p_hi"), sem("p_lo")
        x_ple = sem("x_ple")
        sb_first_in, sb_second_in, sb_v_in = sem("sb_first_in"), sem("sb_second_in"), sem("sb_v_in")
        sb_z, sb_sig, sb_past = sem("sb_z"), sem("sb_sig"), sem("sb_past")
        sb_weight, sb_turned, sb_wT_done = sem("sb_weight"), sem("sb_turned"), sem("sb_wT_done")
        sb_o, sb_o_out, sb_ones = sem("sb_o"), sem("sb_o_out"), sem("sb_ones")
        low_in, low_pad, low_split, low_z = sem("low_in"), sem("low_pad"), sem("low_split"), sem("low_z")
        lowT_done, la_z, la_act, la_cum = sem("lowT_done"), sem("la_z"), sem("la_act"), sem("la_cum")
        gla_q, gout_done = sem("gla_q"), sem("gout_done")
        sb_gate_in, gla_gate_in = sem("sb_gate_in"), sem("gla_gate_in")
        gates_stored = [sem(f"gates_stored{s}") for s in range(2)]
        gl_dist, gl_exp, gl_prod, gl_mm, gl_copied = (sem("gl_dist"), sem("gl_exp"), sem("gl_prod"),
                                                      sem("gl_mm"), sem("gl_copied"))
        g_att_zero, gl_edge, gl_edge_exp, gl_scaled = (sem("g_att_zero"), sem("gl_edge"),
                                                       sem("gl_edge_exp"), sem("gl_scaled"))
        gkend_turned, gkend_done = sem("gkend_turned"), sem("gkend_done")
        gl_ds, gl_state, gl_o, gl_sq = sem("gl_ds"), sem("gl_state"), sem("gl_o"), sem("gl_sq")
        gl_ss, gl_sd, gl_rs, gl_rsb, yg_done = (sem("gl_ss"), sem("gl_sd"), sem("gl_rs"),
                                                sem("gl_rsb"), sem("yg_done"))
        mixed = sem("mixed")
        hid_hi_done, hid_sq, hid_lo_done = sem("hid_hi_done"), sem("hid_sq"), sem("hid_lo_done")
        out_stored = sem("out_stored")

        block = ctx.enter_context(nc.Block())

        ROWS_ONLY = (3, 6)

        def turned_before(n):
            return 2 * NT * (n - sum(m < n for m in ROWS_ONLY))

        def rows_count(n, t):
            if n in (3, 4):
                return 3 * NT + ((1, 2, 4, 6) if n == 3 else (3, 5, 7, 8))[t]
            return n * NT + t + 1

        def all_out(g):
            return g.tile1 + 4

        def taken(g):
            return out_act if g.taker == "act" else out_dve

        def gla_bank(n):
            return mb[(0, 1, 3)[n % 3]]

        def pair_number(i, r):
            return i if r is None else i + r * PAIRS

        def col(i):
            return slice(i, i + 1) if isinstance(i, int) else ds(i, 1)

        @block.sync
        def _(sp):
            def load_chunk(c, s, w, cols, kc, ktiles=4):
                if isinstance(c, int):
                    if c >= 2:
                        sp.wait_ge(w_lo_done, c - 1)
                else:
                    sp.wait_ge(w_lo_done, c - 1)
                src = w[kc * 512:kc * 512 + ktiles * P, cols].rearrange("(k p) n -> p k n", p=P)
                sp.dma_start(w_stage[s][:, 0:ktiles, :], src).then_inc(w_loaded[s], 16)

            def load_unit(g, u, w, col):
                for kc in range(g.chunks):
                    c = g.chunk0 + u * g.chunks + kc
                    load_chunk(c, c % 2, w, slice(col, col + 512), kc, g.ktiles)

            def load_units(g, w, col, k0=0):
                if g.units * g.chunks == 2:
                    for u in range(g.units):
                        load_unit(g, u, w, col + 512 * u)
                    return
                with sp.Fori(0, g.units) as u:
                    for kc in range(g.chunks):
                        load_chunk(g.chunk0 + g.chunks * u + kc, kc % 2, w,
                                   ds(u * 512 + col, 512), k0 + kc, g.ktiles)

            def load_gain(n, g):
                if n in (2, 4):
                    dst, done = (gain_2, gain_2_in) if n == 2 else (gain_4, gain_4_in)
                    sp.dma_start(dst[:, :], g.rearrange("(o d) -> o d", o=1).broadcast_to([P, D])).then_inc(done, 16)
                    return
                if n == 5:
                    sp.wait_ge(y_lo, AT_YG + KT)
                elif n:
                    sp.wait_ge(n_xn, NT * (2 if n == 3 else n))
                sp.dma_start(gain[:, :], g.rearrange("(o d) -> o d", o=1).broadcast_to([P, D]))\
                    .then_inc(gain_in, 16)

            x_dram = A["x"][0].rearrange("(t p) d -> t p d", p=P)
            w_in = A["w_in"][0]
            for t in range(NT):
                sp.dma_start(x[:, t, :], x_dram[t]).then_inc(x_in[t], 16)
                if t == 0:
                    load_gain(0, A["g_mix"][0])
                if t % 2:
                    load_chunk(t // 2, t // 2, w_in, slice(512, 2 * 512), t // 2)
            load_unit(g_vi, 1, w_in, 4 * 512)
            for u, col in enumerate((3, 2, 0, 5)):
                load_unit(g_fquo, u, w_in, col * 512)
            load_units(g_ga, w_in, 6 * 512)
            load_units(g_gb, w_in, 8 * 512)
            load_units(g_upa, A["w_up_a"][0], 0)
            load_units(g_upb, A["w_up_b"][0], 0)
            load_units(g_out, A["w_out"][0], 0)
            load_gain(1, A["g_ffn"][0])

            def piece_used(n, j):
                if j < 8:
                    sp.wait_ge(up_done, n * 4 + (j // 2 + 1))
                else:
                    sp.wait_ge(down_done, n * 2 + ((j - 8) // 2 + 1))

            def load_piece(j, e0, dst=None, done=None):
                q = j % 2
                e = e0 + q
                h = (j // 2) % 2
                if j < 8:
                    w = A["w1"] if j < 4 else A["w3"]
                    src = w[0, ds(e, 1), h * 512:(h + 1) * 512, :].rearrange("e (k p) n -> p (e k) n", p=P)
                else:
                    src = A["w2"][0, ds(e, 1), :, h * 512:(h + 1) * 512]\
                        .rearrange("e (k p) n -> p (e k) n", p=P)
                dst, done = (ring[j], ring_in[j // 2]) if dst is None else (dst, done)
                sp.dma_start(dst[:, :, :], src).then_inc(done, 16)

            sp.wait_ge(y_lo, AT_MERGED + KT)
            for j in range(6):
                load_piece(j, 0)
            sp.wait_ge(w_lo_done, g_out.chunk1)
            sp.dma_start(route_f[:, :, 0:NG], A["w_grp"][0].rearrange("(k p) n -> p k n", p=P))\
                .then_inc(route_in, 16)
            sp.dma_start(route_f[:, :, NG:ROUTED], A["w_exp"][0].rearrange("(k p) n -> p k n", p=P))\
                .then_inc(route_in, 16)
            for j in range(6, 12):
                load_piece(j, 0)
            def load_extra(j):
                load_piece(j, 2, extra[j], extra_in)

            load_extra(0)
            sp.wait_ge(pe_tiles, 4 * g_out.chunk1)
            load_extra(2)
            load_extra(3)
            sp.wait_ge(logits_done, 1)
            load_extra(1)

            for j in range(EXTRA):
                piece_used(0, j)
                load_piece(j, 4)
            for j in range(EXTRA, 12):
                piece_used(0, j)
                load_piece(j, 2)
            for j in range(EXTRA, 12):
                piece_used(1, j)
                load_piece(j, 4)
            with sp.Fori(2, PAIRS - 1) as i:
                for j in range(12):
                    piece_used(i, j)
                    load_piece(j, i * 2 + 2)
            load_unit(g_pg, 0, A["w_pg"][0], 0)
            sp.wait_ge(routed, 1)
            fullest = sp.value_load(most[0:1, 0:1], min_val=0, max_val=T)
            with sp.If(fullest > SLOTS):
                with sp.Fori(1, ROUNDS) as r:
                    with sp.If(fullest > r * SLOTS):
                        with sp.Fori(0, PAIRS) as i:
                            for j in range(12):
                                piece_used(i + r * PAIRS - 1, j)
                                load_piece(j, i * 2)
                        sp.wait_ge(spread_done, r * (8 * PAIRS) + 8 * PAIRS)
                        sp.sem_inc(wait_carrier, 1)
            sp.wait_ge(up_done, 4 * PAIRS)
            load_gain(2, A["g_ple"][0])
            sp.dma_start(p_tm[:, :, :], A["p"][0, 0].rearrange("(t p) d -> p t d", p=P)).then_inc(p_in, 16)
            load_unit(g_pg, 1, A["w_pg"][0], 512)
            sp.wait_ge(spread_done, 8 * PAIRS)
            load_gain(3, A["g_final"])
            load_gain(4, A["norm_mix_2"][0])
            load_units(g_ple, A["w_ple"][0], 0)
            w_in2 = A["w_in_2"][0]
            load_unit(g_sv, 0, w_in2, 2 * 512)
            sp.wait_ge(low_pad, 1)
            sp.dma_start(low_f[:, :, 0:GR], w_in2[:, 9 * 512:9 * 512 + GR]
                         .rearrange("(k p) n -> p k n", p=P)).then_inc(low_in, 16)
            sp.dma_start(gate_up[:, :], A["w_gate_up_2"][0]).then_inc(low_in, 16)
            load_units(g_gv, w_in2, 5 * 512)
            load_units(g_qk, w_in2, 0)
            for u, col in enumerate((3, 4, 7, 8)):
                load_unit(g_gla, u, w_in2, col * 512)
            load_units(g_gates, w_in2, 9 * 512 + GR)
            load_units(g_psb, A["w_proj_sb_2"][0], 0)
            for s in range(2):
                sp.wait_ge(gates_stored[s], 16 * KT)
            sp.wait_ge(gl_o, KT)
            for gates, half, done in ((gs_fm, gates_dram[0:KT], sb_gate_in),
                                      (gg_fm, gates_dram[KT:2 * KT], gla_gate_in)):
                sp.dma_start(gates[:, :, :], half.rearrange("k p t -> p k t")).then_inc(done, 16)
            load_units(g_pgla, A["w_proj_gla_2"][0], 0)
            load_units(g_out2, A["w_out_2"][0], 0)
            load_gain(5, A["norm_mlp_2"][0])
            for h, (up, down) in enumerate(g_ff):
                load_units(up, A["w_ff1_2"][0], h * FH)
                load_units(down, A["w_ff2_2"][0], 0, k0=h * FH // 512)
            load_gain(6, A["norm_final_2"])
            out_dram = out[0].rearrange("(t p) d -> t p d", p=P)
            for t in range(NT):
                sp.wait_ge(n_xn, rows_count(6, t))
                sp.dma_start(out_dram[t], xn_at[6][:, t, :]).then_inc(out_stored, 16)
            sp.wait_ge(out_stored, 16 * NT)

        @block.gpsimd
        def _(pool):
            own = Chain(pool, pool_own)

            own.did(pool.memset(ident[:, :], 0.0))
            own.did(pool.memset(earlier[:, :], 1.0))
            own.did(pool.memset(group_sel[:, :], 1.0))
            own.did(pool.iota(level_mask[:, 0, :], pattern=[[0, P]], base=0, channel_multiplier=1))
            own.did(pool.iota(level_mask[:, 1, :], pattern=[[1, P]], base=0, channel_multiplier=0))
            own.settle()
            pool.affine_select(out=ident[:, :], in_=ident[:, :], compare_op=ALU.not_equal, fill=1.0,
                               base=0, pattern=[[-1, P]], channel_multiplier=1).then_inc(const_pool, 1)
            pool.affine_select(out=earlier[:, :], in_=earlier[:, :], compare_op=ALU.is_gt, fill=0.0,
                               base=0, pattern=[[1, P]], channel_multiplier=-1).then_inc(const_pool, 1)
            pool.memset(ones[:, :], 1.0).then_inc(const_pool, 1)
            pool.memset(eps_col[:, :], EPS).then_inc(const_pool, 1)
            pool.memset(one_col[:, :], 1.0).then_inc(const_pool, 1)
            own.did(pool.affine_select(out=group_sel[:, :], in_=group_sel[:, :], compare_op=ALU.is_ge,
                                       fill=0.0, base=0, pattern=[[1, GW]], channel_multiplier=-GD))
            own.settle()
            pool.affine_select(out=group_sel[:, :], in_=group_sel[:, :], compare_op=ALU.is_ge, fill=0.0,
                               base=GD - 1, pattern=[[-1, GW]], channel_multiplier=GD)\
                .then_inc(const_pool, 1)
            pool.dma_start(lb_par[:, :, :], A["hg_lb_param"].rearrange("l (h p) -> p l h", p=P),
                           allow_slow_non_contiguous=True).then_inc(params_in, 16)
            pool.dma_start(hg_gain[:, :], A["hg_norm_g"][0].rearrange("(h p) -> p h", p=P),
                           allow_slow_non_contiguous=True).then_inc(params_in, 16)
            pool.dma_start(gate_bias[:, :], A["b_gate_up_2"][0].rearrange("(h p) -> p h", p=P),
                           allow_slow_non_contiguous=True).then_inc(params_in, 16)
            pool.dma_start(gla_gain[:, :], A["gla_norm_2"][0].rearrange("(h p) -> p h", p=P),
                           allow_slow_non_contiguous=True).then_inc(params_in, 16)
            pool.dma_start(w_sp[:, :, :], A["gm_w_sp"][0].rearrange("g t s -> t g s")).then_inc(params_in, 16)
            pool.dma_start(b_sp[:, :], A["gm_b_sp"][0]).then_inc(params_in, 16)
            for t, name in ((ln_g, "gm_ln_g"), (ln_b, "gm_ln_b")):
                pool.dma_start(t[:, :], A[name].broadcast_to([P, GW])).then_inc(params_in, 16)

            opts = dict(allow_small_or_imprecise_dtypes=True)
            own.did(pool.iota(iota_row[:, :], pattern=[[1, P]], base=0, channel_multiplier=0, **opts))
            own.did(pool.iota(iota_place[:, :], pattern=[[1, P]], base=FIRST_PLACE, channel_multiplier=0, **opts))
            own.did(pool.iota(first_place[:, :], pattern=[[0, PAIRS], [SLOTS, 2]], base=FIRST_PLACE,
                              channel_multiplier=0, **opts))
            own.settle()
            pool.sem_inc(r_pool, 1)
            pool.wait_ge(const_dve, 1)
            pool.affine_select(out=level_mask[:, 2, :], in_=level_mask[:, 2, :], compare_op=ALU.is_gt,
                               fill=0.0, base=0, pattern=[[1, P]], channel_multiplier=-1)\
                .then_inc(const_pool, 1)
            pool.wait_ge(params_in, 16 * 8)
            pool.affine_select(out=w_sp[:, :, :], in_=w_sp[:, :, :], compare_op=ALU.is_ge, fill=0.0,
                               base=0, pattern=[[0, GG], [-1, P]], channel_multiplier=1)\
                .then_inc(wsp_masked, 1)

            pool.wait_ge(ya_done, NH)
            pool.memset(attT[:, :, :, :], 0.0).then_inc(att_zero, 1)
            for t in range(NT):
                pool.wait_ge(hg_att_out, 3 * (t + 1))
                pool.affine_select(out=attT[:, t, :, :], in_=attT[:, t, :, :], compare_op=ALU.is_ge,
                                   fill=0.0, base=0, pattern=[[0, NH], [1, P]], channel_multiplier=-1)\
                    .then_inc(att_masked, 1)
            pool.wait_ge(hg_state, NH * (NT - 1))
            own.did(pool.memset(head_sel[:, :, :], 0.0))
            own.settle()
            own.did(pool.affine_select(out=head_sel[:, :, :], in_=head_sel[:, :, :],
                                       compare_op=ALU.not_equal, fill=1.0, base=0,
                                       pattern=[[-32, NH], [0, P]], channel_multiplier=1))
            own.settle()
            pool.sem_inc(r_pool, 1)

            for t in range(NT):
                pool.wait_ge(xn_hi_done, t + 1)
                pool.tensor_tensor(xn_lo[:, t, :], xn_at[1][:, t, :], xn_hi[:, t, :].bitcast(F32), ALU.subtract)\
                    .then_inc(xn_lo_done, 1)
            pool.wait_ge(rows_in, 2 * PAIRS)
            fullest = pool.value_load(most[0:1, 0:1], min_val=0, max_val=T)
            with pool.If(fullest > SLOTS):
                with pool.Fori(1, ROUNDS) as r:
                    with pool.If(fullest > r * SLOTS):
                        pool.wait_ge(rows_in, r * (2 * PAIRS) + 2 * PAIRS)
                        pool.sem_inc(wait_carrier, 1)
            for s in range(2):
                pool.wait_ge(w_hi_done, g_pg.chunk0 + s + 1)
                pool.tensor_tensor(w_lo[s][:, :, :], w_stage[s][:, :, :], w_hi[s][:, :, :].bitcast(F32), ALU.subtract)\
                    .then_inc(w_lo_done, 1)

            pool.wait_ge(x_ple, 2 * NT)
            pool.memset(low_f[:, :, :], 0.0).then_inc(low_pad, 1)

            def sb_turn(h):
                for n in range(2 * NT):
                    s, t = n % 2, n % 4
                    a, b = t * P, (t + 1) * P
                    pool.wait_ge(sb_sig, h * 16 + 2 * n + 4)
                    pool.sem_inc(wait_carrier, 1)
                    pool.affine_select(out=sb_fail[s][:, a:b], in_=sb_fail[s][:, a:b], compare_op=ALU.is_gt,
                                       fill=1.0, base=0, pattern=[[-1, P]], channel_multiplier=1)\
                        .then_inc(sb_past, 1)
                    pool.affine_select(out=sb_w[s][:, a:b], in_=sb_w[s][:, a:b], compare_op=ALU.is_gt,
                                       fill=0.0, base=0, pattern=[[-1, P]], channel_multiplier=1)\
                        .then_inc(sb_past, 1)
                    if n == 0:
                        pool.wait_ge(sb_o, h * 8 + 8)
                        pool.tensor_copy(sb_v[:, :, :], sbv[:, :, ds(h * P, P)]).then_inc(sb_v_in, 1)

            pool.wait_ge(out_act, all_out(g_qk))
            for s in range(2):
                pool.memset(sb_later[s][:, :], 1.0).then_inc(sb_ones, 1)
            with pool.Fori(0, SBH // 2) as h:
                sb_turn(h)
            pool.wait_ge(sb_z, 8 * (SBH // 2))
            pool.memset(g_att[:, :, :, :], 0.0).then_inc(g_att_zero, 1)
            with pool.Fori(0, KT) as i:
                for s in range(2):
                    pool.wait_ge(out_act, i * 2 + (g_gates.tile0 + 4 + s + 1))
                    pool.sem_inc(wait_carrier, 1)
                    pool.dma_start(gates_dram[ds(i * 2 + s, 1)].rearrange("o p t -> p (o t)"), gate_out[s][:, :])\
                        .then_inc(gates_stored[s], 16)
            pool.wait_ge(gl_state, NH * (NT - 1))
            own.did(pool.memset(gsel[:, :, :], 0.0))
            own.settle()
            own.did(pool.affine_select(out=gsel[:, :, :], in_=gsel[:, :, :],
                                       compare_op=ALU.not_equal, fill=1.0, base=0,
                                       pattern=[[-32, NH], [0, P]], channel_multiplier=1))
            own.settle()
            pool.sem_inc(r_pool, 1)

        @block.scalar
        def _(act):
            own = Chain(act, act_own)

            def split_hi(c, s, ktiles=4):
                act.wait_ge(w_loaded[s], (c // 2 + 1) * 16 if isinstance(c, int) else c * 8 + (16 - 8 * s))
                if not isinstance(c, int) or c >= 2:
                    act.wait_ge(pe_tiles, (c - 1) * 4)
                act.activation(w_hi[s][:, 0:ktiles, :], w_stage[s][:, 0:ktiles, :], ACT.Copy)\
                    .then_inc(w_hi_done, 1)

            def evac_unit(last_chunk, put):
                for j in range(4):
                    act.wait_ge(pe_tiles, last_chunk * 4 + j + 1)
                    put(j).then_inc(out_act, 1)

            def evac_f(dst, func, scale=1.0):
                return lambda j: act.activation(dst[:, j, :], gb[j][:, :], func, scale=scale)

            def at_tile(dst, u, j):
                return dst[:, ds(u * 4 + j, 1), :].rearrange("p o t -> p (o t)")

            def sum_squares(n, t):
                own.did(act.activation(xn_at[n][:, t, :], x[:, t, :], ACT.Square, accum_out=ssq[:, t:t + 1]))
                own.settle()
                act.activation(rstd[:, t:t + 1], ssq[:, t:t + 1], ACT.Sqrt, bias=eps_col[:, 0:1],
                               scale=1.0 / D).then_inc(n_sd, 1)

            def norm(n, ready, mid=lambda: None):
                def root(t):
                    ready(t)
                    sum_squares(n, t)

                def high(t):
                    if n in ROWS_ONLY:
                        return
                    for b in range(2):
                        q = 2 * t + b
                        act.wait_ge(n_tp, turned_before(n) + q + 1)
                        act.activation(act_hi[:, 4 * b:4 * b + 4, t * P:(t + 1) * P],
                                       mb[q % 4][:, :].rearrange("p (k t) -> p k t", k=4), ACT.Copy)\
                            .then_inc(n_hi, 1)

                root(0)
                for t in range(1, NT):
                    root(t)
                    if t == 1:
                        mid()
                    high(t - 1)
                high(NT - 1)

            def rows_added(g, t):
                act.wait_ge(taken(g), all_out(g) - NT + t + 1)

            act.wait_ge(const_pool, 5)
            c = g_vi.chunk0
            norm(0, lambda t: act.wait_ge(x_in[t], 16), mid=lambda: split_hi(c, 0))
            split_hi(c + 1, 1)
            act.wait_ge(lb_diff, 1)
            act.activation(lb[:, :], lb_neg[:, :], ACT.Sigmoid).then_inc(lb_sig, 1)
            split_hi(c + 2, 0)
            evac_unit(c + 1, evac_f(v_tm, ACT.Gelu_apprx_tanh))
            split_hi(c + 3, 1)
            act.wait_ge(ln_var, 1)
            act.activation(ln_rstd[:, :], ln_mv[:, :, 1], ACT.Sqrt, bias=eps_col[:, 0:1]).then_inc(ln_sd, 1)
            for u, (dst, func) in enumerate(((f_fm, ACT.Sigmoid), (q_fm, ACT.Silu),
                                             (u_fm, ACT.Gelu_apprx_tanh), (og_fm, ACT.Sigmoid))):
                split_hi(g_fquo.chunk0 + 2 * u, 0)
                if u == 0:
                    evac_unit(g_vi.chunk1 - 1, evac_f(i_tm, ACT.Copy))
                else:
                    evac_unit(g_fquo.chunk0 + 2 * u - 1, evac_f(*prev))
                split_hi(g_fquo.chunk0 + 2 * u + 1, 1)
                prev = (dst, func)
            for b in range(2):
                act.wait_ge(wsp_turned, b + 1)
                act.activation(w_spT[:, 4 * b:4 * b + 4, :],
                               mb[b][:, :].rearrange("p (g t) -> p g t", g=4), ACT.Copy).then_inc(wspT_done, 1)
            split_hi(g_ga.chunk0, 0)
            evac_unit(g_fquo.chunk1 - 1, evac_f(og_fm, ACT.Sigmoid))
            split_hi(g_ga.chunk0 + 1, 1)
            act.wait_ge(ya_done, NH)
            act.wait_ge(const_dve, 2)
            for h in range(NH):
                act.activation(b_fm[:, h, :], f_fm[:, h, :], ACT.Ln, bias=lb[:, h:h + 1],
                               scale=lb_not[:, h:h + 1]).then_inc(hg_log, 1)
            split_hi(g_ga.chunk0 + 2, 0)
            evac_unit(g_ga.chunk0 + 1, evac_f(ga_fm, ACT.Sigmoid))
            split_hi(g_ga.chunk0 + 3, 1)
            act.wait_ge(hg_cum, NH * (T // HC))
            act.activation(eb_fm[:, :, :], kend_fm[:, :, :], ACT.Exp).then_inc(hg_exp, 1)
            act.activation(b_fm[:, :, :], kend_fm[:, :, :], ACT.Exp, scale=-1.0).then_inc(hg_exp, 1)
            for t in range(NT):
                act.wait_ge(att_zero, 1)
                act.wait_ge(hg_att, 2 * t + 1)
                diag = mb[2 * (t % 2)][:, :].rearrange("p (h t) -> p h t", h=NH)
                act.activation(attT[0:HC, t, :, 0:HC], diag[0:HC, :, 0:HC], ACT.Copy).then_inc(hg_att_out, 1)
                act.activation(attT[HC:P, t, :, HC:P], diag[HC:P, :, HC:P], ACT.Copy).then_inc(hg_att_out, 1)
                act.wait_ge(hg_att, 2 * t + 2)
                low = mb[2 * (t % 2) + 1][:, :].rearrange("p (h t) -> p h t", h=NH)
                act.activation(attT[0:HC, t, :, HC:P], low[0:HC, :, HC:P], ACT.Copy).then_inc(hg_att_out, 1)
            split_hi(g_gb.chunk0, 0)
            evac_unit(g_ga.chunk1 - 1, lambda j: act.activation(ga_fm[:, 4 + j, :], gb[j][:, :], ACT.Sigmoid))
            split_hi(g_gb.chunk0 + 1, 1)
            for t in range(NT):
                act.wait_ge(kend_turned, t + 1)
                act.activation(kend_tm[:, t, :], mb[t][:, :], ACT.Copy).then_inc(kend_done, 1)
            split_hi(g_gb.chunk0 + 2, 0)
            evac_unit(g_gb.chunk0 + 1, evac_f(gb_fm, ACT.Sigmoid))
            split_hi(g_gb.chunk0 + 3, 1)
            split_hi(g_upa.chunk0, 0)
            evac_unit(g_gb.chunk1 - 1, lambda j: act.activation(gb_fm[:, 4 + j, :], gb[j][:, :], ACT.Sigmoid))
            act.wait_ge(ya_done, NH)
            for h in range(NH):
                act.activation(act_hi[:, h, :], u_fm[:, h, :], ACT.Copy).then_inc(y_hi, 1)
            for h in range(NH):
                act.wait_ge(hg_o, h + 1)
                act.activation(o_fm[:, h, :], mb[h][:, :], ACT.Copy)
                act.activation(sq_fm[:, h, :], mb[h][:, :], ACT.Square).then_inc(hg_sq, 1)
            act.wait_ge(hg_ss, 1)
            act.activation(rs_hg[:, :], mb[0][:, :], ACT.Sqrt, bias=eps_col[:, 0:1], scale=1.0 / P)\
                .then_inc(hg_sd, 1)
            split_hi(g_upa.chunk0 + 1, 1)
            split_hi(g_upb.chunk0, 0)
            for h in range(NH):
                act.wait_ge(yb_done, h + 1)
                act.activation(act_hi[:, 4 + h, :], o_fm[:, h, :], ACT.Copy).then_inc(y_hi, 1)
            split_hi(g_upb.chunk0 + 1, 1)
            for u in range(2):
                split_hi(g_out.chunk0 + u, u)
                act.wait_ge(pe_tiles, 4 * (g_upa if u == 0 else g_upb).chunk1)
                for k in range(4 * u, 4 * u + 4):
                    act.wait_ge(merged, k + 1)
                    act.activation(act_hi[:, k, :], ga_fm[:, k, :], ACT.Copy).then_inc(y_hi, 1)
            split_hi(g_out.chunk0 + 2, 0)
            split_hi(g_out.chunk0 + 3, 1)

            act.wait_ge(route_in, 32)
            act.activation(route_hi[:, :, :], route_f[:, :, :], ACT.Copy).then_inc(rw_hi, 1)
            norm(1, lambda t: rows_added(g_out, t))
            for h in range(2):
                act.wait_ge(logitT_done, h + 1)
                half = slice(h * T // 2, (h + 1) * T // 2)
                act.activation(logitT[:, half], gb[2 * h][0:ROUTED, half], ACT.Copy).then_inc(logitT_out, 1)
            def row_high(t):
                act.activation(xn_hi[:, t, :], xn_at[1][:, t, :], ACT.Copy).then_inc(xn_hi_done, 1)

            row_high(0)
            row_high(1)
            act.wait_ge(r_shift, 1)
            act.activation(r_exp[:, :, :], r_grp[:, :, :], ACT.Exp).then_inc(r_expd, 1)
            row_high(2)
            row_high(3)
            act.wait_ge(r_shift, 2)
            act.activation(r_d[:, :], r_top[1][:, :], ACT.Exp).then_inc(r_expd, 1)

            def experts_act(r):
                def rows(n):
                    for b in range(2):
                        act.wait_ge(rows_in, n * 2 + (b + 1))
                        act.activation(xg[:, b * 512:(b + 1) * 512], mb[b][:, :], ACT.Copy).then_inc(xg_out, 1)
                    for b in range(2):
                        act.wait_ge(rows_turned, n * 2 + (b + 1))
                        act.activation(xgT[:, 4 * b:4 * b + 4, :], mb[b][:, :].rearrange("p (k t) -> p k t", k=4),
                                       ACT.Copy).then_inc(rows_out, 1)

                def pair(i, last=False):
                    n = pair_number(i, r)
                    act.wait_ge(up_done, n * 4 + 2)
                    if not isinstance(n, int) or n:
                        act.wait_ge(gated_turned, n)
                    act.activation(gated[:, :], mb[2][:, :], ACT.Silu).then_inc(silu_done, 1)
                    if not last:
                        rows(n + 1)
                    for b in range(2):
                        act.wait_ge(down_done, n * 2 + (b + 1))
                        act.sem_inc(wait_carrier, 1)
                        act.activation(y_hi_sb[:, b * 512:(b + 1) * 512], gb[1 + b][:, :], ACT.Copy,
                                       scale=slot_gate[:, col(i)]).then_inc(y_hi_out, 1)

                rows(pair_number(0, r))
                act.wait_ge(valued, 1 if r is None else r + 1)
                pair(0)
                with act.Fori(1, PAIRS - 1) as i:
                    pair(i)
                pair(PAIRS - 1, last=True)

            experts_act(None)
            fullest = act.value_load(most[0:1, 0:1], min_val=0, max_val=T)
            with act.If(fullest > SLOTS):
                with act.Fori(1, ROUNDS) as r:
                    with act.If(fullest > r * SLOTS):
                        experts_act(r)
                        act.wait_ge(moe_added, r * (8 * PAIRS) + 8 * PAIRS)
                        act.sem_inc(wait_carrier, 1)

            split_hi(g_pg.chunk0, 0)
            norm(2, lambda t: act.wait_ge(moe_added, 8 * (PAIRS - 1) + 2 * (t + 1)),
                 mid=lambda: split_hi(g_pg.chunk0 + 1, 1))
            split_hi(g_pg.chunk0 + 2, 0)
            evac_unit(g_pg.chunk0 + 1, lambda j: act.activation(sg_tm[:, j, 0:512], gb[j][:, :], ACT.Sigmoid))
            split_hi(g_pg.chunk0 + 3, 1)
            for b in range(2):
                act.wait_ge(p_turned, b + 1)
                act.activation(pT_hi[:, b, :], mb[b][:, :], ACT.Copy).then_inc(p_hi, 1)
            split_hi(g_ple.chunk0, 0, g_ple.ktiles)
            evac_unit(g_pg.chunk1 - 1, lambda j: act.activation(sg_tm[:, j, 512:D], gb[j][:, :], ACT.Sigmoid))
            split_hi(g_ple.chunk0 + 1, 1, g_ple.ktiles)

            def end_of_block(t):
                rows_added(g_ple, t)
                act.wait_ge(x_ple, NT + t + 1)
                sum_squares(3, t)

            def next_rows(t):
                if t + 1 < NT:
                    end_of_block(t + 1)
                act.wait_ge(n_xn, rows_count(3, t))

            end_of_block(0)
            norm(4, next_rows, mid=lambda: split_hi(g_sv.chunk0, 0))
            split_hi(g_sv.chunk0 + 1, 1)
            act.wait_ge(low_in, 32)
            act.activation(low_hi[:, :, :], low_f[:, :, :], ACT.Copy).then_inc(low_split, 1)

            def unit(c, put, next_two=True):
                split_hi(c + 2, 0)
                evac_unit(c + 1, put)
                if next_two:
                    split_hi(c + 3, 1)

            unit(g_sv.chunk0, evac_f(sbv, ACT.Copy))
            act.wait_ge(low_z, 1)
            act.activation(lowT[:, :], mb[0][0:GR, :], ACT.Copy).then_inc(lowT_done, 1)
            unit(g_gv.chunk0, lambda j: act.activation(gv_tm[:, j, 0:512], gb[j][:, :], ACT.Copy))
            unit(g_gv.chunk0 + 2, lambda j: act.activation(gv_tm[:, j, 512:D], gb[j][:, :], ACT.Copy))
            for h in range(NH):
                act.wait_ge(la_z, h + 1)
                act.activation(la_tmp[:, h, :], mb[h][:, :], ACT.Abs, bias=gate_bias[:, h:h + 1]).then_inc(la_act, 1)
            act.wait_ge(la_act, NH)
            own.did(act.activation(la_tmp[:, :, :], la_tmp[:, :, :], ACT.Exp, scale=-1.0))
            own.settle()
            act.activation(la_tmp[:, :, :], la_tmp[:, :, :], ACT.Ln, bias=one_col[:, 0:1]).then_inc(la_act, 1)
            unit(g_qk.chunk0, evac_f(sbq, ACT.Copy))
            unit(g_qk.chunk0 + 2, evac_f(sbk, ACT.Copy), False)

            def gla_out(h, j):
                act.wait_ge(pe_tiles, h * 8 + (4 * (g_gla.chunk0 + 1) + j + 1))
                act.activation(at_tile(g_all, h, j), gb[j][:, :], ACT.Copy).then_inc(out_act, 1)

            def turn_end(h):
                for j in (2, 3):
                    gla_out(h, j)
                act.wait_ge(sb_o, h * 8 + 16)
                act.activation(sbq[:, ds(h, 1), :].rearrange("p o t -> p (o t)"), mb[3][:, :], ACT.Copy)\
                    .then_inc(sb_o_out, 1)

            def sb_turn(h, first):
                for n in range(2 * NT):
                    s, t = n % 2, n % 4
                    end = (t + 1) * P
                    act.wait_ge(sb_z, h * 8 + n + 1)
                    if n >= 2 or not first:
                        act.wait_ge(sb_turned, h * 8 + n - 1)
                    act.activation(sb_fail[s][:, 0:end], mb[s][:, 0:end], ACT.Sigmoid, scale=-SBD ** -0.5)\
                        .then_inc(sb_sig, 1)
                    act.activation(sb_w[s][:, 0:end], mb[s][:, 0:end], ACT.Sigmoid, scale=SBD ** -0.5)\
                        .then_inc(sb_sig, 1)
                    if n == 0 and not first:
                        turn_end(h - 1)
                    if n == 1:
                        split_hi(h * 2 + (g_gla.chunk0 + 1), 1)
                    if n == 5:
                        split_hi(h * 2 + (g_gla.chunk0 + 2), 0)
                    if n >= 6:
                        gla_out(h, n - 6)

            act.wait_ge(la_cum, NH * NT)
            sb_turn(0, True)
            with act.Fori(1, SBH // 2) as h:
                sb_turn(h, False)
            turn_end(SBH // 2 - 1)

            def gate_unit(u):
                for j in range(4):
                    n = 4 * u + j
                    act.wait_ge(pe_tiles, 4 * (g_gates.chunk0 + 2 * u + 1) + j + 1)
                    if n >= 2:
                        act.wait_ge(gates_stored[n % 2], 16 * (n // 2))
                    act.activation(gate_out[n % 2][:, :], gb[j][:, :], ACT.Sigmoid).then_inc(out_act, 1)

            for n in range(LEVELS):
                act.wait_ge(gl_dist, 2 * n + 2)
                act.activation(gl_e[:, :, :], gl_e[:, :, :], ACT.Exp, scale=1.0 / 16).then_inc(gl_exp, 1)
                if n == 0:
                    act.wait_ge(out_act, all_out(g_gla))
                    act.activation(gq_fm[:, :, :], gq_fm[:, :, :], ACT.Copy, scale=float(P) ** -0.5)\
                        .then_inc(gla_q, 1)
                if n and n % 2 == 0:
                    gate_unit(n // 2 - 1)
                split_hi(g_gates.chunk0 + n + 1, (n + 1) % 2)
            act.wait_ge(gl_edge, 1)
            act.activation(gl_e[:, :, :], la_sum[:, :, :], ACT.Exp, scale=1.0 / 16).then_inc(gl_edge_exp, 1)
            act.activation(gl_qk[:, :, :], gl_qk[:, :, :], ACT.Exp, scale=1.0 / 16).then_inc(gl_edge_exp, 1)
            act.activation(decay[:, :, 0:NT], la_sum[:, :, P - 1:T:P], ACT.Exp, scale=1.0 / 16)\
                .then_inc(gl_edge_exp, 1)
            split_hi(g_psb.chunk0, 0)
            gate_unit(3)
            split_hi(g_psb.chunk0 + 1, 1)
            for t in range(NT):
                act.wait_ge(gkend_turned, t + 1)
                act.activation(gkend_tm[:, t, :], mb[t][:, :], ACT.Copy).then_inc(gkend_done, 1)
            for h in range(NH):
                act.activation(act_hi[:, h, :], sbq[:, h, :], ACT.Copy).then_inc(y_hi, 1)
            act.activation(gout_fm[:, :, :], gout_fm[:, :, :], ACT.Silu).then_inc(gout_done, 1)
            for n in range(KT):
                h = n // 2
                act.wait_ge(gl_o, n + 1)
                act.activation(go[n], gla_bank(n)[:, :], ACT.Copy)
                if n >= 4:
                    act.wait_ge(gl_ss, h - 1)
                act.activation(gsq[h % 2][:, n % 2, :], gla_bank(n)[:, :], ACT.Square).then_inc(gl_sq, 1)
            act.wait_ge(gl_ss, NH)
            act.activation(rs_gla[:, :], mb[2][:, :], ACT.Sqrt, bias=eps_col[:, 0:1], scale=1.0 / DV)\
                .then_inc(gl_sd, 1)
            for u in range(2):
                if u:
                    split_hi(g_pgla.chunk0, 0)
                    split_hi(g_pgla.chunk0 + 1, 1)
                    act.wait_ge(pe_tiles, 4 * g_psb.chunk1)
                for k in range(4 * u, 4 * u + 4):
                    act.wait_ge(yg_done, k + 1)
                    act.activation(act_hi[:, (k + 4) % KT, :], go[k], ACT.Copy).then_inc(y_hi, 1)
            split_hi(g_pgla.chunk0 + 2, 0)
            split_hi(g_pgla.chunk0 + 3, 1)
            for u in range(2):
                for k in range(4 * u, 4 * u + 4):
                    act.wait_ge(mixed, k + 1)
                    act.activation(mix_hi[:, k, :], gs_fm[:, k, :], ACT.Copy).then_inc(y_hi, 1)
                if u == 0:
                    split_hi(g_out2.chunk0, 0)
                    split_hi(g_out2.chunk0 + 1, 1)
            split_hi(g_out2.chunk0 + 2, 0)
            split_hi(g_out2.chunk0 + 3, 1)

            split_hi(g_ff[0][0].chunk0, 0)
            norm(5, lambda t: rows_added(g_out2, t))

            def relu_unit(h, u, chunk):
                for j in range(4):
                    act.wait_ge(pe_tiles, chunk * 4 + j + 1)
                    seen = u * 4 + (j + 1) + (4 * up.units * h - 4)
                    if not (h == 0 and isinstance(u, int) and u == 0):
                        act.wait_ge(hid_sq, seen)
                    act.activation(relu_t[j][:, :], gb[j][:, :], ACT.Relu).then_inc(out_act, 1)
                for j in range(4):
                    act.wait_ge(out_act, (u * 4) + up.tile0 + 4 + j + 1)
                    if h:
                        act.wait_ge(pe_tiles, 4 * g_ff[h - 1][1].chunk1)
                    act.activation(at_tile(hid_hi, u, j), relu_t[j][:, :], ACT.Square).then_inc(hid_hi_done, 1)

            for h, (up, down) in enumerate(g_ff):
                if h:
                    split_hi(up.chunk0, 0)
                split_hi(up.chunk0 + 1, 1)
                split_hi(up.chunk0 + 2, 0)
                relu_unit(h, 0, up.chunk0 + 1)
                split_hi(up.chunk0 + 3, 1)
                with act.Fori(2, up.units) as u:
                    split_hi(u * 2 + up.chunk0, 0)
                    relu_unit(h, u - 1, u * 2 + (up.chunk0 - 1))
                    split_hi(u * 2 + up.chunk0 + 1, 1)
                split_hi(down.chunk0, 0)
                relu_unit(h, up.units - 1, up.chunk1 - 1)
                split_hi(down.chunk0 + 1, 1)
                with act.Fori(1, down.units * down.chunks // 2) as i:
                    for s in range(2):
                        split_hi(i * 2 + down.chunk0 + s, s)
            norm(6, lambda t: rows_added(g_ff[-1][1], t))

        @block.vector
        def _(dve):
            own = Chain(dve, dve_own)

            def split_lo(c, s, ktiles=4):
                dve.wait_ge(w_hi_done, c + 1)
                dve.tensor_tensor(w_lo[s][:, 0:ktiles, :], w_stage[s][:, 0:ktiles, :],
                                  w_hi[s][:, 0:ktiles, :].bitcast(F32), ALU.subtract).then_inc(w_lo_done, 1)

            def split_los(g):
                n = g.units * g.chunks // 2
                if n == 1:
                    for s in range(2):
                        split_lo(g.chunk0 + s, s, g.ktiles)
                    return
                with dve.Fori(0, n) as i:
                    for s in range(2):
                        split_lo(i * 2 + g.chunk0 + s, s, g.ktiles)

            def rest(dst, src, hi):
                return dve.tensor_tensor(dst, src, hi.bitcast(F32), ALU.subtract)

            own_gain = {2: (gain_2, gain_2_in), 4: (gain_4, gain_4_in)}

            def scale_rows(n, t):
                gains, gains_in = own_gain.get(n, (gain, gain_in))
                if t == 0:
                    dve.wait_ge(gains_in, 16 * (1 if n in own_gain else n + 1 - sum(m < n for m in own_gain)))
                dve.wait_ge(n_sd, rows_count(n, t))
                own.did(dve.reciprocal(rstd[:, t:t + 1], rstd[:, t:t + 1]))
                own.settle()
                dst = x if n == 3 else xn_at[n]
                dve.scalar_tensor_tensor(dst[:, t, :], x[:, t, :], rstd[:, t:t + 1], gains[:, :],
                                         ALU.mult, ALU.mult).then_inc(n_xn, 1)

            def norm(n, before=lambda t: None, mid=lambda: None):
                def scale(t):
                    if t + 1 < NT:
                        before(t + 1)
                    scale_rows(n, t)

                def low(t):
                    if n in ROWS_ONLY:
                        return
                    for b in range(2):
                        q = 2 * t + b
                        dve.wait_ge(n_hi, turned_before(n) + q + 1)
                        rest(act_lo[:, 4 * b:4 * b + 4, t * P:(t + 1) * P],
                             mb[q % 4][:, :].rearrange("p (k t) -> p k t", k=4),
                             act_hi[:, 4 * b:4 * b + 4, t * P:(t + 1) * P]).then_inc(n_lo, 1)

                before(0)
                scale(0)
                for t in range(1, NT):
                    scale(t)
                    if t == 1:
                        mid()
                    low(t - 1)
                low(NT - 1)

            def evac_unit(last_chunk, put):
                for j in range(4):
                    dve.wait_ge(pe_tiles, last_chunk * 4 + j + 1)
                    put(j)

            def rows_of(g):
                def put(t):
                    dve.wait_ge(pe_tiles, (g.chunk1 - 1) * 4 + t + 1)
                    add_tile(g.units - 1, t).then_inc(out_dve, 1)
                return put

            dve.wait_ge(const_pool, 5)
            dve.wait_ge(pool_own, 5)
            dve.tensor_tensor(level_mask[:, 2, :], level_mask[:, 0, :], level_mask[:, 1, :],
                              ALU.bitwise_xor).then_inc(const_dve, 1)

            norm(0, mid=lambda: split_lo(0, 0))
            dve.wait_ge(const_pool, 7)
            own.did(dve.tensor_copy(order_xor[:, :], level_mask[:, 2, :]))
            for n in range(LEVELS):
                own.settle()
                own.did(dve.tensor_scalar(level_mask[:, n, :], order_xor[:, :], n, None, ALU.arith_shift_right))
            own.settle()
            own.did(dve.tensor_scalar(level_mask[:, :, :], level_mask[:, :, :], 1, None, ALU.is_equal))
            split_lo(1, 1)
            dve.wait_ge(params_in, 16 * 8)
            dve.tensor_tensor(lb_neg[:, :], lb_par[:, 0, :], lb_par[:, 1, :], ALU.subtract).then_inc(lb_diff, 1)
            dve.wait_ge(lb_sig, 1)
            own.did(dve.tensor_scalar(lb_neg[:, :], lb[:, :], -1.0, None, ALU.add))
            dve.tensor_scalar(lb_not[:, :], lb[:, :], -1.0, 1.0, ALU.mult, ALU.add).then_inc(const_dve, 1)
            split_lo(2, 0)
            for t in range(NT):
                dve.wait_ge(out_act, 4 + t + 1)
                own.did(dve.bn_stats(ln_stats[:, t, :], v_tm[:, t, :]))
            for t in range(NT):
                own.settle()
                if t < NT - 1:
                    own.did(dve.bn_aggr(ln_mv[:, t, :], ln_stats[:, t, :]))
                else:
                    dve.bn_aggr(ln_mv[:, t, :], ln_stats[:, t, :]).then_inc(ln_var, 1)
            split_lo(3, 1)
            dve.wait_ge(ln_sd, 1)
            own.did(dve.reciprocal(ln_rstd[:, :], ln_rstd[:, :]))
            own.settle()
            for t in range(NT):
                own.did(dve.tensor_scalar(v_tm[:, t, :], v_tm[:, t, :], ln_mv[:, t, 0:1], ln_rstd[:, t:t + 1],
                                          ALU.subtract, ALU.mult))
                own.settle()
                own.did(dve.tensor_tensor(v_tm[:, t, :], v_tm[:, t, :], ln_g[:, :], ALU.mult))
                own.settle()
                dve.tensor_tensor(v_tm[:, t, :], v_tm[:, t, :], ln_b[:, :], ALU.add).then_inc(v_normed, 1)
            split_los(g_fquo)
            split_lo(g_ga.chunk0, 0)
            dve.wait_ge(out_act, g_fquo.tile0 + 4 + 12)
            for j in range(NH):
                dve.wait_ge(spatial_done, j + 1)
                dve.tensor_tensor(u_fm[:, j, :], u_fm[:, j, :], mb[j][:, :], ALU.mult).then_inc(ya_done, 1)
            split_lo(g_ga.chunk0 + 1, 1)
            for h in range(NH):
                dve.wait_ge(hg_log, h + 1)
                for c in range(T // HC):
                    dve.tensor_tensor_scan(kend_fm[:, h, c * HC:(c + 1) * HC], ones[:, 0:HC],
                                           b_fm[:, h, c * HC:(c + 1) * HC], 0.0, ALU.mult, ALU.add)\
                        .then_inc(hg_cum, 1)
            split_lo(g_ga.chunk0 + 2, 0)
            for h in range(NH):
                own.did(dve.tensor_scalar(f_fm[:, h, :], f_fm[:, h, :], lb_neg[:, h:h + 1], lb_not[:, h:h + 1],
                                          ALU.mult, ALU.add))
            split_lo(g_ga.chunk0 + 3, 1)
            dve.wait_ge(hg_exp, 2)
            own.settle()
            dve.tensor_tensor(q_fm[:, :, :], q_fm[:, :, :], eb_fm[:, :, :], ALU.mult).then_inc(hg_ready, 1)
            dve.tensor_tensor(f_fm[:, :, :], f_fm[:, :, :], b_fm[:, :, :], ALU.mult).then_inc(hg_ready, 1)
            own.did(dve.tensor_copy(decay[:, :, :], eb_fm[:, :, HC - 1:T:HC]))
            dve.wait_ge(hg_ready, 2)
            own.settle()
            last = decay[:, :, :].rearrange("p h (c o) -> p (h c) o", o=1).broadcast_to([P, NH * (T // HC), HC])
            dve.tensor_tensor(kend_fm[:, :, :].rearrange("p h (c t) -> p (h c) t", t=HC),
                              f_fm[:, :, :].rearrange("p h (c t) -> p (h c) t", t=HC), last,
                              ALU.mult).then_inc(hg_ready, 1)
            dve.wait_ge(hg_att, 2 * NT)
            dve.wait_ge(hg_ready, 3)
            q2 = q_fm[:, :, :].rearrange("p h (c t) -> p (h c) t", t=HC)
            k2 = kend_fm[:, :, :].rearrange("p h (c t) -> p (h c) t", t=HC)
            dl = decay[:, :, :].rearrange("p h (c o) -> p (h c) o", o=1)
            half = [P, NH * NT, HC]
            dve.tensor_tensor(k2[:, 0::2, :], k2[:, 0::2, :], dl[:, 1::2, :].broadcast_to(half), ALU.mult)\
                .then_inc(hg_scaled, 1)
            dve.tensor_tensor(q2[:, 1::2, :], q2[:, 1::2, :], dl[:, 0::2, :].broadcast_to(half), ALU.mult)\
                .then_inc(hg_scaled, 1)
            own.did(dve.tensor_tensor(ln_stats[:, :, 0:NH], decay[:, :, 0::2].rearrange("p h c -> p c h"),
                                      decay[:, :, 1::2].rearrange("p h c -> p c h"), ALU.mult))
            own.settle()
            for u in range(2):
                for s in range(2):
                    split_lo(g_gb.chunk0 + 2 * u + s, s)
            split_lo(g_upa.chunk0, 0)
            for t in range(NT - 1):
                for h in range(NH):
                    dve.wait_ge(hg_ds, t + 1)
                    ds_h = mb[t][:, h * P:(h + 1) * P]
                    if t == 0:
                        dve.tensor_copy(s_hg[:, 0, h, :], ds_h).then_inc(hg_state, 1)
                    else:
                        dve.wait_ge(hg_state, NH * (t - 1) + h + 1)
                        dve.scalar_tensor_tensor(s_hg[:, t, h, :], s_hg[:, t - 1, h, :], ln_stats[:, t, h:h + 1],
                                                 ds_h, ALU.mult, ALU.add).then_inc(hg_state, 1)
            for h in range(NH):
                dve.wait_ge(y_hi, h + 1)
                rest(act_lo[:, h, :], u_fm[:, h, :], act_hi[:, h, :]).then_inc(y_lo, 1)
            def gate_tile(dst, k, j):
                return dve.tensor_tensor(dst[:, k, :], dst[:, k, :], gb[j][:, :], ALU.mult).then_inc(out_dve, 1)

            dve.wait_ge(hg_sd, 1)
            dve.reciprocal(rs_hg[:, :], rs_hg[:, :]).then_inc(hg_rs, 1)
            split_lo(g_upa.chunk0 + 1, 1)
            evac_unit(g_upa.chunk0, lambda j: gate_tile(ga_fm, j, j))
            for h in range(NH):
                dve.wait_ge(hg_rsb, h + 1)
                own.did(dve.scalar_tensor_tensor(o_fm[:, h, :], o_fm[:, h, :], hg_gain[:, h:h + 1], mb[h][:, :],
                                                 ALU.mult, ALU.mult))
                own.settle()
                dve.tensor_tensor(o_fm[:, h, :], o_fm[:, h, :], og_fm[:, h, :], ALU.mult).then_inc(yb_done, 1)
            split_lo(g_upb.chunk0, 0)
            for h in range(NH):
                dve.wait_ge(y_hi, NH + h + 1)
                rest(act_lo[:, 4 + h, :], o_fm[:, h, :], act_hi[:, 4 + h, :]).then_inc(y_lo, 1)
            evac_unit(g_upa.chunk0 + 1, lambda j: gate_tile(ga_fm, 4 + j, j))
            split_lo(g_upb.chunk0 + 1, 1)
            for u in range(2):
                def both(j, u=u):
                    gate_tile(gb_fm, 4 * u + j, j)
                    dve.wait_ge(out_dve, g_upb.tile0 + 4 + 4 * u + j + 1)
                    dve.tensor_tensor(ga_fm[:, 4 * u + j, :], ga_fm[:, 4 * u + j, :], gb_fm[:, 4 * u + j, :],
                                      ALU.add).then_inc(merged, 1)

                evac_unit(g_upb.chunk0 + u, both)
                split_lo(g_out.chunk0 + u, u)
                for k in range(4 * u, 4 * u + 4):
                    dve.wait_ge(y_hi, AT_MERGED + k + 1)
                    rest(act_lo[:, k, :], ga_fm[:, k, :], act_hi[:, k, :]).then_inc(y_lo, 1)

            def add_tile(u, j, width=512):
                xt = x[:, j, u * 512:(u + 1) * 512]
                return dve.tensor_tensor(xt, xt, gb[j][:, :], ALU.add)

            split_lo(g_out.chunk0 + 2, 0)
            evac_unit(g_out.chunk0 + 1, lambda j: add_tile(0, j).then_inc(out_dve, 1))
            split_lo(g_out.chunk0 + 3, 1)

            dve.wait_ge(rw_hi, 1)
            rest(route_lo[:, :, :], route_f[:, :, :], route_hi[:, :, :]).then_inc(rw_lo, 1)
            norm(1, rows_of(g_out))
            dve.wait_ge(logits_done, 1)
            own.did(dve.tensor_copy(logits[:, :, :], gb[1][:, 0:NT * ROUTED].rearrange("p (t e) -> p t e", t=NT)))
            own.settle()
            dve.wait_ge(r_pool, 1)
            grp = logits[:, :, 0:NG]

            def per_token(v, n):
                return v.rearrange("p (t o) -> p t o", o=1).broadcast_to([P, NT, n])

            def did(ins):
                own.did(ins)
                own.settle()

            def first_of_max(pick, values, best, n, spare, mark=ALU.is_equal):
                index = iota_row[:, 0:n].rearrange("p (o e) -> p o e", o=1).broadcast_to([P, NT, n])
                did(dve.tensor_tensor(pick, values, per_token(best, n), ALU.is_equal))
                did(dve.scalar_tensor_tensor(spare, pick, -64.0, index, ALU.mult, ALU.add))
                did(dve.tensor_reduce(r_first[:, :], spare, AX.X, ALU.min))
                did(dve.tensor_tensor(pick, spare, per_token(r_first[:, :], n), mark))

            did(dve.tensor_reduce(r_max[:, :], grp, AX.X, ALU.max))
            dve.tensor_tensor(r_grp[:, :, :], grp, per_token(r_max[:, :], NG), ALU.subtract).then_inc(r_shift, 1)
            first_of_max(r_gpick[:, :, :], grp, r_max[:, :], NG, r_bias[:, :, :], ALU.not_equal)
            by_group = [P, NT, NG, EG]
            did(dve.scalar_tensor_tensor(r_sel[:, :, :].rearrange("p t (g e) -> p t g e", g=NG),
                                         r_gpick[:, :, :].rearrange("p t (g o) -> p t g o", o=1).broadcast_to(by_group),
                                         -HUGE, logits[:, :, NG:ROUTED].rearrange("p t (g e) -> p t g e", g=NG),
                                         ALU.mult, ALU.add))
            for n in range(2):
                did(dve.tensor_reduce(r_top[n][:, :], r_sel[:, :, :], AX.X, ALU.max))
                first_of_max(r_pick[n], r_sel[:, :, :], r_top[n][:, :], NE, r_tmp[:, :, :])
                if n == 0:
                    did(dve.scalar_tensor_tensor(r_sel[:, :, :], r_pick[0], -HUGE, r_sel[:, :, :],
                                                 ALU.mult, ALU.add))
            dve.tensor_tensor(r_any[:, :, :], r_pick[0], r_pick[1], ALU.add).then_inc(picked, 1)
            dve.tensor_tensor(r_top[1][:, :], r_top[1][:, :], r_top[0][:, :], ALU.subtract).then_inc(r_shift, 1)
            dve.wait_ge(ranked, 1)
            ranks = mb[2][:, 0:NT * NE].rearrange("p (t e) -> p t e", t=NT)
            own.did(dve.tensor_copy(r_hi[:, :, :], ranks))
            own.did(dve.tensor_tensor(r_rank[:, :, :], ranks, first_place[:, :].rearrange("p (o e) -> p o e", o=1)
                                      .broadcast_to([P, NT, NE]), ALU.add))
            own.settle()
            did(dve.tensor_scalar(r_hi[:, :, :], r_hi[:, :, :], SLOTS.bit_length() - 1, None, ALU.arith_shift_right))
            did(dve.scalar_tensor_tensor(r_rank[:, :, :], r_hi[:, :, :], float(FAR - SLOTS), r_rank[:, :, :],
                                         ALU.mult, ALU.add))
            for n in range(2):
                own.did(dve.tensor_tensor(r_tmps[:, n * NT:(n + 1) * NT, :], r_pick[n], r_rank[:, :, :], ALU.mult))
            own.settle()

            def over_pair(dst):
                did(dve.tensor_reduce(dst[:, :, :].rearrange("p n e -> p (n e)"),
                                      r_tmps[:, :, :].rearrange("p n (e q) -> p (n e) q", q=2), AX.X, ALU.add))

            over_pair(place_in)

            def gate_columns():
                dve.wait_ge(r_expd, 2)
                did(dve.tensor_reduce(r_pg[:, :], r_exp[:, :, :], AX.X, ALU.add))
                did(dve.reciprocal(r_pg[:, :], r_pg[:, :]))
                did(dve.tensor_scalar(choice_gates[:, 0:NT], r_d[:, :], 1.0, None, ALU.add))
                did(dve.reciprocal(choice_gates[:, 0:NT], choice_gates[:, 0:NT]))
                did(dve.tensor_tensor(choice_gates[:, 0:NT], choice_gates[:, 0:NT], r_pg[:, :], ALU.mult))
                did(dve.tensor_tensor(choice_gates[:, NT:2 * NT], choice_gates[:, 0:NT], r_d[:, :], ALU.mult))
                did(dve.tensor_tensor(r_tmps[:, :, :], r_picks[:, :, :],
                                      choice_gates[:, :].rearrange("p (n o) -> p n o", o=1)
                                      .broadcast_to([P, 2 * NT, NE]), ALU.mult))
                over_pair(pair_gate)
                did(dve.tensor_reduce(r_place[:, :], place_in[:, :, :], AX.X, ALU.add))
                dve.wait_ge(ranked, 2)
                did(dve.tensor_reduce(r_max[:, 0:1], mb[3][:, 0:NE], AX.X, ALU.max))
                did(dve.tensor_copy(most[:, :], r_max[:, 0:1]))
                dve.sem_inc(routed, 1)

            def make_sel(i, n):
                def place(c):
                    return place_in[:, c, col(i)]

                if not isinstance(n, int) or n:
                    dve.wait_ge(sel_turned, n)
                for t in range(NT):
                    dve.tensor_scalar(sel[:, t, :], iota_place[:, :], place(t), None, ALU.is_equal).then_inc(sel_made, 1)
                dve.wait_ge(sel_made, n * 8 + 4)
                for t in range(NT):
                    dve.scalar_tensor_tensor(sel[:, t, :], iota_place[:, :], place(NT + t), sel[:, t, :].bitcast(F32),
                                             ALU.is_equal, ALU.add).then_inc(sel_made, 1)

            def add_spread(n, u, bank):
                t, half = u // 2, u % 2
                dve.wait_ge(spread_done, n * 8 + (u + 1))
                xt = x[:, t, half * 512:(half + 1) * 512]
                dve.tensor_tensor(xt, xt, bank[:, :], ALU.add).then_inc(moe_added, 1)

            def experts_dve(r):
                if r is not None:
                    for places in (r_place[:, :], place_in[:, :, :]):
                        dve.tensor_scalar(places, places, -float(FAR), None, ALU.add).then_inc(next_round, 1)
                    dve.wait_ge(next_round, r * 2)
                make_sel(0, pair_number(0, r))
                if r is None:
                    gate_columns()
                for n in range(2 * NT):
                    dve.tensor_scalar(place_1h[:, n, :], iota_place[:, :], r_place[:, n:n + 1], None, ALU.is_equal)\
                        .then_inc(placed, 1)
                dve.wait_ge(tabled, 1 if r is None else r + 1)
                dve.tensor_copy(slot_gate[:, :], gb[1][:, 0:PAIRS]).then_inc(valued, 1)

                def pair(i, first=False, last=False):
                    n = pair_number(i, r)
                    if not last:
                        make_sel(i + 1, n + 1)
                    if not first:
                        if not isinstance(n, int) or n > 1:
                            dve.wait_ge(moe_added, n * 8 - 8)
                        for u in range(2 * NT):
                            add_spread(n - 1, u, mb[u % 2])
                    dve.wait_ge(sel_turned, n + 1)
                    dve.tensor_copy(selT[:, :], gb[3][:, :]).then_inc(selT_out, 1)
                    dve.wait_ge(silu_done, n + 1)
                    dve.wait_ge(up_done, n * 4 + 4)
                    dve.tensor_tensor(gated[:, :], gated[:, :], mb[3][:, :], ALU.mult).then_inc(gated_done, 1)
                    dve.wait_ge(gated_turned, n + 1)
                    dve.tensor_copy(gatedT[:, :, :], gb[0][:, :].rearrange("p (k t) -> p k t", k=4))\
                        .then_inc(gatedT_out, 1)
                    for b in range(2):
                        dve.wait_ge(y_hi_out, n * 2 + (b + 1))
                        half = slice(b * 512, (b + 1) * 512)
                        dve.scalar_tensor_tensor(y_lo_sb[:, half], gb[1 + b][:, :], slot_gate[:, col(i)],
                                                 y_hi_sb[:, half].bitcast(F32), ALU.mult, ALU.subtract)\
                            .then_inc(y_lo_out, 1)

                pair(0, first=True)
                with dve.Fori(1, PAIRS - 1) as i:
                    pair(i)
                pair(PAIRS - 1, last=True)
                n = pair_number(PAIRS - 1, r)
                dve.wait_ge(moe_added, n * 8)
                for u in range(2 * NT):
                    add_spread(n, u, gb[u % 4])

            experts_dve(None)
            fullest = dve.value_load(most[0:1, 0:1], min_val=0, max_val=T)
            with dve.If(fullest > SLOTS):
                with dve.Fori(1, ROUNDS) as r:
                    with dve.If(fullest > r * SLOTS):
                        dve.wait_ge(moe_added, r * (8 * PAIRS))
                        experts_dve(r)
            norm(2)
            dve.wait_ge(w_loaded[1], ((g_pg.chunk0 + 3) // 2 + 1) * 16)
            split_lo(g_pg.chunk0 + 2, 0)
            split_lo(g_pg.chunk0 + 3, 1)
            for b in range(2):
                dve.wait_ge(p_hi, b + 1)
                rest(pT_lo[:, b, :], mb[b][:, :], pT_hi[:, b, :]).then_inc(p_lo, 1)
            split_los(g_ple)
            dve.wait_ge(out_act, all_out(g_pg))

            def embed(u, j):
                dve.wait_ge(pe_tiles, 4 * (g_ple.chunk0 + u) + j + 1)
                if u or j >= 2:
                    dve.wait_ge(x_ple, 4 * u + j - 1)
                dve.tensor_tensor(ple_t[j % 2][:, :], gb[j][:, :], sg_tm[:, j, u * 512:(u + 1) * 512], ALU.mult)\
                    .then_inc(out_dve, 1)
                dve.wait_ge(out_dve, g_ple.tile0 + 4 + 4 * u + j + 1)
                xt = x[:, j, u * 512:(u + 1) * 512]
                dve.tensor_tensor(xt, xt, ple_t[j % 2][:, :], ALU.add).then_inc(x_ple, 1)

            for j in range(NT):
                embed(0, j)

            def end_of_block(t):
                if t + 1 < NT:
                    embed(1, t + 1)
                scale_rows(3, t)

            embed(1, 0)
            norm(4, end_of_block, mid=lambda: split_lo(g_sv.chunk0, 0))
            split_lo(g_sv.chunk0 + 1, 1)
            dve.wait_ge(low_split, 1)
            rest(low_lo[:, :, :], low_f[:, :, :], low_hi[:, :, :]).then_inc(low_split, 1)
            for c in range(6):
                split_lo(g_gv.chunk0 + c, c % 2)
            for h in range(NH):
                dve.wait_ge(la_act, h + 1)
                own.did(dve.tensor_scalar(la_fm[:, h, :], mb[h][:, :], gate_bias[:, h:h + 1], 0.0, ALU.add, ALU.min))
            own.settle()
            dve.wait_ge(la_act, NH + 1)
            own.did(dve.tensor_tensor(la_fm[:, :, :], la_fm[:, :, :], la_tmp[:, :, :], ALU.subtract))
            own.settle()
            for h in range(NH):
                for t in range(NT):
                    dve.tensor_tensor_scan(la_sum[:, h, t * P:(t + 1) * P], ones[:, 0:P],
                                           la_fm[:, h, t * P:(t + 1) * P], 0.0, ALU.mult, ALU.add)\
                        .then_inc(la_cum, 1)
            split_lo(g_qk.chunk0 + 2, 0)
            split_lo(g_qk.chunk0 + 3, 1)
            def copy_head(h, first):
                rows = slice(0, SBD) if first else slice(SBD, 2 * SBD)
                for staged, whole in ((sb_q, sbq),) if first else ((sb_q, sbq), (sb_k, sbk)):
                    dve.tensor_copy(staged[rows, :], whole[rows, col(h), :].rearrange("p o t -> p (o t)"))\
                        .then_inc(sb_first_in if first else sb_second_in, 1)

            dve.wait_ge(out_act, all_out(g_qk))
            copy_head(0, True)
            copy_head(0, False)
            split_lo(g_gla.chunk0, 0)
            dve.wait_ge(sb_ones, 2)

            def sb_turn(h, last):
                for n in range(2 * NT):
                    s, t = n % 2, n % 4
                    end = (t + 1) * P
                    dve.wait_ge(sb_past, h * 16 + 2 * n + 2)
                    dve.tensor_tensor_scan(sb_later[s][:, end - 2::-1], sb_fail[s][:, end - 1:0:-1],
                                           ones[:, 0:end - 1], 1.0, ALU.mult, ALU.mult).then_inc(sb_weight, 1)
                    dve.wait_ge(sb_weight, h * 16 + 2 * n + 1)
                    dve.tensor_tensor(sb_w[s][:, 0:end], sb_w[s][:, 0:end], sb_later[s][:, 0:end], ALU.mult)\
                        .then_inc(sb_weight, 1)
                    dve.wait_ge(sb_turned, h * 8 + n + 1)
                    dve.tensor_copy(sb_wT[:, 0:t + 1, :],
                                    mb[2][:, 0:(t + 1) * P].rearrange("p (k t) -> p k t", t=P)).then_inc(sb_wT_done, 1)
                    if n == 1:
                        split_lo(h * 2 + (g_gla.chunk0 + 1), 1)
                    if n == 5:
                        split_lo(h * 2 + (g_gla.chunk0 + 2), 0)
                    if n in (NT, 2 * NT - 1) and not last:
                        copy_head(h + 1, n == NT)

            with dve.Fori(0, SBH // 2 - 1) as h:
                sb_turn(h, False)
            sb_turn(SBH // 2 - 1, True)
            dve.wait_ge(la_cum, NH * NT)
            dve.wait_ge(sb_o, 8 * (SBH // 2) + 8)

            def copy_scores(n):
                for t in range(NT):
                    dve.wait_ge(gl_mm, NT * n + t + 1)
                    mask = (level_mask[:, n, :] if n < LEVELS else ident[:, :].bitcast(I32))
                    dve.copy_predicated(g_att[:, t, :, :],
                                        mask.rearrange("p (o t) -> p o t", o=1).broadcast_to([P, NH, P]),
                                        mb[t][:, :].rearrange("p (h t) -> p h t", h=NH)).then_inc(gl_copied, 1)

            def halves(a, m):
                v = a[:, :, :].rearrange("p h (c t) -> p (h c) t", t=2 * m)
                return v[:, :, 0:m], v[:, :, m:2 * m], v[:, :, m - 1:m].broadcast_to([P, NH * T // (2 * m), m])

            def distances(n):
                b0, b1, mid = halves(la_sum, 1 << n)
                e0, e1, _ = halves(gl_e, 1 << n)
                dve.tensor_tensor(e0, mid, b0, ALU.subtract).then_inc(gl_dist, 1)
                dve.tensor_tensor(e1, b1, mid, ALU.subtract).then_inc(gl_dist, 1)

            distances(0)
            dve.wait_ge(out_act, all_out(g_gla))
            dve.wait_ge(g_att_zero, 1)
            for n in range(LEVELS):
                (e0, e1, _), (k0, _, _), (_, q1, _), (qk0, qk1, _) = (
                    halves(a, 1 << n) for a in (gl_e, gk_fm, gq_fm, gl_qk))
                dve.wait_ge(gl_exp, n + 1)
                if n:
                    dve.wait_ge(gl_mm, NT * n)
                dve.tensor_tensor(qk0, e0, k0, ALU.mult).then_inc(gl_prod, 1)
                dve.wait_ge(gla_q, 1)
                dve.tensor_tensor(qk1, e1, q1, ALU.mult).then_inc(gl_prod, 1)
                if n < LEVELS - 1:
                    dve.wait_ge(gl_prod, 2 * n + 2)
                    distances(n + 1)
                copy_scores(n)
                split_lo(g_gates.chunk0 + n + 1, (n + 1) % 2)
            by_tile = "p h (c t) -> p (h c) t"
            sums = la_sum[:, :, :].rearrange(by_tile, t=P)
            dve.wait_ge(gl_prod, 2 * LEVELS)
            dve.tensor_tensor(gl_qk[:, :, :].rearrange(by_tile, t=P), sums[:, :, P - 1:P].broadcast_to([P, NH * NT, P]),
                              sums, ALU.subtract).then_inc(gl_edge, 1)
            copy_scores(LEVELS)
            dve.wait_ge(gl_edge_exp, 3)
            dve.tensor_tensor(gk_fm[:, :, :], gk_fm[:, :, :], gl_qk[:, :, :], ALU.mult).then_inc(gl_scaled, 1)
            dve.tensor_tensor(gq_fm[:, :, :], gq_fm[:, :, :], gl_e[:, :, :], ALU.mult).then_inc(gl_scaled, 1)
            split_lo(g_psb.chunk0, 0)
            split_lo(g_psb.chunk0 + 1, 1)
            for t in range(NT - 1):
                for h in range(NH):
                    dve.wait_ge(gl_ds, 2 * t + h // 2 + 1)
                    ds_h = mb[2 * (t % 2) + h // 2][:, (h % 2) * DV:(h % 2 + 1) * DV]
                    if t == 0:
                        dve.tensor_copy(s_gla[0][:, h, :], ds_h).then_inc(gl_state, 1)
                    else:
                        dve.wait_ge(gl_state, NH * (t - 1) + h + 1)
                        dve.scalar_tensor_tensor(s_gla[t][:, h, :], s_gla[t - 1][:, h, :], decay[:, h, t:t + 1],
                                                 ds_h, ALU.mult, ALU.add).then_inc(gl_state, 1)
            for h in range(NH):
                dve.wait_ge(y_hi, AT_YO + h + 1)
                rest(act_lo[:, h, :], sbq[:, h, :], act_hi[:, h, :]).then_inc(y_lo, 1)
            dve.wait_ge(gl_sd, 1)
            dve.reciprocal(rs_gla[:, :], rs_gla[:, :]).then_inc(gl_rs, 1)
            dve.wait_ge(sb_gate_in, 16)
            dve.wait_ge(gout_done, 1)
            def attention_out(u, tiles):
                for j in tiles:
                    dve.wait_ge(pe_tiles, (g_psb.chunk0 + u) * 4 + j + 1)
                    gate_tile(gs_fm, 4 * u + j, j)

            def gained(k):
                dve.wait_ge(gl_rsb, k // 2 + 1)
                own.did(dve.scalar_tensor_tensor(go[k], go[k], gla_gain[:, k % 2:k % 2 + 1], mb[k // 2][:, :],
                                                 ALU.mult, ALU.mult))
                own.settle()
                dve.tensor_tensor(go[k], go[k], gout_fm[:, k, :], ALU.mult).then_inc(yg_done, 1)

            def gla_low(k):
                dve.wait_ge(y_hi, AT_YG + k + 1)
                rest(act_lo[:, (k + 4) % KT, :], go[k], act_hi[:, (k + 4) % KT, :]).then_inc(y_lo, 1)

            attention_out(0, (0, 1))
            for k in range(6):
                gained(k)
            attention_out(0, (2, 3))
            split_lo(g_pgla.chunk0, 0)
            for k in range(4):
                gla_low(k)
            attention_out(1, range(4))
            for k in (6, 7):
                gained(k)
            split_lo(g_pgla.chunk0 + 1, 1)
            for k in range(4, 8):
                gla_low(k)
            split_lo(g_pgla.chunk0 + 2, 0)
            dve.wait_ge(gla_gate_in, 16)
            for u in range(2):
                def mix(j, u=u):
                    gate_tile(gg_fm, 4 * u + j, j)
                    dve.wait_ge(out_dve, g_pgla.tile0 + 4 + 4 * u + j + 1)
                    dve.tensor_tensor(gs_fm[:, 4 * u + j, :], gs_fm[:, 4 * u + j, :], gg_fm[:, 4 * u + j, :],
                                      ALU.add).then_inc(mixed, 1)

                evac_unit(g_pgla.chunk0 + 2 * u + 1, mix)
                if u == 0:
                    split_lo(g_pgla.chunk0 + 3, 1)
                else:
                    split_lo(g_out2.chunk0 + 1, 1)
                for k in range(4 * u, 4 * u + 4):
                    dve.wait_ge(y_hi, AT_MIX + k + 1)
                    rest(mix_lo[:, k, :], gs_fm[:, k, :], mix_hi[:, k, :]).then_inc(y_lo, 1)
                if u == 0:
                    split_lo(g_out2.chunk0, 0)
            split_lo(g_out2.chunk0 + 2, 0)
            evac_unit(g_out2.chunk0 + 1, lambda j: add_tile(0, j).then_inc(out_dve, 1))
            split_lo(g_out2.chunk0 + 3, 1)
            split_lo(g_ff[0][0].chunk0, 0)

            norm(5, rows_of(g_out2))

            def hidden_unit(h, u):
                for j in range(4):
                    seen = u * 4 + (4 * up.units * h + j + 1)
                    dve.wait_ge(out_act, u * 4 + (up.tile0 + 4 + j + 1))
                    dve.tensor_tensor(relu_sq[j][:, :], relu_t[j][:, :], relu_t[j][:, :], ALU.mult)\
                        .then_inc(hid_sq, 1)
                for j in range(4):
                    seen = u * 4 + (4 * up.units * h + j + 1)
                    dve.wait_ge(hid_hi_done, seen)
                    dve.wait_ge(hid_sq, seen)
                    dst = [hidden[:, ds(u * 4 + j, 1), :].rearrange("p o t -> p (o t)") for hidden in (hid_lo, hid_hi)]
                    rest(dst[0], relu_sq[j][:, :], dst[1]).then_inc(hid_lo_done, 1)

            for h, (up, down) in enumerate(g_ff):
                split_lo(up.chunk0 + 1, 1)
                with dve.Fori(1, up.units) as u:
                    split_lo(u * 2 + up.chunk0, 0)
                    hidden_unit(h, u - 1)
                    split_lo(u * 2 + up.chunk0 + 1, 1)
                split_lo(down.chunk0, 0)
                hidden_unit(h, up.units - 1)
                split_lo(down.chunk0 + 1, 1)
                for u in range(down.units):
                    for c in range(2 if u == 0 else 1, down.chunks):
                        split_lo(down.chunk0 + u * down.chunks + c, c % 2)
                    if u + 1 < down.units:
                        split_lo(down.chunk0 + (u + 1) * down.chunks, 0)
                    elif h + 1 < HALVES:
                        split_lo(g_ff[h + 1][0].chunk0, 0)
                    if h + 1 < HALVES or u + 1 < down.units:
                        evac_unit(down.chunk0 + (u + 1) * down.chunks - 1,
                                  lambda j, u=u: add_tile(u, j).then_inc(out_dve, 1))
            norm(6, rows_of(g_ff[-1][1]))

        @block.tensor
        def _(pe):
            def tile_passes(g, chunk, tile, s, kc, j, fm, a_hi=act_hi, a_lo=act_lo, base=(0, 4, 8, 12)):
                hi, lo = w_hi[s], w_lo[s]
                if j == 0:
                    pe.wait_ge(w_lo_done, chunk + 1)
                if kc == 0:
                    pe.wait_ge(taken(g), tile + 1)
                    before = g.after
                    if before and before.taker != g.taker and not (isinstance(tile, int) and tile >= g.tile0 + 4):
                        pe.wait_ge(taken(before), before.tile1 + j + 1)
                cols = slice(j * P, (j + 1) * P)
                for k in range(g.ktiles):
                    ka = base[kc] + k
                    if fm:
                        passes = ((hi[:, k, cols], a_hi[:, ka, :]), (hi[:, k, cols], a_lo[:, ka, :]),
                                  (lo[:, k, cols], a_hi[:, ka, :]))
                    else:
                        passes = ((a_hi[:, ka, cols], hi[:, k, :]), (a_hi[:, ka, cols], lo[:, k, :]),
                                  (a_lo[:, ka, cols], hi[:, k, :]))
                    for n_pass, (left, right) in enumerate(passes):
                        ins = pe.matmul(gb[j][:, :], left, right, start=(kc == 0 and k == 0 and n_pass == 0),
                                        stop=(kc == g.chunks - 1 and k == g.ktiles - 1 and n_pass == 2))
                ins.then_inc(pe_tiles, 1)

            def multiply(g, i, per_body, ready, after, **operand):
                for u in range(per_body):
                    for kc in range(g.chunks):
                        n = u * g.chunks + kc
                        for j in range(4):
                            ready(kc, j)
                            tile_passes(g, i * (g.chunks * per_body) + (g.chunk0 + n),
                                        i * (4 * per_body) + (g.tile0 + 4 * u + j), n % 2, kc, j, **operand)
                    after(u)

            def gemm(g, ready=lambda kc, j: None, after=lambda u: None, **operand):
                per_body = 2 if g.chunks == 1 else 1
                if g.units == per_body:
                    multiply(g, 0, per_body, ready, after, **operand)
                    return
                with pe.Fori(0, g.units // per_body) as i:
                    multiply(g, i, per_body, ready, after, **operand)

            def turn(dst, src, rows=P):
                return pe.transpose(dst, src, ident[0:rows, 0:rows])

            def turn_rows(n, t):
                pe.wait_ge(n_xn, rows_count(n, t))
                for b in range(2):
                    q = 2 * t + b
                    if q >= 4:
                        pe.wait_ge(n_lo, turned_before(n) + q - 3)
                    for k in range(4):
                        ins = turn(mb[q % 4][:, k * P:(k + 1) * P], xn_at[n][:, t, (4 * b + k) * P:(4 * b + k + 1) * P])
                    ins.then_inc(n_tp, 1)

            def norm_and_product(n, g):
                def first(j):
                    pe.wait_ge(n_lo, turned_before(n) + 2 * (j + 1))
                    tile_passes(g, g.chunk0, g.tile0 + j, 0, 0, j, fm=False)

                turn_rows(n, 0)
                for t in range(1, NT):
                    turn_rows(n, t)
                    first(t - 1)
                first(NT - 1)
                for j in range(4):
                    tile_passes(g, g.chunk0 + 1, g.tile0 + j, 1, 1, j, fm=False)

            def product_and_norm(g, n, ready, **operand):
                for u in range(2):
                    for kc in range(2):
                        for j in range(4):
                            if u == 0:
                                ready(kc, j)
                            tile_passes(g, g.chunk0 + 2 * u + kc, g.tile0 + 4 * u + j, kc, kc, j, fm=False, **operand)
                            if u == kc == 1 and j >= 2:
                                turn_rows(n, j - 2)
                for t in (2, 3):
                    turn_rows(n, t)

            def second_unit(g):
                for kc in range(2):
                    for j in range(4):
                        tile_passes(g, g.chunk0 + 2 + kc, g.tile0 + 4 + j, kc, kc, j, fm=False)

            def all_split(n):
                pe.wait_ge(n_lo, turned_before(n) + 2 * NT)

            def half_split(count):
                return lambda kc, j: j == 0 and pe.wait_ge(y_lo, count + 4 * (kc + 1))

            for sem_out in (out_act, out_dve):
                pe.sem_inc(sem_out, 4)
            pe.wait_ge(const_pool, 6)
            norm_and_product(0, g_vi)
            second_unit(g_vi)
            gemm(g_fquo, fm=True)
            pe.wait_ge(wsp_masked, 1)
            for b in range(2):
                for g in range(4):
                    ins = turn(mb[b][:, g * P:(g + 1) * P], w_sp[:, 4 * b + g, :])
                ins.then_inc(wsp_turned, 1)
            pe.wait_ge(v_normed, NT)
            pe.wait_ge(wspT_done, 2)
            for j in range(NH):
                for t in range(NT):
                    cols = slice(t * P, (t + 1) * P)
                    ins = pe.matmul(mb[j][:, cols], group_sel[:, j * P:(j + 1) * P], b_sp[:, :], start=True, stop=False,
                                    skip_group_check=True)
                    for q in range(2):
                        g = 2 * j + q
                        ins = pe.matmul(mb[j][q * GD:(q + 1) * GD, cols], v_tm[:, t, g * GD:(g + 1) * GD],
                                        w_spT[:, g, :], start=False, stop=True, skip_group_check=True)
                ins.then_inc(spatial_done, 1)
            gemm(g_ga, fm=True)
            pe.wait_ge(hg_ready, 3)
            pe.wait_ge(ya_done, NH)
            for t in range(NT):
                cols = slice(t * P, (t + 1) * P)
                if t >= 2:
                    pe.wait_ge(hg_att_out, 3 * (t - 1))
                for h in range(NH):
                    ins = pe.matmul(mb[2 * (t % 2)][:, h * P:(h + 1) * P], f_fm[:, h, cols], q_fm[:, h, cols],
                                    start=True, stop=True, skip_group_check=True)
                ins.then_inc(hg_att, 1)
                for h in range(NH):
                    ins = pe.matmul(mb[2 * (t % 2) + 1][0:HC, h * P:(h + 1) * P], kend_fm[:, h, t * P:t * P + HC],
                                    q_fm[:, h, cols], start=True, stop=True, skip_group_check=True)
                ins.then_inc(hg_att, 1)
            pe.wait_ge(hg_scaled, 2)
            pe.wait_ge(hg_att_out, 3 * NT)
            for t in range(NT):
                for h in range(NH):
                    ins = turn(mb[t][:, h * P:(h + 1) * P], kend_fm[:, h, t * P:(t + 1) * P])
                ins.then_inc(kend_turned, 1)
            gemm(g_gb, fm=True)
            for t in range(NT - 1):
                pe.wait_ge(kend_done, NT)
                for h in range(NH):
                    cols = slice(h * P, (h + 1) * P)
                    ins = pe.matmul(mb[t][:, cols], kend_tm[:, t, cols], i_tm[:, t, cols], start=True, stop=True,
                                    skip_group_check=True)
                ins.then_inc(hg_ds, 1)
            pe.wait_ge(att_masked, NT)
            pe.wait_ge(hg_state, NH * (NT - 1))
            for h in range(NH):
                for t in range(NT):
                    cols = slice(t * P, (t + 1) * P)
                    ins = pe.matmul(mb[h][:, cols], i_tm[:, t, h * P:(h + 1) * P], attT[:, t, h, :], start=True,
                                    stop=(t == 0), skip_group_check=True)
                    if t:
                        ins = pe.matmul(mb[h][:, cols], s_hg[:, t - 1, h, :], q_fm[:, h, cols], start=False, stop=True,
                                        skip_group_check=True)
                ins.then_inc(hg_o, 1)
            pe.wait_ge(hg_sq, NH)
            for h in range(NH):
                ins = pe.matmul(mb[0][32 * h:32 * h + 32, :], ones[:, 0:32], sq_fm[:, h, :], start=True, stop=True,
                                skip_group_check=True)
            ins.then_inc(hg_ss, 1)
            pe.wait_ge(y_lo, NH)

            def spread_roots(u):
                if u == 0:
                    pe.wait_ge(hg_rs, 1)
                    pe.wait_ge(r_pool, 2)
                    for h in range(NH):
                        pe.matmul(mb[h][:, :], head_sel[:, h, :], rs_hg[:, :], start=True, stop=True)\
                            .then_inc(hg_rsb, 1)

            gemm(g_upa, fm=True, after=spread_roots)
            pe.wait_ge(y_lo, 2 * NH)
            gemm(g_upb, fm=True, a_hi=act_hi[:, 4:8, :], a_lo=act_lo[:, 4:8, :])
            product_and_norm(g_out, 1, half_split(AT_MERGED))

            pe.wait_ge(rw_lo, 1)
            for h in range(2):
                pe.wait_ge(n_lo, turned_before(1) + NT * (h + 1))
                tokens = slice(h * T // 2, (h + 1) * T // 2)
                for k in range(KT):
                    for n, (left, right) in enumerate(((route_hi, act_hi), (route_hi, act_lo), (route_lo, act_hi))):
                        ins = pe.matmul(gb[2 * h][0:ROUTED, tokens], left[:, k, :], right[:, k, tokens],
                                        start=(k == 0 and n == 0), stop=(k == KT - 1 and n == 2))
                ins.then_inc(logitT_done, 1)
            for t in range(NT):
                pe.wait_ge(logitT_out, t // 2 + 1)
                ins = turn(gb[1][:, t * ROUTED:(t + 1) * ROUTED], logitT[:, t * P:(t + 1) * P], ROUTED)
            ins.then_inc(logits_done, 1)
            pe.wait_ge(picked, 1)
            any_flat = r_any[:, :, :].rearrange("p t e -> p (t e)")
            for back in range(NT):
                ins = pe.matmul(mb[2][:, back * NE:NT * NE], (ones if back else earlier)[:, 0:P],
                                any_flat[:, 0:(NT - back) * NE], start=(back == 0), stop=(back == NT - 1),
                                skip_group_check=True)
            ins.then_inc(ranked, 1)
            for t in range(NT):
                ins = pe.matmul(mb[3][:, 0:NE], ones[:, 0:P], r_any[:, t, :], start=(t == 0), stop=(t == NT - 1))
            ins.then_inc(ranked, 1)

            def experts_pe(r):
                def gather(n, first=False):
                    pe.wait_ge(sel_made, n * 8 + 8)
                    if not first:
                        pe.wait_ge(rows_out, n * 2)
                        if not isinstance(n, int) or n > 1:
                            pe.wait_ge(moe_added, n * 8 - 8)
                    elif r is not None:
                        pe.wait_ge(moe_added, n * 8)
                    for b in range(2):
                        for part in (xn_hi, xn_lo):
                            for t in range(NT):
                                ins = pe.matmul(mb[b][:, :], sel[:, t, :], part[:, t, b * 512:(b + 1) * 512],
                                                start=(part is xn_hi and t == 0), stop=(part is xn_lo and t == NT - 1))
                        ins.then_inc(rows_in, 1)
                    if not isinstance(n, int) or n:
                        pe.wait_ge(selT_out, n)
                    for t in range(NT):
                        ins = turn(gb[3][:, t * P:(t + 1) * P], sel[:, t, :].bitcast(F32))
                    ins.then_inc(sel_turned, 1)

                def turn_gathered(n):
                    for b in range(2):
                        pe.wait_ge(xg_out, n * 2 + (b + 1))
                        for k in range(4):
                            ins = turn(mb[b][:, k * P:(k + 1) * P], xg[:, (4 * b + k) * P:(4 * b + k + 1) * P])
                        ins.then_inc(rows_turned, 1)

                def spread(n, u, bank):
                    t, half = u // 2, slice(u % 2 * 512, (u % 2 + 1) * 512)
                    for part in (y_hi_sb, y_lo_sb):
                        ins = pe.matmul(bank[:, :], selT[:, t * P:(t + 1) * P], part[:, half],
                                        start=(part is y_hi_sb), stop=(part is y_lo_sb))
                    ins.then_inc(spread_done, 1)

                def output_cut(n):
                    pe.wait_ge(y_lo_out, n * 2 + 2)
                    pe.wait_ge(selT_out, n + 1)

                def piece_in(n, k, ahead):
                    if k >= EXTRA // 2 or (isinstance(n, int) and n == 0):
                        pe.wait_ge(ring_in[k], n * 32 + 32)
                    elif ahead:
                        pe.wait_ge(extra_in, 16 * EXTRA)
                    else:
                        pe.wait_ge(ring_in[k], n * 32)

                def pair(i, first=False, ahead=False, last=False):
                    n = pair_number(i, r)
                    pe.wait_ge(rows_out, n * 2 + 2)
                    for w, dst in ((0, mb[2]), (1, mb[3])):
                        if not isinstance(n, int) or n:
                            pe.wait_ge(gated_done, n)
                        for kh in range(2):
                            piece_in(n, 2 * w + kh, ahead)
                            for k in range(4):
                                for q in range(2):
                                    mine = slice(q * SLOTS, (q + 1) * SLOTS)
                                    from_extra = ahead and 2 * w + kh < EXTRA // 2
                                    weights = (extra if from_extra else ring)[4 * w + 2 * kh + q]
                                    ins = pe.matmul(dst[mine, :], xgT[:, 4 * kh + k, mine], weights[:, k, :],
                                                    start=(kh == 0 and k == 0), stop=(kh == 1 and k == 3),
                                                    skip_group_check=True)
                            ins.then_inc(up_done, 1)
                            if not first:
                                if w == 0 and kh == 0:
                                    output_cut(n - 1)
                                for b in range(2):
                                    u = 4 * w + 2 * kh + b
                                    if u >= 2:
                                        pe.wait_ge(moe_added, n * 8 + (u - 9))
                                    spread(n - 1, u, mb[b])
                    if not last:
                        gather(n + 1)
                    pe.wait_ge(gated_done, n + 1)
                    for k in range(4):
                        ins = turn(gb[0][:, k * P:(k + 1) * P], gated[:, k * P:(k + 1) * P])
                    ins.then_inc(gated_turned, 1)
                    if not last:
                        turn_gathered(n + 1)
                    pe.wait_ge(gatedT_out, n + 1)
                    for nh in range(2):
                        piece_in(n, 4 + nh, ahead)
                        for k in range(4):
                            for q in range(2):
                                mine = slice(q * SLOTS, (q + 1) * SLOTS)
                                ins = pe.matmul(gb[1 + nh][mine, :], gatedT[:, k, mine],
                                                ring[8 + 2 * nh + q][:, k, :], start=(k == 0), stop=(k == 3),
                                                skip_group_check=True)
                        ins.then_inc(down_done, 1)

                gather(pair_number(0, r), first=True)
                turn_gathered(pair_number(0, r))
                pe.wait_ge(placed, 2 * NT if r is None else r * (2 * NT) + 2 * NT)
                for c in range(2 * NT):
                    ins = pe.matmul(gb[1][:, 0:PAIRS], place_1h[:, c, :], pair_gate[:, c, :], start=(c == 0),
                                    stop=(c == 2 * NT - 1))
                ins.then_inc(tabled, 1)
                pe.wait_ge(valued, 1 if r is None else r + 1)
                pair(0, first=True)
                if r is None:
                    pair(1, ahead=True)
                with pe.Fori(2 if r is None else 1, PAIRS - 1) as i:
                    pair(i)
                pair(PAIRS - 1, last=True)
                n = pair_number(PAIRS - 1, r)
                output_cut(n)
                for u in range(2 * NT):
                    if u >= 4:
                        pe.wait_ge(moe_added, n * 8 + (u - 3))
                    spread(n, u, gb[u % 4])

            pe.wait_ge(xn_lo_done, NT)
            experts_pe(None)
            fullest = pe.value_load(most[0:1, 0:1], min_val=0, max_val=T)
            with pe.If(fullest > SLOTS):
                with pe.Fori(1, ROUNDS) as r:
                    with pe.If(fullest > r * SLOTS):
                        experts_pe(r)

            norm_and_product(2, g_pg)
            pe.wait_ge(p_in, 16)
            for b in range(2):
                for t in range(NT):
                    ins = turn(mb[b][:, t * P:(t + 1) * P], p_tm[:, t, b * P:(b + 1) * P])
                ins.then_inc(p_turned, 1)
            second_unit(g_pg)
            pe.wait_ge(p_lo, 2)
            gemm(g_ple, fm=False, a_hi=pT_hi, a_lo=pT_lo)

            norm_and_product(4, g_sv)
            pe.wait_ge(low_split, 2)
            for k in range(KT):
                for n, (left, right) in enumerate(((low_hi, act_hi), (low_hi, act_lo), (low_lo, act_hi))):
                    ins = pe.matmul(mb[0][:, :], left[:, k, :], right[:, k, :], start=(k == 0 and n == 0),
                                    stop=(k == KT - 1 and n == 2))
            ins.then_inc(low_z, 1)
            gemm(g_gv, fm=False)
            pe.wait_ge(lowT_done, 1)
            for h in range(NH):
                pe.matmul(mb[h][:, :], gate_up[:, h * P:(h + 1) * P], lowT[:, :], start=True, stop=True)\
                    .then_inc(la_z, 1)
            gemm(g_qk, fm=True)
            pe.wait_ge(la_cum, NH * NT)
            pe.sem_inc(sb_o, 8)
            pe.sem_inc(sb_sig, 2)
            pe.sem_inc(sb_wT_done, 1)
            pe.sem_inc(sb_o_out, 1)

            def scores(h, n):
                s, t = n % 2, n % 4
                rows = slice((n // 4) * SBD, (n // 4 + 1) * SBD)
                if n == 0:
                    pe.wait_ge(sb_first_in, h + 1)
                elif n == NT:
                    pe.wait_ge(sb_second_in, h * 2 + 2)
                if n or not isinstance(h, int):
                    pe.wait_ge(sb_sig, h * 16 + 2 * n)
                if not isinstance(h, int) and n < NT:
                    pe.sem_inc(wait_carrier, 1)
                k = sbk[rows, col(h), :].rearrange("p o t -> p (o t)") if n < NT else sb_k[rows, :]
                pe.matmul(mb[s][:, 0:(t + 1) * P], sb_q[rows, t * P:(t + 1) * P], k[:, 0:(t + 1) * P],
                          start=True, stop=True).then_inc(sb_z, 1)

            def sb_turn(h, last):
                for n in range(2 * NT):
                    s, t = n % 2, n % 4
                    if n < 2 * NT - 1:
                        scores(h, n + 1)
                    elif not last:
                        scores(h + 1, 0)
                    pe.wait_ge(sb_weight, h * 16 + 2 * n + 2)
                    pe.wait_ge(sb_wT_done, h * 8 + n + 1)
                    for b in range(t + 1):
                        ins = turn(mb[2][:, b * P:(b + 1) * P], sb_w[s][:, b * P:(b + 1) * P])
                    ins.then_inc(sb_turned, 1)
                    kc, j = n // 4, n % 4
                    tile_passes(g_gla, h * 2 + (g_gla.chunk0 + kc), h * 4 + (g_gla.tile0 + j), kc, kc, j, fm=True)
                    pe.wait_ge(sb_wT_done, h * 8 + n + 2)
                    if n == 0:
                        pe.wait_ge(sb_o_out, h + 1)
                        pe.wait_ge(sb_v_in, h + 1)
                    rows = slice((n // 4) * SBD, (n // 4 + 1) * SBD)
                    for b in range(t + 1):
                        ins = pe.matmul(mb[3][rows, t * P:(t + 1) * P], sb_v[:, b, rows], sb_wT[:, b, :],
                                        start=(b == 0), stop=(b == t), skip_group_check=True)
                    ins.then_inc(sb_o, 1)

            scores(0, 0)
            with pe.Fori(0, SBH // 2 - 1) as h:
                sb_turn(h, False)
            sb_turn(SBH // 2 - 1, True)
            pe.wait_ge(sb_o_out, SBH // 2 + 1)

            def gates_tiles(first, count):
                for i in range(first, first + count):
                    n, j = divmod(i, 4)
                    tile_passes(g_gates, g_gates.chunk0 + n, g_gates.tile0 + 4 * (n // 2) + j, n % 2, n % 2, j, fm=True)

            AHEAD = 2
            gates_tiles(0, AHEAD)
            for n in range(LEVELS + 1):
                if n < LEVELS:
                    pe.wait_ge(gl_prod, 2 * n + 2)
                for t in range(NT):
                    cols = slice(t * P, (t + 1) * P)
                    if n:
                        pe.wait_ge(gl_copied, NT * (n - 1) + t + 1)
                    for h in range(NH):
                        left, right = (gl_qk, gl_qk) if n < LEVELS else (gk_fm, gq_fm)
                        ins = pe.matmul(mb[t][:, h * P:(h + 1) * P], left[:, h, cols], right[:, h, cols],
                                        start=True, stop=True, skip_group_check=True)
                    ins.then_inc(gl_mm, 1)
                gates_tiles(AHEAD + 4 * n, 4 if n < LEVELS else 4 - AHEAD)
            pe.wait_ge(gl_scaled, 2)
            pe.wait_ge(gl_copied, NT * (LEVELS + 1))
            for t in range(NT):
                for h in range(NH):
                    ins = turn(mb[t][:, h * P:(h + 1) * P], gk_fm[:, h, t * P:(t + 1) * P])
                ins.then_inc(gkend_turned, 1)
            for t in range(NT - 1):
                pe.wait_ge(gkend_done, min(2 * t + 2, NT))
                if t == 2:
                    pe.wait_ge(gl_state, NH)
                for h in range(NH):
                    ins = pe.matmul(mb[2 * (t % 2) + h // 2][:, (h % 2) * DV:(h % 2 + 1) * DV],
                                    gkend_tm[:, t, h * P:(h + 1) * P], gv_tm[:, t, h * DV:(h + 1) * DV],
                                    start=True, stop=True, skip_group_check=True)
                    if h % 2:
                        ins.then_inc(gl_ds, 1)
            pe.wait_ge(gl_state, NH * (NT - 1))

            def squares(h):
                pe.wait_ge(gl_sq, 2 * h + 2)
                for v in range(2):
                    ins = pe.matmul(mb[2][32 * h:32 * h + 32, :], ones[:, 0:32], gsq[h % 2][:, v, :],
                                    start=(v == 0), stop=(v == 1), skip_group_check=True)
                ins.then_inc(gl_ss, 1)

            for n in range(KT):
                h = n // 2
                if n >= 3:
                    pe.wait_ge(gl_sq, n - 2)
                for t in range(NT):
                    cols = slice(t * P, (t + 1) * P)
                    vals = slice((n % 2) * P, (n % 2 + 1) * P)
                    ins = pe.matmul(gla_bank(n)[:, cols], gv_tm[:, t, n * P:(n + 1) * P], g_att[:, t, h, :], start=True,
                                    stop=(t == 0), skip_group_check=True)
                    if t:
                        ins = pe.matmul(gla_bank(n)[:, cols], s_gla[t - 1][:, h, vals], gq_fm[:, h, cols], start=False,
                                        stop=True, skip_group_check=True)
                ins.then_inc(gl_o, 1)
                if n and n % 2 == 0:
                    squares(h - 1)
            squares(NH - 1)
            pe.wait_ge(y_lo, AT_YO + NH)

            psb_tiles = []

            def spread_gla(kc, j):
                psb_tiles.append(j)
                if len(psb_tiles) == 3:
                    pe.wait_ge(gl_rs, 1)
                    pe.wait_ge(r_pool, 3)
                    for h in range(NH):
                        pe.matmul(mb[h][:, :], gsel[:, h, :], rs_gla[:, :], start=True, stop=True)\
                            .then_inc(gl_rsb, 1)

            gemm(g_psb, fm=True, ready=spread_gla)
            gemm(g_pgla, fm=True, base=(4, 0), ready=half_split(AT_YG))
            product_and_norm(g_out2, 5, half_split(AT_MIX), a_hi=mix_hi, a_lo=mix_lo)

            all_split(5)
            for h, (up, down) in enumerate(g_ff):
                gemm(up, fm=True)
                gemm(down, fm=False, ready=lambda kc, j, h=h, up=up: j == 0 and pe.wait_ge(
                         hid_lo_done, h * 4 * up.units + 4 * (kc + 1)),
                      a_hi=hid_hi, a_lo=hid_lo, base=tuple(range(0, FH // P, 4)))


_INS = ["x", "p", "g_mix", "w_in", "gm_ln_g", "gm_ln_b", "gm_w_sp", "gm_b_sp", "w_up_a", "hg_lb_param",
        "hg_norm_g", "w_up_b", "w_out", "g_ffn", "w_grp", "w_exp", "w1", "w3", "w2", "g_ple", "w_pg",
        "w_ple", "g_final", "norm_mix_2", "w_in_2", "w_gate_up_2", "b_gate_up_2", "gla_norm_2",
        "w_proj_sb_2", "w_proj_gla_2", "w_out_2", "norm_mlp_2", "w_ff1_2", "w_ff2_2", "norm_final_2"]


def kernel(**inputs):
    import numpy as np
    import concourse.bacc as bacc
    from concourse.bass_utils import run_bass_kernel_spmd

    nc = bacc.Bacc("TRN2", target_bir_lowering=False, num_devices=1)
    arrays, aps = {}, {}
    for name in _INS:
        a = np.ascontiguousarray(inputs[name])
        arrays[f"in_{name}"] = a
        aps[name] = nc.dram_tensor(f"in_{name}", a.shape, mybir.dt.from_np(a.dtype), kind="ExternalInput").ap()
    out = nc.dram_tensor("out", inputs["x"].shape, F32, kind="ExternalOutput").ap()
    two_blocks(nc, aps, out)
    r = run_bass_kernel_spmd(nc, [arrays], core_ids=[0])
    return r.results[0]["out"]
```
